# Optimizing a Trainium2 kernel written in Bass

```python
import math
import jax, jax.numpy as jnp
from jax import lax
import numpy as np

D_MODEL = 1024
BATCH = 1
SEQ = 256
DEPTH = 2
DEC_BATCH = 8
DEC_SEQ = 1
PAST_LEN = 2048
PAGE_SIZE = 128

D_MIX = D_MODEL
W_A = D_MIX // 2
RG_BLOCKS = 8
RG_BW = W_A // RG_BLOCKS
CONV_W = 4
RG_C = 8.0
W_B = D_MIX - W_A
HG_HEADS = 4
HG_DK = W_B // HG_HEADS
HG_DV = W_B // HG_HEADS
HK = HG_HEADS * HG_DK
HG_CHUNK = 64
D_IN = 2 * W_A + 2 * HK + 2 * W_B
D_FF = ((8 * D_MODEL // 3 + 255) // 256) * 256
N_EXPERTS = 8
TOP_K = 2
N_DENSE = (DEPTH + 1) // 2
N_MOE = DEPTH // 2
EPS = 1e-6

kernel_name = "hymba_style_rglru_hgrn2_moe_adaln_decode"

F32 = jnp.float32

def rmsnorm(x, g):
    xf = x.astype(F32)
    y = xf * lax.rsqrt(jnp.mean(xf * xf, axis=-1, keepdims=True) + EPS)
    return y * g.astype(F32)

def causal_conv(x, buf, w, b):
    T = x.shape[1]
    xp = jnp.concatenate([buf.astype(x.dtype), x], axis=1)
    y = b.astype(F32)
    for j in range(CONV_W):
        y = y + xp[:, j:j + T].astype(F32) * w[j].astype(F32)
    return y, xp[:, -(CONV_W - 1):]

def rglru(xc, h0, pos0, wa, ba, wx, bx, lam):
    Bn, T, _ = xc.shape
    xb = xc.reshape(Bn, T, RG_BLOCKS, RG_BW)
    r = jax.nn.sigmoid(jnp.einsum('btnc,ncd->btnd', xb, wa.astype(F32)).reshape(Bn, T, W_A) + ba.astype(F32))
    i = jax.nn.sigmoid(jnp.einsum('btnc,ncd->btnd', xb, wx.astype(F32)).reshape(Bn, T, W_A) + bx.astype(F32))
    log_a = -RG_C * jax.nn.softplus(-lam.astype(F32)) * r
    reset = ((jnp.arange(T) + pos0) == 0)[None, :, None]
    a = jnp.where(reset, 0.0, jnp.exp(log_a))
    mult = jnp.where(reset, 1.0, jnp.sqrt(-jnp.expm1(2.0 * log_a)))
    b = mult * (i * xc)
    b = b.at[:, 0].add(a[:, 0] * h0.astype(F32))

    def combine(lft, rgt):
        a1, b1 = lft
        a2, b2 = rgt
        return a1 * a2, a2 * b1 + b2

    _, h = lax.associative_scan(combine, (a, b), axis=1)
    return h, h[:, -1]

def hgrn2_chunked(q, k, v, logf, S0):
    Bn, T, H, _ = q.shape
    C = math.gcd(T, HG_CHUNK)
    NC = T // C

    def to_chunks(z):
        return z.reshape(Bn, NC, C, H, z.shape[-1]).transpose(1, 0, 3, 2, 4)

    mask = jnp.tril(jnp.ones((C, C), dtype=bool))[None, None, :, :, None]

    def step(S, inp):
        qc, kc, vc, gc = inp
        bcum = jnp.cumsum(gc, axis=2)
        o_inter = jnp.einsum('bhcd,bhde->bhce', qc * jnp.exp(bcum), S)
        diff = bcum[:, :, :, None, :] - bcum[:, :, None, :, :]
        decay = jnp.exp(jnp.where(mask, diff, -jnp.inf))
        A = jnp.einsum('bhtd,bhsd,bhtsd->bhts', qc, kc, decay)
        o_intra = jnp.einsum('bhts,bhse->bhte', A, vc)
        b_last = bcum[:, :, -1:, :]
        S_new = jnp.exp(b_last[:, :, 0, :])[..., None] * S + jnp.einsum(
            'bhsd,bhse->bhde', kc * jnp.exp(b_last - bcum), vc)
        return S_new, o_inter + o_intra

    S_fin, o = lax.scan(step, S0, (to_chunks(q), to_chunks(k), to_chunks(v), to_chunks(logf)))
    o = o.transpose(1, 0, 3, 2, 4).reshape(Bn, T, H, v.shape[-1])
    return o, S_fin

def swiglu(h, w1, w3, w2):
    return (jax.nn.silu(h @ w1) * (h @ w3)) @ w2

def moe_swiglu(h, router, w1, w3, w2):
    logits = (h @ router).astype(F32)
    topv, topi = lax.top_k(logits, TOP_K)
    wts = jax.nn.softmax(topv, axis=-1)
    gates = jnp.sum(jax.nn.one_hot(topi, N_EXPERTS, dtype=F32) * wts[..., None], axis=-2)
    out = jnp.zeros(h.shape[:-1] + (D_MODEL,), F32)
    for e in range(N_EXPERTS):
        out = out + gates[..., e:e + 1] * swiglu(h, w1[e], w3[e], w2[e]).astype(F32)
    return out

def setup_inputs(seed: int = 0) -> dict:
    key = jax.random.key(seed)
    ks = iter(jax.random.split(key, 40))

    def nrm(shape, scale=1.0):
        return jax.random.normal(next(ks), shape, F32) * scale

    u = jax.random.uniform(next(ks), (DEPTH, W_A), F32, minval=0.9, maxval=0.999)
    s = u ** (1.0 / RG_C)
    rg_lambda = jnp.log(s) - jnp.log1p(-s)
    return {
        "x_prompt": nrm((BATCH, SEQ, D_MODEL)),
        "x_sample": nrm((DEC_BATCH, DEC_SEQ, D_MODEL)),
        "c_prompt": nrm((BATCH, D_MODEL)),
        "c_sample": nrm((DEC_BATCH, D_MODEL)),
        "state_rglru_h": nrm((DEPTH, DEC_BATCH, W_A)),
        "state_rglru_conv": nrm((DEPTH, DEC_BATCH, CONV_W - 1, W_A)),
        "state_hgrn": nrm((DEPTH, DEC_BATCH, HG_HEADS, HG_DK, HG_DV), 0.5),
        "mod_w": nrm((DEPTH, D_MODEL, 6 * D_MODEL), 0.5 * D_MODEL ** -0.5),
        "mod_b": nrm((DEPTH, 6 * D_MODEL), 0.02),
        "norm1_g": 1.0 + nrm((DEPTH, D_MODEL), 0.02),
        "norm2_g": 1.0 + nrm((DEPTH, D_MODEL), 0.02),
        "w_in": nrm((DEPTH, D_MODEL, D_IN), D_MODEL ** -0.5),
        "conv_w": nrm((DEPTH, CONV_W, W_A), CONV_W ** -0.5),
        "conv_b": nrm((DEPTH, W_A), 0.02),
        "rg_wa": nrm((DEPTH, RG_BLOCKS, RG_BW, RG_BW), RG_BW ** -0.5),
        "rg_ba": nrm((DEPTH, W_A), 0.02),
        "rg_wx": nrm((DEPTH, RG_BLOCKS, RG_BW, RG_BW), RG_BW ** -0.5),
        "rg_bx": nrm((DEPTH, W_A), 0.02),
        "rg_lambda": rg_lambda,
        "rg_out_g": 1.0 + nrm((DEPTH, W_A), 0.02),
        "hg_lb_logits": nrm((DEPTH, HK), 0.1),
        "hg_norm_g": 1.0 + nrm((DEPTH, W_B), 0.02),
        "w_out": nrm((DEPTH, D_MIX, D_MODEL), D_MIX ** -0.5),
        "ffn_w1": nrm((N_DENSE, D_MODEL, D_FF), D_MODEL ** -0.5),
        "ffn_w3": nrm((N_DENSE, D_MODEL, D_FF), D_MODEL ** -0.5),
        "ffn_w2": nrm((N_DENSE, D_FF, D_MODEL), D_FF ** -0.5),
        "router_w": nrm((N_MOE, D_MODEL, N_EXPERTS), D_MODEL ** -0.5),
        "moe_w1": nrm((N_MOE, N_EXPERTS, D_MODEL, D_FF), D_MODEL ** -0.5),
        "moe_w3": nrm((N_MOE, N_EXPERTS, D_MODEL, D_FF), D_MODEL ** -0.5),
        "moe_w2": nrm((N_MOE, N_EXPERTS, D_FF, D_MODEL), D_FF ** -0.5),
        "final_g": 1.0 + nrm((D_MODEL,), 0.02),
    }

def reference(x_prompt, x_sample, c_prompt, c_sample, state_rglru_h, state_rglru_conv, state_hgrn,
              mod_w, mod_b, norm1_g, norm2_g, w_in, conv_w, conv_b, rg_wa, rg_ba, rg_wx, rg_bx,
              rg_lambda, rg_out_g, hg_lb_logits, hg_norm_g, w_out, ffn_w1, ffn_w3, ffn_w2,
              router_w, moe_w1, moe_w3, moe_w2, final_g):
    p_lb = jax.nn.softmax(hg_lb_logits.astype(F32), axis=0)
    lower_bounds = jnp.cumsum(p_lb, axis=0) - p_lb[0]

    def layer(l, x, c, h0, conv0, S0, pos0):
        dt = x.dtype
        Bn, T, _ = x.shape
        mod = jax.nn.silu(c.astype(F32)) @ mod_w[l].astype(F32) + mod_b[l].astype(F32)
        sh1, sc1, gt1, sh2, sc2, gt2 = jnp.split(mod[:, None, :], 6, axis=-1)
        h = (rmsnorm(x, norm1_g[l]) * (1.0 + sc1) + sh1).astype(dt)
        u = h @ w_in[l]
        xa, ga, qb, fb, ib, gb = jnp.split(
            u, [W_A, 2 * W_A, 2 * W_A + HK, 2 * W_A + 2 * HK, 2 * W_A + 2 * HK + W_B], axis=-1)
        xc, convN = causal_conv(xa, conv0, conv_w[l], conv_b[l])
        hseq, hN = rglru(xc, h0, pos0, rg_wa[l], rg_ba[l], rg_wx[l], rg_bx[l], rg_lambda[l])
        yA = rmsnorm(hseq * jax.nn.gelu(ga.astype(F32)), rg_out_g[l])
        lb = lower_bounds[l]
        f = lb + (1.0 - lb) * jax.nn.sigmoid(fb.astype(F32))
        q = jax.nn.silu(qb.astype(F32)).reshape(Bn, T, HG_HEADS, HG_DK)
        k = (1.0 - f).reshape(Bn, T, HG_HEADS, HG_DK)
        logf = jnp.log(f).reshape(Bn, T, HG_HEADS, HG_DK)
        v = ib.astype(F32).reshape(Bn, T, HG_HEADS, HG_DV)
        o, SN = hgrn2_chunked(q, k, v, logf, S0.astype(F32))
        o = rmsnorm(o, hg_norm_g[l].reshape(HG_HEADS, HG_DV)) * jax.nn.silu(
            gb.astype(F32)).reshape(Bn, T, HG_HEADS, HG_DV)
        yB = o.reshape(Bn, T, W_B)
        y = jnp.concatenate([yA, yB], axis=-1).astype(dt) @ w_out[l]
        x = (x.astype(F32) + gt1 * y.astype(F32)).astype(dt)
        h2 = (rmsnorm(x, norm2_g[l]) * (1.0 + sc2) + sh2).astype(dt)
        if l % 2 == 0:
            fo = swiglu(h2, ffn_w1[l // 2], ffn_w3[l // 2], ffn_w2[l // 2]).astype(F32)
        else:
            fo = moe_swiglu(h2, router_w[l // 2], moe_w1[l // 2], moe_w3[l // 2], moe_w2[l // 2])
        x = (x.astype(F32) + gt2 * fo).astype(dt)
        return x, hN.astype(dt), convN.astype(dt), SN.astype(dt)

    xp, xs = x_prompt, x_sample
    dtp = x_prompt.dtype
    hp0 = jnp.zeros((BATCH, W_A), dtp)
    convp0 = jnp.zeros((BATCH, CONV_W - 1, W_A), dtp)
    Sp0 = jnp.zeros((BATCH, HG_HEADS, HG_DK, HG_DV), dtp)
    hp_l, convp_l, Sp_l, hs_l, convs_l, Ss_l = [], [], [], [], [], []
    for l in range(DEPTH):
        xp, hp, cp, sp = layer(l, xp, c_prompt, hp0, convp0, Sp0, 0)
        xs, hs, cs, ss = layer(l, xs, c_sample, state_rglru_h[l], state_rglru_conv[l], state_hgrn[l], PAST_LEN)
        hp_l.append(hp); convp_l.append(cp); Sp_l.append(sp)
        hs_l.append(hs); convs_l.append(cs); Ss_l.append(ss)
    y_prompt = rmsnorm(xp, final_g).astype(x_prompt.dtype)
    y_sample = rmsnorm(xs, final_g).astype(x_sample.dtype)
    return (y_prompt, y_sample,
            jnp.stack(hp_l), jnp.stack(convp_l), jnp.stack(Sp_l),
            jnp.stack(hs_l), jnp.stack(convs_l), jnp.stack(Ss_l))


_drawn_inputs = setup_inputs


def setup_inputs(seed=0):
    import zlib

    import numpy as np

    out = dict(_drawn_inputs(seed))
    spreads = {}
    factors = {'norm1_g': 2.754,
     'norm2_g': 4.389,
     'rg_ba': 8.0,
     'rg_bx': 6.847,
     'rg_out_g': 23.43,
     'hg_norm_g': 8.0,
     'final_g': 7.749}
    for name, (base, spread) in spreads.items():
        noise = np.random.default_rng([zlib.crc32(name.encode()), seed]).standard_normal(out[name].shape)
        drawn = base * np.exp(spread * noise) if base else spread * noise
        out[name] = __import__('jax').numpy.asarray(drawn.astype(out[name].dtype))
    for name, factor in factors.items():
        out[name] = (out[name] * factor).astype(out[name].dtype)
    return out
```

```python
import concourse.bass as bass
from concourse import mybir
from contextlib import ExitStack

D = 1024
T = 256
NS = 8
N = T + NS
P = 128
KC = D // P
L = 2
WA = 512
AC = WA // P
H = 4
U = 3072 // P
F = 2816
FC = F // P
NE = 8
CW = 4
EPS = 1e-6
COND = 1 + NS
LOT = 128
MAXLOTS = NE + 2 * N // (LOT + 1)
G = F // 256
R = 9
SLAB = 2048
LEVELS = 8


def trunk(nc, a, o):
    fp32 = mybir.dt.float32
    i32 = mybir.dt.int32
    u32 = mybir.dt.uint32
    ALU = mybir.AluOpType
    ACT = mybir.ActivationFunctionType
    AX = mybir.AxisListType

    ctx = ExitStack()
    with ctx:
        def sb(name, shape, dt=fp32):
            return ctx.enter_context(nc.sbuf_tensor(name, shape, dt))

        def sem(name):
            return ctx.enter_context(nc.semaphore(name))

        ring = sb("ring", [P, R, SLAB])
        xT = sb("xT", [P, KC, N])
        hT = sb("hT", [P, KC, N])
        par = sb("par", [P, 5 * P])
        modT = sb("modT", [P, L, 6 * KC, COND])
        uT = sb("uT", [P, U * N])
        mixed = nc.sbuf_base
        yT = sb("yT", [P, KC, N])
        AT = sb("AT", [P, 2, H, P])
        ATx = sb("ATx", [P, H, P])
        vtok = sb("vtok", [P, 2, H, P])
        S = sb("S", [P, NS * H, P])
        oT = sb("oT", [P, H, N])
        bT = sb("bT", [P, H, T])
        xaP = sb("xaP", [P, AC, CW - 1 + T])
        gw = sb("gw", [P, 2, AC, P])
        mixed_end = nc.sbuf_base
        short = nc.sbuf_base
        ar = sb("ar", [P, 7 * H * N])
        mask = sb("mask", [P, LEVELS, P], mybir.dt.uint8)
        ident = sb("ident", [P, P])
        ones = sb("ones", [P, P])
        mean = {w: sb(f"mean{w}", [P, P]) for w in (D, WA, P)}
        before = sb("before", [P, P])
        rtr = sb("rtr", [P, KC, NE])
        rs = sb("rs", [P, N])
        modA = sb("modA", [P, KC, COND])
        cond = sb("cond", [P, KC, COND])
        lb = sb("lb", [P, L, H])
        omlb = sb("omlb", [P, L, H])
        coef = sb("coef", [P, L, AC])
        sm = sb("sm", [P, 16, 16])
        iota = sb("iota", [P, P])
        outc = sb("outc", [P, 80])
        outr = [sb(f"outr{l}", [80, P]) for l in range(L)]
        eps = sb("eps", [P, 1])
        ridx = sb("ridx", [P, 3, NE], u32)
        gsl = sb("gsl", [P, 3, 2])
        wts = sb("wts", [P, 3, 2])
        tab = sb("tab", [P, 8], i32)
        f32r = mybir.dt.float32r

        def split_at(name, n, offset, words):
            return [[nc.alloc_sbuf_tensor_at(f"{name}_{part}{i}", [P, words], f32r,
                                             offset=offset + 4 * words * (2 * i + x))
                     for i in range(n)] for x, part in enumerate(("hi", "lo"))]

        assert 6 * 4 * SLAB <= mixed_end - mixed
        wH, wL = split_at("slab", 3, mixed, SLAB)
        (hH,), (hL,) = split_at("tokens", 1, short + 4 * 4608, 1024)
        aH, aL = split_at("act", 2, short, 256)
        ps = [ctx.enter_context(nc.psum_tensor(f"ps{i}", [P, 512], fp32)) for i in range(8)]

        u = uT[:, :].rearrange("p (c n) -> p c n", n=N)
        XA, GA, QB, FB, IB, GB = (u[:, 4 * i:4 * i + 4, :] for i in range(6))
        prow = uT[:, 0:5 * P].rearrange("p (t c) -> p t c", c=P)
        xrow = uT[:, 1024:1024 + 3 * D].rearrange("p (t c) -> p t c", c=D)
        modrow = uT[0:COND, 0:24 * P]
        yrow = xrow
        act = uT[:, 0:FC * N].rearrange("p (c n) -> p c n", n=N)
        h2tok = uT[:, 0:3 * D].rearrange("p (t c) -> p t c", c=D)
        acc = uT[:, 3 * D:3 * D + KC * N].rearrange("p (c n) -> p c n", n=N)
        rt = uT[:, 5184:5184 + 24 * 3 * NE].rearrange("p (n t e) -> p n t e", t=3, e=NE)
        W4 = H * N

        def lot(i):
            return ar[:, i * W4:(i + 1) * W4].rearrange("p (h n) -> p h n", n=N)

        xc, rg, ig, ag, mu, gt, g2 = (lot(i) for i in range(7))
        LD = [ar[:, 1024 * i:1024 * (i + 1)] for i in range(2)]
        LW = [ar[:, 2048 + 1024 * i:3072 + 1024 * i] for i in range(2)]
        keT = ar[:, 4096:5120].rearrange("p (t h d) -> p t h d", t=2, h=H)
        ke = ar[:, 5120:6144].rearrange("p (h t) -> p h t", h=H)
        vbk = ar[:, 6144:6656].rearrange("p (g e) -> p g e", e=P)
        hgH, hgL = (x[:, :].rearrange("p (c j) -> p c j", j=LOT) for x in (hH, hL))
        ytok = ar[:, 1024:2048]
        sg = [ar[:, 2048 + 256 * i:2304 + 256 * i].rearrange("p (m j) -> p m j", m=2) for i in range(2)]
        ac = [ar[:, 2560 + 256 * i:2816 + 256 * i].rearrange("p (m j) -> p m j", m=2) for i in range(2)]
        sel = ar[:, 3072:3456].rearrange("p (t j) -> p t j", j=LOT)
        gat = ar[:, 3456:3840].rearrange("p (t j) -> p t j", j=LOT)
        gatT = ar[:, 3840:3840 + N]
        stmp = ar[:, 4224:4608].rearrange("p (t j) -> p t j", j=LOT)
        fsg = [ar[:, 4608 + N * i:4608 + N * (i + 1)] for i in range(2)]
        sfin = ar[:, 5120:5632]

        MODB, G1, G2 = 0, 96, 112
        CWW, CB, BA, BX, LAM, OG, LBL, HG, FG, CP = 128, 160, 168, 176, 184, 192, 200, 208, 216, 224
        CS, SH, SCV = 256, 320, 384

        class Stream:
            def __init__(self):
                self.pos = self.n = 0
                self.loads = [0] * R
                self.user = [None] * R

            def take(self):
                s = self.pos % R
                before_, self.user[s] = self.user[s], self.n
                self.pos += 1
                self.n += 1
                self.loads[s] += 1
                return s, self.loads[s], before_

            def align(self):
                self.pos += -self.pos % R

        IT = 4 * R
        LS = 3 * G

        full = [sem(f"slot_full{i}") for i in range(R)]
        used = sem("slab_used")
        s_row = sem("param_rows_loaded")
        s_xrow = sem("x_rows_loaded")
        s_gw = sem("gate_weights_loaded")
        s_gwz = sem("gate_weights_cleared")
        s_S = sem("sample_state_loaded")
        s_cst = sem("constants_ready")
        s_parT = sem("param_transposed")
        s_par = sem("param_ready")
        s_xTp = sem("x_transposed")
        s_xT = sem("x_ready")
        s_act0 = sem("setup_act")
        s_dve0 = sem("setup_dve")
        s_cond = sem("cond_ready")
        s_mev = sem("mod_rows")
        s_mtr = sem("mod_transposed")
        s_mod = sem("mod_ready")
        s_sq = sem("squares_ready")
        s_ms = sem("mean_square_ready")
        s_rs = sem("rsqrt_ready")
        s_h = sem("h_ready")
        s_up = sem("u_psum")
        s_u = sem("u_evacuated")
        s_fe = sem("f_exp")
        s_f = sem("f_ready")
        s_lnf = sem("ln_f")
        s_tq = sem("tanh_q")
        s_xc = sem("conv_ready")
        s_gp = sem("gate_psum")
        s_tg = sem("gate_tanh")
        s_rdy = sem("r_ready")
        s_a = sem("a_ready")
        s_m2 = sem("mult_squared")
        s_mu = sem("mult_ready")
        s_gi = sem("gelu_inner")
        s_tge = sem("gelu_tanh")
        s_tgb = sem("tanh_gb")
        s_z = sem("z_ready")
        s_zs = sem("z_squared")
        s_b = sem("b_ready")
        s_ld = sem("level_diff")
        s_le = sem("level_exp")
        s_lw = sem("level_operand")
        s_lp = sem("level_psum")
        s_lc = sem("level_copied")
        s_vp = sem("v_transposed")
        s_v = sem("vtok_ready")
        s_kx = sem("ke_exp")
        s_ke = sem("ke_ready")
        s_kp = sem("ke_transposed")
        s_keT = sem("keT_ready")
        s_sf = sem("final_state_psum")
        s_sfs = sem("final_state_ready")
        s_op = sem("o_psum")
        s_o = sem("o_evacuated")
        s_vb = sem("v_broadcast")
        s_vbd = sem("v_broadcast_used")
        s_S1 = sem("decayed_state")
        s_osp = sem("o_sample_psum")
        s_os = sem("o_squared")
        s_oms = sem("o_mean_square")
        s_ors = sem("o_rsqrt")
        s_y = sem("y_ready")
        s_wp = sem("w_out_psum")
        s_x1 = sem("residual_chunk")
        s_x = sem("x_updated")
        s_oc = sem("vector_outputs")
        s_ocp = sem("vector_outputs_transposed")
        s_or = sem("vector_output_rows")
        s_fp = sem("ffn_up_psum")
        s_fs = sem("ffn_silu")
        s_fa = sem("ffn_act")
        s_fd = sem("ffn_down_psum")
        s_fx = sem("ffn_down_used")
        s_lg = sem("logits_psum")
        s_lgc = sem("logits_used")
        s_htp = sem("h2_transposed")
        s_htk = sem("h2tok_ready")
        s_red = sem("router_exp_in")
        s_re = sem("router_exp")
        s_msk = sem("choice_mask")
        s_rk = sem("ranks_psum")
        s_tab = sem("lot_table")
        s_sel = sem("lot_choice")
        s_gth = sem("gather_psum")
        s_hgH = sem("gathered_hi")
        s_hgL = sem("gathered_lo")
        s_hi = sem("slab_hi")
        s_lo = sem("slab_lo")
        s_aT = sem("moe_act_transposed")
        s_aH = sem("moe_act_hi")
        s_aL = sem("moe_act_lo")
        s_gTp = sem("gate_transposed")
        s_gT = sem("gateT_ready")
        s_mus = sem("moe_silu")
        s_mua = sem("moe_act")
        s_yt = sem("moe_y_ready")
        s_sc = sem("scatter_psum")
        s_scd = sem("scatter_added")
        s_rtr = sem("router_loaded")
        s_moe = sem("moe_done")
        s_fin = sem("final_x")
        s_ft = sem("final_transposed")
        s_fr = sem("final_rows")
        s_out = sem("outputs_stored")
        c_dve = sem("dve_chain")
        c_lot = sem("choice_step")
        c_act = sem("act_chain")
        c_pool = sem("pool_chain")
        outs = [0]

        class Chain:
            def __init__(self, eng, s, base=0):
                self.eng, self.s, self.n, self.base = eng, s, 0, base

            def __call__(self, ins):
                self.n += 1
                ins.then_inc(self.s, 1)
                self.eng.wait_ge(self.s, self.base + self.n)

        def wide(x, n):
            return x.unsqueeze(len(x.shape)).broadcast_to(list(x.shape) + [n])

        def slots(eng, i):
            def at(t):
                s = t % R
                per = len(range(s, LS, R))
                eng.wait_ge(full[s], i * (16 * per) + 16 * (LOADS[s] + t // R + 1))
                return ring[:, s, :]
            return at

        block = ctx.enter_context(nc.Block())

        @block.sync
        def _(sp):
            st = Stream()

            def load(src, base_used=None):
                s, _, prev = st.take()
                if prev is not None:
                    sp.wait_ge(used, prev + 1)
                w = src.shape[1] * src.shape[2]
                dst = ring[:, s, 0:w].rearrange("p (k n) -> p k n", k=src.shape[1])
                sp.dma_start(dst, src).then_inc(full[s], 16)

            for l in range(L):
                for g in range(24):
                    load(a["mod_w"][l].rearrange("(k p) n -> p k n", p=P)[:, :, g * 256:(g + 1) * 256])
            for l in range(L):
                for g in ORDER_SLABS:
                    load(a["w_in"][l].rearrange("(k p) n -> p k n", p=P)[:, :, g * 256:(g + 1) * 256])
                for g in range(4):
                    load(a["w_out"][l].rearrange("(k p) n -> p k n", p=P)[:, :, g * 256:(g + 1) * 256])
                if l == 0:
                    for g in range(G):
                        for w in ("ffn_w1", "ffn_w3"):
                            load(a[w][0].rearrange("(k p) n -> p k n", p=P)[:, :, g * 256:(g + 1) * 256])
                    for q in range(4):
                        for k0, k1 in DOWN:
                            load(a["ffn_w2"][0].rearrange("(k p) n -> p k n", p=P)
                                 [:, k0:k1, q * 256:(q + 1) * 256])
            st.align()
            held = dict(enumerate(st.user))
            w1 = a["moe_w1"][0].rearrange("e (k p) n -> p e k n", p=P)
            w3 = a["moe_w3"][0].rearrange("e (k p) n -> p e k n", p=P)
            w2 = a["moe_w2"][0].rearrange("e (k p) n -> p e k n", p=P)

            def lot_slabs(e, i, first_lot):
                last = [None] * R
                for t in range(LS):
                    last[t % R] = t
                cur = list(last)
                new = [False] * R
                for t, (kind, g) in enumerate(LOT_ORDER):
                    s = t % R
                    if new[s]:
                        sp.wait_ge(s_lo, i * LS + cur[s] + 1)
                    elif first_lot:
                        sp.wait_ge(used, held[s] + 1)
                    else:
                        sp.wait_ge(s_lo, i * LS - LS + cur[s] + 1)
                    cur[s], new[s] = t, True
                    if kind == 2:
                        src = w2[:, bass.ds(e, 1), 2 * g:2 * g + 2, :].rearrange("p e k n -> p (e k) n")
                        dst = ring[:, s, :].rearrange("p (k n) -> p k n", k=2)
                    else:
                        src = (w1, w3)[kind][:, bass.ds(e, 1), :, g * 256:(g + 1) * 256]\
                            .rearrange("p e k n -> p (e k) n")
                        dst = ring[:, s, :].rearrange("p (k n) -> p k n", k=KC)
                    sp.dma_start(dst, src).then_inc(full[s], 16)

            lot_slabs(0, 0, True)
            with sp.Fori(1, NE) as i:
                lot_slabs(i, i, False)
            sp.wait_ge(s_tab, 1)
            lots = sp.value_load(tab[0:1, 0:1], min_val=NE, max_val=MAXLOTS)
            with sp.If(lots > NE):
                with sp.Fori(NE, lots) as i:
                    e = sp.value_load(tab[0:1, bass.ds(i - (NE - 1), 1)], min_val=0, max_val=NE - 1)
                    lot_slabs(e, i, False)

        @block.gpsimd
        def _(pool):
            ch = Chain(pool, c_pool)
            g = nc.gpsimd
            g.memset(gw[:], 0.0).then_inc(s_gwz, 1)
            ch(g.memset(ident[:], 0.0))
            ch(g.affine_select(out=ident[:], in_=ident[:], compare_op=ALU.not_equal, fill=1.0, base=0,
                               pattern=[[-1, P]], channel_multiplier=1))
            ch(g.memset(before[:], 1.0))
            ch(g.affine_select(out=before[:], in_=before[:], compare_op=ALU.is_gt, fill=0.0, base=0,
                               pattern=[[1, P]], channel_multiplier=-1))
            ch(g.memset(ones[:], 1.0))
            for w in (D, WA, P):
                ch(g.memset(mean[w][:], 1.0 / w))
            ch(g.memset(eps[:], EPS))
            ch(g.iota(iota[:], pattern=[[1, P]], base=0, channel_multiplier=0,
                      allow_small_or_imprecise_dtypes=True))
            ch(g.iota(ar[:, 0:P].bitcast(i32), pattern=[[1, P]], base=0, channel_multiplier=0))
            ch(g.iota(ar[:, P:2 * P].bitcast(i32), pattern=[[0, P]], base=0, channel_multiplier=1))
            ch(g.memset(AT[:], 0.0))
            g.memset(xaP[:, :, 0:CW - 1], 0.0).then_inc(s_cst, 1)
            for l in range(L):
                pool.wait_ge(s_S, 16 * (l + 1))
                pool.wait_ge(s_f, l + 1)
                fb = FB[:, :, T:N].rearrange("p h b -> p b h")
                for b in range(NS):
                    ins = g.tensor_tensor(out=S[:, b * H:(b + 1) * H, :], in0=S[:, b * H:(b + 1) * H, :],
                                          in1=wide(fb[:, b, :], P), op=ALU.mult)
                ins.then_inc(s_S1, 1)

        @block.tensor
        def _(pe):
            st = Stream()
            mm = nc.tensor.matmul

            def slab():
                s, n, _ = st.take()
                pe.wait_ge(full[s], 16 * n)
                return ring[:, s, :]

            pe.wait_ge(s_cst, 1)
            pe.wait_ge(s_row, 16 * PARAM_LOADS)
            for t, rows in enumerate((P, 104, P, 96, 96)):
                last = nc.tensor.transpose(ps[t // 4][:, t % 4 * P:t % 4 * P + rows], prow[0:rows, t, :],
                                           ident[0:rows, 0:rows])
            last.then_inc(s_parT, 1)
            pe.wait_ge(s_xrow, 16 * 2)
            for c in range(KC):
                b = ps[2 + c % 4]
                if c >= 4:
                    pe.wait_ge(s_xT, c - 3)
                for t in range(2):
                    nc.tensor.transpose(b[:, t * P:(t + 1) * P], xrow[:, t, c * P:(c + 1) * P], ident[:])
                nc.tensor.transpose(b[:, T:N], xrow[0:NS, 2, c * P:(c + 1) * P], ident[0:NS, 0:NS])\
                    .then_inc(s_xTp, 1)

            pe.wait_ge(s_cond, 1)
            for l in range(L):
                for half in range(2):
                    for g in range(12):
                        n = 24 * l + 12 * half + g
                        w = slab()[:, 0:2048].rearrange("p (k n) -> p k n", k=KC)
                        if n >= 2:
                            pe.wait_ge(s_mev, n - 1)
                        for k in range(KC):
                            last = mm(ps[6 + g % 2][0:COND, 0:256], cond[:, k, :], w[:, k, :],
                                      start=(k == 0), stop=(k == KC - 1))
                        last.then_inc(used, 1)
                    pe.wait_ge(s_mev, 24 * l + 12 * half + 12)
                    if l or half:
                        pe.wait_ge(s_mod, 2 * l + half)
                    for c in range(24):
                        last = nc.tensor.transpose(ps[1][:, c * COND:(c + 1) * COND],
                                                   modrow[:, c * P:(c + 1) * P], ident[0:COND, 0:COND])
                    last.then_inc(s_mtr, 1)

            def mean_square(n, l):
                pe.wait_ge(s_sq, n)
                for k in range(KC):
                    last = mm(ps[0][:, 0:N], mean[D][:], yT[:, k, :], start=(k == 0), stop=(k == KC - 1))
                last.then_inc(s_ms, 1)

            def layer(l):
                mean_square(2 * l + 1, l)
                pe.wait_ge(s_h, 2 * l + 1)
                j = 0
                for grp in ORDER:
                    for half in range(2):
                        w = slab()[:, 0:2048].rearrange("p (k n) -> p k n", k=KC)
                        for m in range(2):
                            if j >= 4:
                                pe.wait_ge(s_u, U * l + j - 3)
                            for k in range(KC):
                                last = mm(ps[j % 4][:, 0:N], w[:, k, m * P:(m + 1) * P], hT[:, k, :],
                                          start=(k == 0), stop=(k == KC - 1))
                            if m == 0:
                                last.then_inc(s_up, 1)
                            j += 1
                        last.then_inc(used, 1)
                    if grp == 4:
                        pe.wait_ge(s_u, U * l + j)
                        for t in range(2):
                            for h in range(H):
                                last = nc.tensor.transpose(ps[4 + t][:, h * P:(h + 1) * P],
                                                           IB[:, h, t * P:(t + 1) * P], ident[:])
                        last.then_inc(s_vp, 1)
                        pe.wait_ge(s_v, l + 1)
                        pe.wait_ge(s_xc, l + 1)
                        pe.wait_ge(s_gw, 64 * (l + 1))
                        for c in range(AC):
                            for w in range(2):
                                b = 4 + (2 * c + w) % 4
                                if c >= 2:
                                    pe.wait_ge(s_tg, 8 * l + 2 * c + w - 3)
                                mm(ps[b][:, 0:N], gw[:, w, c, :], xc[:, c, :], start=True, stop=True)\
                                    .then_inc(s_gp, 1)
                pe.wait_ge(s_u, U * (l + 1))
                pe.wait_ge(s_zs, l + 1)
                for c in range(AC):
                    last = mm(ps[7][:, 0:N], mean[WA][:], g2[:, c, :], start=(c == 0), stop=(c == AC - 1))
                last.then_inc(s_ms, 1)
                for v in range(LEVELS + 1):
                    pe.wait_ge(s_lw, (LEVELS + 1) * l + v + 1)
                    if v >= 2:
                        pe.wait_ge(s_lc, (LEVELS + 1) * l + v - 1)
                    lw = LW[v % 2].rearrange("p (h t) -> p h t", h=H)
                    if v == LEVELS:
                        for h in range(H):
                            last = mm(ps[2 * (v % 2)][:, h * P:(h + 1) * P], lw[:, h, 0:P], lw[:, h, P:T],
                                      start=True, stop=True)
                    else:
                        for t in range(2):
                            for h in range(H):
                                kk = lw[:, h, t * P:(t + 1) * P] if v else FB[:, h, t * P:(t + 1) * P]
                                qq = lw[:, h, t * P:(t + 1) * P] if v else QB[:, h, t * P:(t + 1) * P]
                                last = mm(ps[2 * (v % 2) + t][:, h * P:(h + 1) * P], kk, qq,
                                          start=True, stop=True)
                    last.then_inc(s_lp, 1)
                pe.wait_ge(s_ke, l + 1)
                for t in range(2):
                    for h in range(H):
                        last = nc.tensor.transpose(ps[4 + t][:, h * P:(h + 1) * P], ke[:, h, t * P:(t + 1) * P],
                                                   ident[:])
                last.then_inc(s_kp, 1)
                pe.wait_ge(s_lc, (LEVELS + 1) * (l + 1))
                for h in range(H):
                    b = ps[h // 2]
                    w = h % 2 * T
                    mm(b[:, w:w + P], vtok[:, 0, h, :], AT[:, 0, h, :], start=True, stop=True)
                    mm(b[:, w + P:w + T], vtok[:, 0, h, :], ATx[:, h, :], start=True, stop=False)
                    last = mm(b[:, w + P:w + T], vtok[:, 1, h, :], AT[:, 1, h, :], start=False, stop=True)
                last.then_inc(s_op, 1)
                pe.wait_ge(s_keT, l + 1)
                for h in range(H):
                    for t in range(2):
                        last = mm(ps[6][:, h * P:(h + 1) * P], keT[:, t, h, :], vtok[:, t, h, :],
                                  start=(t == 0), stop=(t == 1))
                last.then_inc(s_sf, 1)
                for b in range(NS):
                    if b >= 2:
                        pe.wait_ge(s_vbd, NS * l + b - 1)
                    for h in range(H):
                        last = mm(ps[2 + b % 2][:, h * P:(h + 1) * P],
                                  IB[:, h, T + b:T + b + 1].broadcast_to([P, P]), ident[:],
                                  start=True, stop=True)
                    last.then_inc(s_vb, 1)
                pe.wait_ge(s_vbd, NS * (l + 1))
                pe.wait_ge(s_keT, l + 1)
                for b in range(NS):
                    for h in range(H):
                        c = h * NS + b
                        last = mm(ps[4][:, c:c + 1], S[:, b * H + h, :], QB[:, h, T + b:T + b + 1],
                                  start=True, stop=True)
                last.then_inc(s_osp, 1)
                pe.wait_ge(s_os, l + 1)
                for h in range(H):
                    last = mm(ps[h][:, 0:N], mean[P][:], yT[:, AC + h, :], start=True, stop=True)
                last.then_inc(s_oms, 1)
                pe.wait_ge(s_y, l + 1)
                for g in range(4):
                    w = slab()[:, 0:2048].rearrange("p (k n) -> p k n", k=KC)
                    for m in range(2):
                        c = 2 * g + m
                        if c >= 4:
                            pe.wait_ge(s_x1, KC * l + c - 3)
                        for k in range(KC):
                            last = mm(ps[c % 4][:, 0:N], w[:, k, m * P:(m + 1) * P], yT[:, k, :],
                                      start=(k == 0), stop=(k == KC - 1))
                        if m == 0:
                            last.then_inc(s_wp, 1)
                    last.then_inc(used, 1)
                pe.wait_ge(s_oc, l + 1)
                nc.tensor.transpose(ps[6][0:80, 0:P], outc[:, :], ident[:]).then_inc(s_ocp, 1)
                mean_square(2 * l + 2, l)
                pe.wait_ge(s_h, 2 * l + 2)

            def dense():
                for g in range(G):
                    w1 = slab()[:, 0:2048].rearrange("p (k n) -> p k n", k=KC)
                    w3 = slab()[:, 0:2048].rearrange("p (k n) -> p k n", k=KC)
                    for m in range(2):
                        c = 2 * g + m
                        if c >= 3:
                            pe.wait_ge(s_fa, c - 2)
                        for x, w in enumerate((w1, w3)):
                            for k in range(KC):
                                last = mm(ps[c % 3 * 2 + x][:, 0:N], w[:, k, m * P:(m + 1) * P], hT[:, k, :],
                                          start=(k == 0), stop=(k == KC - 1))
                            if m == 0 and x == 1:
                                last.then_inc(s_fp, 1)
                            elif m == 1:
                                last.then_inc(used, 1)
                pe.wait_ge(s_fa, FC)
                for q in range(4):
                    if q >= 2:
                        pe.wait_ge(s_fx, 2 * q - 2)
                    for i, (k0, k1) in enumerate(DOWN):
                        w = slab()[:, 0:(k1 - k0) * 256].rearrange("p (k n) -> p k n", k=k1 - k0)
                        for m in range(2):
                            for k in range(k0, k1):
                                last = mm(ps[q % 2 * 2 + m][:, 0:N], w[:, k - k0, m * P:(m + 1) * P],
                                          act[:, k, :], start=(k == 0), stop=(k == FC - 1))
                            if i == 2 and m == 0:
                                last.then_inc(s_fd, 1)
                        last.then_inc(used, 1)

            def route():
                rows = (P, P, NS)
                pe.wait_ge(s_rtr, 16)
                for t in range(3):
                    for k in range(KC):
                        last = mm(ps[1][0:rows[t], t * NE:(t + 1) * NE], hT[:, k, t * P:t * P + rows[t]],
                                  rtr[:, k, :], start=(k == 0), stop=(k == KC - 1))
                last.then_inc(s_lg, 1)
                for t in range(3):
                    for q in range(2):
                        n = 2 * t + q
                        if n >= 2:
                            pe.wait_ge(s_htk, n - 1)
                        for c in range(4):
                            last = nc.tensor.transpose(ps[2 + n % 2][0:rows[t], c * P:(c + 1) * P],
                                                       hT[:, 4 * q + c, t * P:t * P + rows[t]], ident[:])
                        last.then_inc(s_htp, 1)
                pe.wait_ge(s_msk, 1)
                m = rt[:, 2]
                for t in range(3):
                    o_ = ps[0][0:rows[t], t * NE:(t + 1) * NE]
                    for s in range(t):
                        mm(o_, ones[:, 0:rows[t]], m[:, s, :], start=(s == 0), stop=False)
                    mm(o_, before[0:rows[t], 0:rows[t]], m[0:rows[t], t, :], start=(t == 0), stop=True)
                for t in range(3):
                    last = mm(ps[0][:, 3 * NE:4 * NE], ones[0:rows[t], :], m[0:rows[t], t, :],
                              start=(t == 0), stop=(t == 2))
                last.then_inc(s_rk, 1)

            def gather(n, q):
                pe.wait_ge(s_sel, n + 1)
                for c in range(4 * q, 4 * q + 4):
                    for t in range(3):
                        last = mm(ps[7][:, c % 4 * P:c % 4 * P + P],
                                  h2tok[0:ROWS[t], t, c * P:(c + 1) * P], sel[0:ROWS[t], t, :],
                                  start=(t == 0), stop=(t == 2))
                last.then_inc(s_gth, 1)

            def turn_gates():
                for t in range(3):
                    last = nc.tensor.transpose(ps[7][:, t * P:t * P + ROWS[t]], gat[0:ROWS[t], t, :],
                                               ident[0:ROWS[t], 0:ROWS[t]])
                last.then_inc(s_gTp, 1)

            def products(out, x, xl, w, wl, start, stop):
                mm(out, x, w, start=start, stop=False)
                mm(out, x, wl, start=False, stop=False)
                return mm(out, xl, w, start=False, stop=stop)

            def moe():
                pe.wait_ge(s_tab, 1)
                lots = pe.value_load(tab[0:1, 0:1], min_val=NE, max_val=MAXLOTS)
                pe.wait_ge(s_htk, 6)
                gather(0, 0)
                pe.wait_ge(s_hgL, 1)
                gather(0, 1)
                with pe.Fori(0, lots) as i:
                    pe.wait_ge(s_hgL, i * 2 + 2)
                    for t, (kind, g) in enumerate(LOT_ORDER):
                        b = t % 3
                        pe.wait_ge(s_lo, i * LS + t + 1)
                        if kind < 2:
                            if g >= 2:
                                pe.wait_ge(s_mua, i * G + g - 1)
                            h_, l_ = (x[b][:, :].rearrange("p (k n) -> p k n", k=KC) for x in (wH, wL))
                            for k in range(KC):
                                last = products(ps[2 * kind + g % 2][:, 0:256], hgH[:, k, :], hgL[:, k, :],
                                                h_[:, k, :], l_[:, k, :], k == 0, k == KC - 1)
                        else:
                            if g == 0:
                                pe.wait_ge(s_yt, i * 2 + 2)
                            pe.wait_ge(s_aL, i * G + g + 1)
                            h_, l_ = (x[b][:, :].rearrange("p (k n) -> p k n", k=2) for x in (wH, wL))
                            for m in range(2):
                                js = slice(m * LOT, (m + 1) * LOT)
                                for n in range(2):
                                    cs = slice(n * 512, (n + 1) * 512)
                                    last = products(ps[4 + n][:, :], aH[g % 2][:, js], aL[g % 2][:, js],
                                                    h_[:, m, cs], l_[:, m, cs],
                                                    g == 0 and m == 0, g == G - 1 and m == 1)
                        last.then_inc(used, 1)
                        if t in TURN_AT:
                            g = TURN_AT[t]
                            pe.wait_ge(s_mua, i * G + g + 1)
                            for m in range(2):
                                last = nc.tensor.transpose(ps[6][:, m * P:(m + 1) * P], ac[g % 2][:, m, :],
                                                           ident[:])
                            last.then_inc(s_aT, 1)
                        if t in SCATTER_AT:
                            c = SCATTER_AT[t]
                            pe.wait_ge(s_gT, i + 1)
                            pe.wait_ge(s_scd, i * KC + c + 1)
                            mm(ps[7][:, 0:N], ytok[:, c * P:(c + 1) * P], gatT, start=True, stop=True)\
                                .then_inc(s_sc, 1)
                        if t == GATES_AT:
                            pe.wait_ge(s_scd, i * KC + KC + 1)
                            turn_gates()
                        if t == LS - 3:
                            pe.wait_ge(s_gT, i + 2)
                            gather(i + 1, 0)
                        if t == LS - 2:
                            pe.wait_ge(s_hgL, i * 2 + 3)
                            gather(i + 1, 1)
                pe.wait_ge(s_yt, lots * 2 + 2)
                pe.wait_ge(s_hgL, lots * 2 + 2)
                for c in range(KC):
                    if c >= 2:
                        pe.wait_ge(s_scd, lots * KC + c)
                    mm(ps[6 + c % 2][:, 0:N], ytok[:, c * P:(c + 1) * P], gatT, start=True, stop=True)\
                        .then_inc(s_sc, 1)

            layer(0)
            dense()
            layer(1)
            route()
            st.align()
            assert st.n == SLABS
            moe()
            pe.wait_ge(s_sq, 2 * L + 1)
            for k in range(KC):
                last = mm(ps[0][:, 0:N], mean[D][:], yT[:, k, :], start=(k == 0), stop=(k == KC - 1))
            last.then_inc(s_ms, 1)
            pe.wait_ge(s_fin, 1)
            rows = (P, P, NS)
            for t in range(3):
                for q in range(2):
                    n = 2 * t + q
                    if n >= 2:
                        pe.wait_ge(s_fr, n - 1)
                    for c in range(4):
                        last = nc.tensor.transpose(ps[2 + n % 2][0:rows[t], c * P:(c + 1) * P],
                                                   hT[:, 4 * q + c, t * P:t * P + rows[t]], ident[:])
                    last.then_inc(s_ft, 1)

        @block.scalar
        def _(act_):
            A = nc.scalar.activation
            ch = Chain(act_, c_act)

            def rows(name, tile, r0, src, n):
                act_.dma_start(prow[r0:r0 + n, tile, :], src).then_inc(s_row, 16)

            def flat(x, names):
                return x.rearrange(names, p=P)

            rows("mod_b", 0, 0, flat(a["mod_b"], "l (c p) -> (l c) p"), 96)
            rows("g1", 0, 96, flat(a["norm1_g"], "l (c p) -> (l c) p"), 16)
            rows("g2", 0, 112, flat(a["norm2_g"], "l (c p) -> (l c) p"), 16)
            rows("cw", 1, 0, flat(a["conv_w"], "l j (c p) -> (l j c) p"), 32)
            for n_, (name, r0) in enumerate((("conv_b", 32), ("rg_ba", 40), ("rg_bx", 48), ("rg_lambda", 56),
                                             ("rg_out_g", 64), ("hg_lb_logits", 72), ("hg_norm_g", 80))):
                rows(name, 1, r0, flat(a[name], "l (c p) -> (l c) p"), 8)
            rows("final_g", 1, 88, a["final_g"].rearrange("(c p) -> c p", p=P), 8)
            rows("c_prompt", 1, 96, flat(a["c_prompt"], "b (c p) -> (b c) p"), 8)
            rows("c_sample", 2, 0, flat(a["c_sample"], "b (c p) -> (b c) p"), 64)
            rows("state_h", 2, 64, flat(a["state_rglru_h"], "l b (c p) -> (l b c) p"), 64)
            for l in range(L):
                rows("conv", 3 + l, 0, flat(a["state_rglru_conv"][l], "b j (c p) -> (b j c) p"), 96)
            act_.dma_start(xrow[:, 0:2, :], a["x_prompt"][0].rearrange("(t p) c -> p t c", p=P))\
                .then_inc(s_xrow, 16)
            act_.dma_start(xrow[0:NS, 2, :], a["x_sample"].rearrange("b t c -> (b t) c")).then_inc(s_xrow, 16)
            act_.dma_start(S[:, :, :], a["state_hgrn"][0].rearrange("b h d e -> d (b h) e")).then_inc(s_S, 16)
            act_.dma_start(rtr[:, :, :], a["router_w"][0].rearrange("(k p) e -> p k e", p=P)).then_inc(s_rtr, 16)
            for l in range(L):
                act_.dma_start(o["new_conv_sample"][l, :, 0:2, :], a["state_rglru_conv"][l, :, 1:3, :])\
                    .then_inc(s_out, 16)
                outs[0] += 1
            act_.wait_ge(s_gwz, 1)

            def gate_weights(l):
                for x, name in enumerate(("rg_wa", "rg_wx")):
                    for half in range(2):
                        src = a[name][l].rearrange("(c two) i j -> two i c j", two=2)[half]
                        act_.dma_start(gw[64 * half:64 * half + 64, x, :, 64 * half:64 * half + 64], src)\
                            .then_inc(s_gw, 16)

            gate_weights(0)
            act_.wait_ge(s_parT, 1)
            ch(A(par[:, 0:232], ps[0][:, 0:232], ACT.Copy))
            ch(A(par[:, 256:480], ps[0][:, 256:480], ACT.Copy))
            A(par[:, 512:608], ps[1][:, 0:96], ACT.Copy).then_inc(s_par, 1)
            act_.wait_ge(s_par, 1)
            A(cond[:, :, 0], par[:, CP:CP + KC], ACT.Tanh, scale=0.5)
            A(cond[:, :, 1:COND], par[:, CS:CS + 64].rearrange("p (b c) -> p c b", c=KC), ACT.Tanh, scale=0.5)\
                .then_inc(s_act0, 1)
            for c in range(KC):
                act_.wait_ge(s_xTp, c + 1)
                A(xT[:, c, :], ps[2 + c % 4][:, 0:N], ACT.Copy).then_inc(s_xT, 1)
            act_.wait_ge(s_dve0, 1)
            A(sm[:, 1, 0:8], sm[:, 0, 0:8], ACT.Exp, scale=-1.0)
            A(sm[:, 3, 0:8], sm[:, 2, 0:8], ACT.Exp).then_inc(s_act0, 1)

            for l in range(L):
                for half in range(2):
                    if l or half:
                        act_.wait_ge(s_mtr, 2 * l + half)
                    for g in range(12):
                        act_.wait_ge(used, 24 * l + 12 * half + g + 1)
                        A(modrow[:, g * 256:(g + 1) * 256], ps[6 + g % 2][0:COND, 0:256], ACT.Copy)\
                            .then_inc(s_mev, 1)

            def rsqrt(out, in_):
                ch(A(out, in_, ACT.Ln, bias=eps[:, 0:1]))
                return A(out, out, ACT.Exp, scale=-0.5)

            def norm(n):
                if n == 0:
                    act_.wait_ge(s_xT, KC)
                else:
                    act_.wait_ge(s_x, n)
                A(yT[:, :, :], xT[:, :, :], ACT.Square).then_inc(s_sq, 1)

            def layer(l):
                if l:
                    norm(2 * l)
                else:
                    norm(0)
                act_.wait_ge(s_ms, 3 * l + 1)
                rsqrt(rs[:, :], ps[0][:, 0:N]).then_inc(s_rs, 1)
                j = 0
                for grp in ORDER:
                    for m in range(4):
                        if m % 2 == 0:
                            act_.wait_ge(s_up, (U // 2) * l + j // 2 + 1)
                        else:
                            act_.wait_ge(used, 48 + (12 + 4 + 34) * l + j // 2 + 1)
                        dst = xaP[:, m, CW - 1:] if grp == 0 else u[:, 4 * grp + m, :]
                        if grp == 0:
                            ch(A(u[:, m, T:N], ps[j % 4][:, T:N], ACT.Copy))
                            A(dst, ps[j % 4][:, 0:T], ACT.Copy).then_inc(s_u, 1)
                        else:
                            A(dst, ps[j % 4][:, 0:N], ACT.Copy).then_inc(s_u, 1)
                        j += 1
                    if grp == 3:
                        act_.wait_ge(s_u, U * l + j)
                        A(FB, FB, ACT.Exp, scale=-1.0).then_inc(s_fe, 1)
                    if grp == 2:
                        act_.wait_ge(s_f, l + 1)
                        A(oT[:, :, 0:T], oT[:, :, 0:T], ACT.Ln)
                        A(bT[:, :, :], bT[:, :, :], ACT.Ln, scale=2.0 ** 66).then_inc(s_lnf, 1)
                        act_.wait_ge(s_u, U * l + j)
                        A(g2, QB, ACT.Tanh, scale=0.5).then_inc(s_tq, 1)
                    if grp == 4:
                        act_.wait_ge(s_vp, l + 1)
                        ch(A(vtok[:, 0, :, :], ps[4][:, :].rearrange("p (h e) -> p h e", h=H), ACT.Copy))
                        A(vtok[:, 1, :, :], ps[5][:, :].rearrange("p (h e) -> p h e", h=H), ACT.Copy)\
                            .then_inc(s_v, 1)
                        for c in range(AC):
                            for w in range(2):
                                act_.wait_ge(s_gp, 8 * l + 2 * c + w + 1)
                                bias = sm[:, 4 + w, AC * l + c:AC * l + c + 1]
                                A((rg, ig)[w][:, c, :], ps[4 + (2 * c + w) % 4][:, 0:N], ACT.Tanh, bias=bias,
                                  scale=0.5).then_inc(s_tg, 1)
                        act_.wait_ge(s_rdy, l + 1)
                        for c in range(AC):
                            A(ag[:, c, :], rg[:, c, :], ACT.Exp, scale=coef[:, l, c:c + 1])
                        for c in range(AC):
                            ins = A(mu[:, c, :], rg[:, c, :], ACT.Tanh, scale=coef[:, l, c:c + 1])
                        ins.then_inc(s_a, 1)
                act_.wait_ge(s_gi, l + 1)
                A(gt, gt, ACT.Tanh, scale=0.7978845608028654).then_inc(s_tge, 1)
                act_.wait_ge(s_u, U * (l + 1))
                A(oT[:, :, :], GB, ACT.Tanh, scale=0.5).then_inc(s_tgb, 1)
                act_.wait_ge(s_m2, l + 1)
                A(mu, mu, ACT.Sqrt).then_inc(s_mu, 1)
                act_.wait_ge(s_ms, 3 * l + 2)
                rsqrt(rs[:, :], ps[7][:, 0:N]).then_inc(s_rs, 1)
                for v in range(1, LEVELS + 1):
                    act_.wait_ge(s_ld, LEVELS * l + v)
                    A(LD[v % 2], LD[v % 2], ACT.Exp).then_inc(s_le, 1)
                for h in range(H):
                    ins = A(ke[:, h, :], bT[:, h, :], ACT.Exp, scale=-1.0, bias=bT[:, h, T - 1:T])
                ins.then_inc(s_kx, 1)
                act_.wait_ge(s_kp, l + 1)
                ch(A(keT[:, 0], ps[4][:, :].rearrange("p (h e) -> p h e", h=H), ACT.Copy))
                A(keT[:, 1], ps[5][:, :].rearrange("p (h e) -> p h e", h=H), ACT.Copy).then_inc(s_keT, 1)
                act_.wait_ge(s_op, l + 1)
                ch(A(oT[:, 0:2, 0:T], ps[0][:, :].rearrange("p (h t) -> p h t", h=2), ACT.Copy))
                A(oT[:, 2:4, 0:T], ps[1][:, :].rearrange("p (h t) -> p h t", h=2), ACT.Copy)
                act_.wait_ge(s_sf, l + 1)
                act_.wait_ge(s_ke, l + 1)
                act_.wait_ge(s_kp, l + 1)
                A(sfin, ps[6][:, :], ACT.Copy).then_inc(s_sfs, 1)
                act_.wait_ge(s_sfs, l + 1)
                act_.dma_start(o["new_S_prompt"][l, 0].rearrange("h d e -> d h e"),
                               sfin.rearrange("p (h e) -> p h e", h=H)).then_inc(s_out, 16)
                outs[0] += 1
                act_.wait_ge(s_osp, l + 1)
                ch(A(oT[:, :, T:N], ps[4][:, 0:H * NS].rearrange("p (h b) -> p h b", h=H), ACT.Copy))
                A(yT[:, AC:, :], oT[:, :, :], ACT.Square).then_inc(s_os, 1)
                act_.wait_ge(s_vbd, NS * (l + 1))
                act_.dma_start(o["new_S_sample"][l].rearrange("b h d e -> d (b h) e"), S[:, :, :])\
                    .then_inc(s_out, 16)
                outs[0] += 1
                act_.wait_ge(s_oms, l + 1)
                for h in range(H):
                    ch(A(LN_OUT(h), ps[h][:, 0:N], ACT.Ln, bias=eps[:, 0:1]))
                A(ar[:, 0:W4], ar[:, 0:W4], ACT.Exp, scale=-0.5).then_inc(s_ors, 1)
                if l + 1 < L:
                    act_.wait_ge(s_out, 16 * outs[0])
                    act_.wait_ge(s_osp, l + 1)
                    act_.dma_start(S[:, :, :], a["state_hgrn"][l + 1].rearrange("b h d e -> d (b h) e"))\
                        .then_inc(s_S, 16)
                    gate_weights(l + 1)
                act_.wait_ge(s_ocp, l + 1)
                A(outr[l][:, :], ps[6][0:80, 0:P], ACT.Copy).then_inc(s_or, 1)
                act_.wait_ge(s_or, l + 1)
                for dst, r0, n_ in (
                        (o["new_h_prompt"][l, 0].rearrange("(c p) -> c p", p=P), 0, 4),
                        (o["new_h_sample"][l].rearrange("b (c p) -> (b c) p", p=P), 4, 32),
                        (o["new_conv_prompt"][l, 0].rearrange("j (c p) -> (j c) p", p=P), 36, 12)):
                    act_.dma_start(dst, outr[l][r0:r0 + n_, :]).then_inc(s_out, 16)
                    outs[0] += 1
                for b in range(NS):
                    act_.dma_start(o["new_conv_sample"][l, b, CW - 2].rearrange("(c p) -> c p", p=P),
                                   outr[l][48 + 4 * b:52 + 4 * b, :]).then_inc(s_out, 16)
                    outs[0] += 1
                norm(2 * l + 1)
                act_.wait_ge(s_ms, 3 * l + 3)
                rsqrt(rs[:, :], ps[0][:, 0:N]).then_inc(s_rs, 1)

            def LN_OUT(h):
                return ar[:, h * N:(h + 1) * N]

            layer(0)
            for c in range(FC):
                if c % 2 == 0:
                    act_.wait_ge(s_fp, c // 2 + 1)
                else:
                    act_.wait_ge(used, 48 + 16 + c + 1)
                if c >= 2:
                    act_.wait_ge(s_fa, c - 1)
                A(fsg[c % 2], ps[c % 3 * 2][:, 0:N], ACT.Silu).then_inc(s_fs, 1)
            layer(1)
            rws = (P, P, NS)
            for n in range(6):
                act_.wait_ge(s_htp, n + 1)
                A(h2tok[0:rws[n // 2], n // 2, n % 2 * 512:n % 2 * 512 + 512], ps[2 + n % 2][0:rws[n // 2], :],
                  ACT.Copy).then_inc(s_htk, 1)
            act_.wait_ge(s_red, 1)
            A(rt[:, 20, :, 0], rt[:, 19, :, 0], ACT.Exp).then_inc(s_re, 1)
            act_.wait_ge(s_tab, 1)
            lots = act_.value_load(tab[0:1, 0:1], min_val=NE, max_val=MAXLOTS)

            cp = nc.scalar.copy

            def gathered(n, q):
                act_.wait_ge(s_gth, n * 2 + q + 1)
                cp(hgH[:, 4 * q:4 * q + 4, :], ps[7][:, :].rearrange("p (c j) -> p c j", c=4)).then_inc(s_hgH, 1)

            def outputs(n):
                act_.wait_ge(used, n * LS + SLABS)
                for m in range(2):
                    cp(ytok[:, m * 512:(m + 1) * 512], ps[4 + m][:, :]).then_inc(s_yt, 1)

            act_.wait_ge(s_out, 16 * outs[0])
            gathered(0, 0)
            gathered(0, 1)
            with act_.Fori(0, lots) as i:
                slot = slots(act_, i)
                for t in range(LS):
                    w = slot(t)
                    act_.wait_ge(used, i * LS + SLABS + t - 2)
                    cp(wH[t % 3][:, :], w).then_inc(s_hi, 1)
                    if t == 2:
                        outputs(i)
                    if t in FORM_AT:
                        g = FORM_AT[t]
                        act_.wait_ge(used, i * LS + SLABS + LOT_ORDER.index((0, g)) + 1)
                        if g >= 2:
                            act_.wait_ge(s_mua, i * G + g - 1)
                        A(sg[g % 2], ps[g % 2][:, 0:256].rearrange("p (m j) -> p m j", m=2), ACT.Silu)\
                            .then_inc(s_mus, 1)
                    if t == LS - 1:
                        gathered(i + 1, 0)
                    if t in DOWN_AT:
                        g = DOWN_AT[t]
                        act_.wait_ge(s_aT, i * G + g + 1)
                        cp(aH[g % 2][:, :], ps[6][:, 0:256]).then_inc(s_aH, 1)
                gathered(i + 1, 1)
            outputs(lots)
            act_.wait_ge(s_x, 2 * L)
            A(yT[:, :, :], xT[:, :, :], ACT.Square).then_inc(s_sq, 1)
            act_.wait_ge(s_ms, 3 * L + 1)
            rsqrt(rs[:, :], ps[0][:, 0:N]).then_inc(s_rs, 1)
            for n in range(6):
                act_.wait_ge(s_ft, n + 1)
                A(yrow[0:rws[n // 2], n // 2, n % 2 * 512:n % 2 * 512 + 512], ps[2 + n % 2][0:rws[n // 2], :],
                  ACT.Copy).then_inc(s_fr, 1)
            act_.wait_ge(s_fr, 6)
            act_.dma_start(o["y_prompt"][0].rearrange("(t p) c -> p t c", p=P), yrow[:, 0:2, :])\
                .then_inc(s_out, 16)
            act_.dma_start(o["y_sample"].rearrange("b t c -> (b t) c"), yrow[0:NS, 2, :]).then_inc(s_out, 16)
            outs[0] += 2
            act_.wait_ge(s_out, 16 * outs[0])

        @block.vector
        def _(dve):
            V = nc.vector
            ch = Chain(dve, c_dve)
            tt, ts, stt = V.tensor_tensor, V.tensor_scalar, V.scalar_tensor_tensor

            dve.wait_ge(s_cst, 1)
            ti, si, xi = (ar[:, n * P:(n + 1) * P].bitcast(i32) for n in (0, 1, 2))
            ch(tt(xi, ti, si, ALU.bitwise_xor))
            ch(ts(mask[:, 0, :], xi, 0.0, None, ALU.is_equal))
            for v in range(1, LEVELS):
                sh = ar[:, 3 * P:4 * P].bitcast(i32)
                ch(ts(sh, xi, v - 1, None, ALU.logical_shift_right))
                ch(stt(mask[:, v, :], sh, 1.0, before[:], ALU.is_equal, ALU.mult))
            dve.wait_ge(s_par, 1)
            lam = par[:, LAM:LAM + 8]
            ch(stt(sm[:, 0, 0:8], lam, -1.0, lam, ALU.mult, ALU.max))
            l0, l1 = par[:, LBL:LBL + 4], par[:, LBL + 4:LBL + 8]
            ch(tt(sm[:, 6, 0:4], l0, l1, ALU.max))
            ch(tt(sm[:, 2, 0:4], l0, sm[:, 6, 0:4], ALU.subtract))
            tt(sm[:, 2, 4:8], l1, sm[:, 6, 0:4], ALU.subtract).then_inc(s_dve0, 1)
            ts(sm[:, 4, 0:8], par[:, BA:BA + 8], 0.5, None, ALU.mult)
            ch(ts(sm[:, 5, 0:8], par[:, BX:BX + 8], 0.5, None, ALU.mult))
            dve.wait_ge(s_act0, 1)
            ch(stt(cond[:, :, 0], cond[:, :, 0], 1.0, par[:, CP:CP + KC], ALU.add, ALU.mult))
            ch(stt(cond[:, :, 1:COND], cond[:, :, 1:COND], 1.0,
                   par[:, CS:CS + 64].rearrange("p (b c) -> p c b", c=KC), ALU.add, ALU.mult))
            ts(cond[:, :, :], cond[:, :, :], 0.5, None, ALU.mult).then_inc(s_cond, 1)
            dve.wait_ge(s_act0, 2)
            z, q, q2, pz = sm[:, 1, 0:8], sm[:, 7, 0:8], sm[:, 8, 0:8], sm[:, 9, 0:8]
            ch(ts(q, z, 2.0, None, ALU.add))
            ch(V.reciprocal(q, q))
            ch(tt(q, q, z, ALU.mult))
            ch(tt(q2, q, q, ALU.mult))
            ch(ts(pz, q2, 1.0 / 15, 1.0 / 13, ALU.mult, ALU.add))
            for d in (11, 9, 7, 5, 3, 1):
                ch(tt(pz, pz, q2, ALU.mult))
                ch(ts(pz, pz, 1.0 / d, None, ALU.add))
            ch(tt(pz, pz, q, ALU.mult))
            ch(ts(q, lam, -1.0, 0.0, ALU.mult, ALU.max))
            ch(stt(q, pz, 2.0, q, ALU.mult, ALU.add))
            ch(ts(coef[:].rearrange("p l c -> p (l c)"), q, -8.0, None, ALU.mult))
            e = sm[:, 3, 0:8]
            ch(tt(sm[:, 10, 0:4], e[:, 0:4], e[:, 4:8], ALU.add))
            ch(V.reciprocal(sm[:, 10, 0:4], sm[:, 10, 0:4]))
            ch(V.memset(lb[:, 0, :], 0.0))
            ch(tt(lb[:, 1, :], e[:, 4:8], sm[:, 10, 0:4], ALU.mult))
            ch(ts(omlb[:], lb[:], -1.0, 1.0, ALU.mult, ALU.add))
            for l in range(L):
                for half in range(2):
                    dve.wait_ge(s_mtr, 2 * l + half + 1)
                    c0 = 24 * half
                    tt(modT[:, l, c0:c0 + 24, :], ps[1][:, 0:24 * COND].rearrange("p (c b) -> p c b", b=COND),
                       wide(par[:, MODB + 48 * l + c0:MODB + 48 * l + c0 + 24], COND), ALU.add)\
                        .then_inc(s_mod, 1)
            dve.wait_ge(s_mod, 2 * L)

            def modulate(l, which, gcol):
                sc = modT[:, l, (3 * which + 1) * KC:(3 * which + 2) * KC, :]
                shf = modT[:, l, 3 * which * KC:(3 * which + 1) * KC, :]
                ch(stt(modA[:, :, :], sc, 1.0, wide(par[:, gcol + KC * l:gcol + KC * (l + 1)], COND),
                       ALU.add, ALU.mult))
                dve.wait_ge(s_rs, 3 * l + (1 if which == 0 else 3))
                ch(tt(hT[:, :, :], xT[:, :, :], rs[:, :].unsqueeze(1).broadcast_to([P, KC, N]), ALU.mult))
                for c in range(KC):
                    ts(hT[:, c, 0:T], hT[:, c, 0:T], modA[:, c, 0:1], shf[:, c, 0:1], ALU.mult, ALU.add)
                ch(tt(hT[:, :, T:N], hT[:, :, T:N], modA[:, :, 1:COND], ALU.mult))
                tt(hT[:, :, T:N], hT[:, :, T:N], shf[:, :, 1:COND], ALU.add).then_inc(s_h, 1)

            def residual(l, part, c, bank):
                gate = modT[:, l, (3 * part + 2) * KC + c, :]
                stt(xT[:, c, 0:T], bank[:, 0:T], gate[:, 0:1], xT[:, c, 0:T], ALU.mult, ALU.add)
                ch(tt(sm[:, 11, 0:NS], bank[:, T:N], gate[:, 1:COND], ALU.mult))
                return tt(xT[:, c, T:N], xT[:, c, T:N], sm[:, 11, 0:NS], ALU.add)

            def layer(l):
                modulate(l, 0, G1)
                dve.wait_ge(s_fe, l + 1)
                ch(ts(FB, FB, 1.0, None, ALU.add))
                ch(V.reciprocal(FB, FB))
                for h in range(H):
                    ins = ts(FB[:, h, :], FB[:, h, :], omlb[:, l, h:h + 1], lb[:, l, h:h + 1], ALU.mult, ALU.add)
                ch(ins)
                ch(ts(oT[:, :, 0:T], FB[:, :, 0:T], 2.0 ** -60, None, ALU.max))
                ts(bT[:, :, :], FB[:, :, 0:T], 2.0 ** -60, None, ALU.min).then_inc(s_f, 1)
                dve.wait_ge(s_tq, l + 1)
                ch(stt(QB, g2, 1.0, QB, ALU.add, ALU.mult))
                ch(ts(QB, QB, 0.5, None, ALU.mult))
                dve.wait_ge(s_lnf, l + 1)
                ch(stt(oT[:, :, 0:T], bT[:, :, :], LN64, oT[:, :, 0:T], ALU.subtract, ALU.add))
                dve.wait_ge(s_S1, l + 1)
                ch(ts(FB, FB, -1.0, 1.0, ALU.mult, ALU.add))
                for h in range(H):
                    ins = V.tensor_tensor_scan(bT[:, h, :], ones[:, 0:1].broadcast_to([P, T]), oT[:, h, 0:T],
                                               0.0, ALU.mult, ALU.add)
                ins.then_inc(s_b, 1)
                dve.wait_ge(s_u, U * l + 12)
                for c in range(AC):
                    for j in range(CW):
                        w = par[:, CWW + 16 * l + 4 * j + c:CWW + 16 * l + 4 * j + c + 1]
                        x = xaP[:, c, j:j + T]
                        if j == 0:
                            ch(ts(xc[:, c, 0:T], x, w, par[:, CB + 4 * l + c:CB + 4 * l + c + 1],
                                  ALU.mult, ALU.add))
                        else:
                            ch(stt(xc[:, c, 0:T], x, w, xc[:, c, 0:T], ALU.mult, ALU.add))
                cst = par[:, SCV + P * l:SCV + P * l + 96].rearrange("p (b j c) -> p j c b", j=CW - 1, c=AC)
                xs = xc[:, :, T:N]
                tmp = sm[:, 12:14, :].rearrange("p a b -> p (a b)").rearrange("p (c b) -> p c b", c=AC)
                for j in range(CW):
                    src = cst[:, j] if j < CW - 1 else XA[:, :, T:N]
                    w = wide(par[:, CWW + 16 * l + 4 * j:CWW + 16 * l + 4 * j + 4], NS)
                    ch(tt(tmp, src, w, ALU.mult))
                    other = wide(par[:, CB + 4 * l:CB + 4 * l + 4], NS) if j == 0 else xs
                    ins = tt(xs, tmp, other, ALU.add)
                    if j < CW - 1:
                        ch(ins)
                ins.then_inc(s_xc, 1)
                if l:
                    dve.wait_ge(s_or, l)
                oc = outc[:, :]
                V.tensor_copy(oc[:, 36:48].rearrange("p (j c) -> p c j", c=AC), xaP[:, :, T:T + 3])
                V.tensor_copy(oc[:, 48:80].rearrange("p (b c) -> p c b", c=AC), XA[:, :, T:N])
                dve.wait_ge(s_tg, 8 * (l + 1))
                ts(rg, rg, 0.5, 0.5, ALU.mult, ALU.add).then_inc(s_rdy, 1)
                ch(stt(ig, ig, 1.0, xc, ALU.add, ALU.mult))
                dve.wait_ge(s_u, U * l + 20)
                ch(tt(gt, GA, GA, ALU.mult))
                ch(ts(gt, gt, 0.044715, 1.0, ALU.mult, ALU.add))
                tt(gt, gt, GA, ALU.mult).then_inc(s_gi, 1)
                dve.wait_ge(s_a, l + 1)
                ch(ts(g2, mu, -1.0, 1.0, ALU.mult, ALU.add))
                ch(V.reciprocal(g2, g2))
                stt(mu, mu, -2.0, g2, ALU.mult, ALU.mult).then_inc(s_m2, 1)
                dve.wait_ge(s_mu, l + 1)
                ch(V.memset(ag[:, :, 0:1], 0.0))
                ch(V.memset(mu[:, :, 0:1], 1.0))
                ch(stt(ig, ig, 0.5, mu, ALU.mult, ALU.mult))
                for c in range(AC):
                    ins = V.tensor_tensor_scan(rg[:, c, 0:T], ag[:, c, 0:T], ig[:, c, 0:T], 0.0,
                                               ALU.mult, ALU.add)
                ch(ins)
                h0 = par[:, SH + 32 * l:SH + 32 * (l + 1)].rearrange("p (b c) -> p c b", c=AC)
                ch(tt(rg[:, :, T:N], ag[:, :, T:N], h0, ALU.mult))
                ch(tt(rg[:, :, T:N], rg[:, :, T:N], ig[:, :, T:N], ALU.add))
                V.tensor_copy(oc[:, 0:4], rg[:, :, T - 1])
                V.tensor_copy(oc[:, 4:36].rearrange("p (b c) -> p c b", c=AC), rg[:, :, T:N]).then_inc(s_oc, 1)
                dve.wait_ge(s_tge, l + 1)
                ch(stt(gt, gt, 1.0, GA, ALU.add, ALU.mult))
                ch(stt(gt, gt, 0.5, rg, ALU.mult, ALU.mult))
                tt(g2, gt, gt, ALU.mult).then_inc(s_zs, 1)
                dve.wait_ge(s_tgb, l + 1)
                ch(stt(GB, oT[:, :, :], 1.0, GB, ALU.add, ALU.mult))
                for h in range(H):
                    ts(GB[:, h, :], GB[:, h, :], 0.5, par[:, HG + 4 * l + h:HG + 4 * l + h + 1],
                       ALU.mult, ALU.mult)
                dve.wait_ge(s_rs, 3 * l + 2)
                for c in range(AC):
                    ins = stt(yT[:, c, :], gt[:, c, :],
                              par[:, OG + 4 * l + c:OG + 4 * l + c + 1], rs[:, :], ALU.mult, ALU.mult)
                ch(ins)

                def diff(v):
                    h2 = 1 << (v - 1)
                    b4 = bT[:, :, :].rearrange("p h (n two i) -> p (h n) two i", two=2, i=h2)
                    d4 = LD[v % 2].rearrange("p (n two i) -> p n two i", two=2, i=h2)
                    mid = b4[:, :, 0, h2 - 1:h2]
                    n = b4.shape[1]
                    midb = mid.broadcast_to([P, n, h2])
                    ch(tt(d4[:, :, 1, :], b4[:, :, 1, :], midb, ALU.subtract))
                    tt(d4[:, :, 0, :], midb, b4[:, :, 0, :], ALU.subtract).then_inc(s_ld, 1)

                def take(v):
                    dve.wait_ge(s_lp, (LEVELS + 1) * l + v + 1)
                    if l or v:
                        dve.wait_ge(s_lc, (LEVELS + 1) * l + v)
                    if v == LEVELS:
                        V.tensor_copy(ATx[:, :, :], ps[0][:, :].rearrange("p (h t) -> p h t", h=H))\
                            .then_inc(s_lc, 1)
                        return
                    for t in range(2):
                        ins = V.copy_predicated(AT[:, t], mask[:, v, :].unsqueeze(1).broadcast_to([P, H, P]),
                                                ps[2 * (v % 2) + t][:, :].rearrange("p (h t) -> p h t", h=H))
                    ins.then_inc(s_lc, 1)

                dve.sem_inc(s_lw, 1)
                diff(1)
                for v in range(1, LEVELS + 1):
                    if v < LEVELS:
                        dve.wait_ge(s_lw, (LEVELS + 1) * l + v)
                        diff(v + 1)
                    h2 = 1 << (v - 1)
                    dve.wait_ge(s_le, LEVELS * l + v)
                    d4, w4 = (x[v % 2].rearrange("p (h n two i) -> p h n two i", h=H, two=2, i=h2)
                              for x in (LD, LW))
                    for h in range(H):
                        qs = QB[:, h, 0:T].rearrange("p (n two i) -> p n two i", two=2, i=h2)
                        ks = FB[:, h, 0:T].rearrange("p (n two i) -> p n two i", two=2, i=h2)
                        tt(w4[:, h, :, 1, :], d4[:, h, :, 1, :], qs[:, :, 1, :], ALU.mult)
                        ins = tt(w4[:, h, :, 0, :], d4[:, h, :, 0, :], ks[:, :, 0, :], ALU.mult)
                    ins.then_inc(s_lw, 1)
                    take(v - 1)
                take(LEVELS)
                dve.wait_ge(s_kx, l + 1)
                tt(ke, ke, FB[:, :, 0:T], ALU.mult).then_inc(s_ke, 1)
                dve.wait_ge(s_S1, l + 1)
                for b in range(NS):
                    dve.wait_ge(s_vb, NS * l + b + 1)
                    if b:
                        dve.wait_ge(s_vbd, NS * l + b)
                    ch(tt(vbk, ps[2 + b % 2][:, :].rearrange("p (h e) -> p h e", h=H),
                          wide(FB[:, :, T + b], P), ALU.mult))
                    ins = tt(S[:, b * H:(b + 1) * H, :], S[:, b * H:(b + 1) * H, :], vbk, ALU.add)
                    ins.then_inc(s_vbd, 1)
                dve.wait_ge(s_ors, l + 1)
                ch(tt(yT[:, AC:, :], oT[:, :, :], ar[:, 0:W4].rearrange("p (h n) -> p h n", n=N), ALU.mult))
                tt(yT[:, AC:, :], yT[:, AC:, :], GB, ALU.mult).then_inc(s_y, 1)
                for c in range(KC):
                    if c % 2 == 0:
                        dve.wait_ge(s_wp, 4 * l + c // 2 + 1)
                    else:
                        dve.wait_ge(used, 48 + 50 * l + 12 + c // 2 + 1)
                    if c:
                        dve.wait_ge(s_x1, KC * l + c)
                    ins = residual(l, 0, c, ps[c % 4])
                    ins.then_inc(s_x1, 1)
                dve.wait_ge(s_x1, KC * (l + 1))
                dve.sem_inc(s_x, 1)
                modulate(l, 1, G2)

            layer(0)
            for c in range(FC):
                dve.wait_ge(s_fs, c + 1)
                tt(act[:, c, :], fsg[c % 2], ps[c % 3 * 2 + 1][:, 0:N], ALU.mult).then_inc(s_fa, 1)
            for c in range(KC):
                if c % 2 == 0:
                    dve.wait_ge(s_fd, c // 2 + 1)
                else:
                    dve.wait_ge(used, 48 + 16 + 22 + 3 * (c // 2 + 1))
                if c:
                    dve.wait_ge(s_fx, c)
                residual(0, 1, c, ps[c // 2 % 2 * 2 + c % 2]).then_inc(s_fx, 1)
            dve.wait_ge(s_fx, KC)
            dve.sem_inc(s_x, 1)
            layer(1)

            rws = (P, P, NS)
            LG, TOP, MSK, POS, OH0, OH1, BLK, EB, GS, T0, T1 = (rt[:, n] for n in (0, 1, 2, 3, 4, 5, 6, 7, 8, 9, 10))
            CNT, EXT, OFF, T2, FI = (rt[:, n, 0, :] for n in (11, 12, 13, 14, 15))
            dve.wait_ge(s_lg, 1)
            ch(V.memset(rt[:, :, :, :], 0.0))
            for t in range(3):
                ch(V.tensor_copy(LG[0:rws[t], t, :], ps[1][0:rws[t], t * NE:(t + 1) * NE]))
            for t in range(3):
                ch(V.max(TOP[:, t, :], LG[:, t, :]))
                ch(V.max_index(ridx[:, t, :], TOP[:, t, :], LG[:, t, :]))
            ch(V.tensor_copy(T0, ridx[:, :, :]))
            io8 = iota[:, 0:NE]
            for t in range(3):
                ch(ts(OH0[:, t, :], io8, T0[:, t, 0:1], None, ALU.is_equal))
                ch(ts(OH1[:, t, :], io8, T0[:, t, 1:2], None, ALU.is_equal))
            tt(MSK, OH0, OH1, ALU.add).then_inc(s_msk, 1)
            tt(rt[:, 19, :, 0], TOP[:, :, 1], TOP[:, :, 0], ALU.subtract).then_inc(s_red, 1)
            dve.wait_ge(s_re, 1)
            ch(ts(wts[:, :, 0], rt[:, 20, :, 0], 1.0, None, ALU.add))
            ch(V.reciprocal(wts[:, :, 0], wts[:, :, 0]))
            ch(tt(wts[:, :, 1], rt[:, 20, :, 0], wts[:, :, 0], ALU.mult))
            dve.wait_ge(s_rk, 1)
            for t in range(3):
                ch(V.tensor_copy(POS[0:rws[t], t, :], ps[0][0:rws[t], t * NE:(t + 1) * NE]))
            ch(V.tensor_copy(CNT, ps[0][:, 3 * NE:4 * NE]))
            ch(ts(T2, CNT, float(LOT), None, ALU.is_gt))
            ch(stt(EXT, CNT, float(2 * LOT), T2, ALU.is_gt, ALU.add))
            ch(V.tensor_tensor_scan(OFF, ones[:, 0:NE], EXT, 0.0, ALU.mult, ALU.add))
            ch(ts(tab[:, 0:1], OFF[:, NE - 1:NE], float(NE), None, ALU.add))
            ch(tt(OFF, OFF, EXT, ALU.subtract))
            ch(ts(OFF, OFF, float(NE), None, ALU.add))
            for i in range(MAXLOTS - NE):
                ch(tt(T2, OFF, EXT, ALU.add))
                ch(ts(T2, T2, float(NE + i), None, ALU.is_gt))
                ch(stt(FI, OFF, float(NE + i), T2, ALU.is_le, ALU.mult))
                ch(tt(FI, FI, io8, ALU.mult))
                ch(V.reduce_sum(sm[:, 15, i:i + 1], FI, AX.X))
            ch(V.tensor_copy(tab[:, 1:1 + MAXLOTS - NE], sm[:, 15, 0:MAXLOTS - NE]))
            ch(ts(BLK, POS, float(LOT), None, ALU.is_ge))
            ch(stt(T2, OFF, -1.0, io8, ALU.add, ALU.subtract))
            ch(tt(EB, BLK, T2.unsqueeze(1).broadcast_to([P, 3, NE]), ALU.mult))
            ch(tt(EB, EB, io8.unsqueeze(1).broadcast_to([P, 3, NE]), ALU.add))
            ch(stt(GS, EB, float(LOT), POS, ALU.mult, ALU.add))
            for n, oh in enumerate((OH0, OH1)):
                ch(tt(T1, GS, oh, ALU.mult))
                ch(V.reduce_sum(gsl[:, :, n], T1, AX.X))
            V.memset(acc[:, :, :], 0.0).then_inc(s_scd, 1)
            dve.wait_ge(s_scd, 1)
            V.memset(gatT, 0.0).then_inc(s_gT, 1)
            ch(V.memset(ps[4][:, :], 0.0))
            ch(V.memset(ps[5][:, :], 0.0))
            dve.sem_inc(s_tab, 1)
            dve.wait_ge(s_tab, 1)

            lots = dve.value_load(tab[0:1, 0:1], min_val=NE, max_val=MAXLOTS)

            def gathered(n, q):
                dve.wait_ge(s_hgH, n * 2 + q + 1)
                tt(hgL[:, 4 * q:4 * q + 4, :], ps[7][:, :].rearrange("p (c j) -> p c j", c=4),
                   hgH[:, 4 * q:4 * q + 4, :].bitcast(fp32), ALU.subtract).then_inc(s_hgL, 1)

            TILES = [(slice(0, ROWS[t]), t) for t in range(3)]

            def choice(step):
                for r, t in TILES:
                    S0, S1, W0 = sel[r, t, :], stmp[r, t, :], gat[r, t, :]
                    if step == 0:
                        ts(S0, iota[r, 0:LOT], gsl[r, t, 0:1], None, ALU.is_equal)
                        ins = ts(S1, iota[r, 0:LOT], gsl[r, t, 1:2], None, ALU.is_equal)
                    elif step == 1:
                        ins = ts(W0, S0, wts[r, t, 0:1], None, ALU.mult)
                    elif step == 2:
                        stt(W0, S1, wts[r, t, 1:2], W0, ALU.mult, ALU.add)
                        ins = tt(S0, S0, S1, ALU.add)
                if step == 2:
                    ins = ts(gsl[:, :, :], gsl[:, :, :], float(-LOT), None, ALU.add)
                return ins

            ch(choice(0))
            ch(choice(1))
            choice(2).then_inc(s_sel, 1)
            gathered(0, 0)
            gathered(0, 1)
            with dve.Fori(0, lots) as i:
                slot = slots(dve, i)
                for t in range(LS):
                    w = slot(t)
                    dve.wait_ge(s_hi, i * LS + t + 1)
                    tt(wL[t % 3][:, :], w, wH[t % 3][:, :].bitcast(fp32), ALU.subtract).then_inc(s_lo, 1)
                    if t in FORM_AT:
                        g = FORM_AT[t]
                        dve.wait_ge(s_mus, i * G + g + 1)
                        dve.wait_ge(used, i * LS + SLABS + LOT_ORDER.index((1, g)) + 1)
                        if g >= 2:
                            dve.wait_ge(s_aT, i * G + g - 1)
                        tt(ac[g % 2], sg[g % 2], ps[2 + g % 2][:, 0:256].rearrange("p (m j) -> p m j", m=2),
                           ALU.mult).then_inc(s_mua, 1)
                    if t == LS - 1:
                        gathered(i + 1, 0)
                    if t in DOWN_AT:
                        g = DOWN_AT[t]
                        dve.wait_ge(s_aH, i * G + g + 1)
                        tt(aL[g % 2][:, :], ps[6][:, 0:256], aH[g % 2][:, :].bitcast(fp32),
                           ALU.subtract).then_inc(s_aL, 1)
                    if t in ADD_AT:
                        c = ADD_AT[t]
                        dve.wait_ge(s_sc, i * KC + c + 1)
                        tt(acc[:, c, :], acc[:, c, :], ps[7][:, 0:N], ALU.add).then_inc(s_scd, 1)
                    if t == GATES_AT + 3:
                        dve.wait_ge(s_gTp, i + 1)
                        V.tensor_copy(gatT, ps[7][:, 0:N]).then_inc(s_gT, 1)
                    if t in CHOOSE_AT:
                        step = CHOOSE_AT[t]
                        dve.wait_ge(c_lot, i * 2 + step) if step else dve.wait_ge(s_sel, i + 1)
                        choice(step).then_inc(c_lot if step < 2 else s_sel, 1)
                gathered(i + 1, 1)
            for c in range(KC):
                dve.wait_ge(s_sc, lots * KC + c + 1)
                tt(acc[:, c, :], acc[:, c, :], ps[6 + c % 2][:, 0:N], ALU.add).then_inc(s_scd, 1)
            dve.wait_ge(s_scd, lots * KC + KC + 1)
            for c in range(KC):
                residual_ins = residual(1, 1, c, acc[:, c, :])
                ch(residual_ins)
            dve.sem_inc(s_x, 1)
            dve.wait_ge(s_rs, 3 * L + 1)
            for c in range(KC):
                ins = stt(hT[:, c, :], xT[:, c, :], par[:, FG + c:FG + c + 1], rs[:, :], ALU.mult, ALU.mult)
            ins.then_inc(s_fin, 1)


ORDER = (3, 2, 0, 4, 1, 5)
ORDER_SLABS = tuple(2 * g + h for g in ORDER for h in range(2))
DOWN = ((0, 8), (8, 16), (16, 22))
PARAM_LOADS = 4 + 7 + 4 + 2
LN64 = 6 * 0.6931471805599453
def _loads():
    n = [0] * R
    for pos in range(48 + 16 + 34 + 16):
        n[pos % R] += 1
    return n


LOADS = _loads()
ROWS = (P, P, NS)
LOT_ORDER = tuple(x for g in range(G) for x in ([(0, g), (1, g)] + ([(2, g - 1)] if g else []))) + ((2, G - 1),)

SLABS = 48 + 16 + 34 + 16
FORM_AT = {LOT_ORDER.index((0, g + 1)) if g < G - 1 else 3 * G - 1: g for g in range(G)}
TURN_AT = {LOT_ORDER.index((0, g + 1)) if g < G - 1 else 3 * G - 2: g for g in range(G)}
SCATTER_AT = {4 + 2 * c: c for c in range(KC)}
ADD_AT = {t + 3: c for t, c in SCATTER_AT.items()}
CHOOSE_AT = {25 + k: k for k in range(3)}
GATES_AT = 22
DOWN_AT = {LOT_ORDER.index((2, g)): g for g in range(G)}

_INS = ["x_prompt", "x_sample", "c_prompt", "c_sample", "state_rglru_h", "state_rglru_conv", "state_hgrn",
        "mod_w", "mod_b", "norm1_g", "norm2_g", "w_in", "conv_w", "conv_b", "rg_wa", "rg_ba", "rg_wx", "rg_bx",
        "rg_lambda", "rg_out_g", "hg_lb_logits", "hg_norm_g", "w_out", "ffn_w1", "ffn_w3", "ffn_w2",
        "router_w", "moe_w1", "moe_w3", "moe_w2", "final_g"]
_OUTS = [("y_prompt", (1, T, D)), ("y_sample", (NS, 1, D)), ("new_h_prompt", (L, 1, WA)),
         ("new_conv_prompt", (L, 1, CW - 1, WA)), ("new_S_prompt", (L, 1, H, P, P)),
         ("new_h_sample", (L, NS, WA)), ("new_conv_sample", (L, NS, CW - 1, WA)),
         ("new_S_sample", (L, NS, H, P, P))]


def kernel(**inputs):
    import numpy as np
    import concourse.bacc as bacc
    from concourse.bass_utils import run_bass_kernel_spmd as run

    nc = bacc.Bacc("TRN2", target_bir_lowering=False, num_devices=1)
    arrays, ins, outs = {}, {}, {}
    for name in _INS:
        x = np.ascontiguousarray(inputs[name])
        arrays[f"in_{name}"] = x
        ins[name] = nc.dram_tensor(f"in_{name}", x.shape, mybir.dt.from_np(x.dtype), kind="ExternalInput").ap()
    for name, shape in _OUTS:
        outs[name] = nc.dram_tensor(f"out_{name}", shape, mybir.dt.float32, kind="ExternalOutput").ap()
    trunk(nc, ins, outs)
    r = run(nc, [arrays], core_ids=[0])
    return tuple(r.results[0][f"out_{name}"] for name, _ in _OUTS)
```

```python
import concourse.bass as bass
from concourse import mybir
from contextlib import ExitStack

D = 1024
T = 256
NS = 8
N = T + NS
P = 128
KC = D // P
L = 2
WA = 512
AC = WA // P
H = 4
U = 3072 // P
F = 2816
FC = F // P
NE = 8
CW = 4
EPS = 1e-6
COND = 1 + NS
LOT = 128
MAXLOTS = NE + 2 * N // (LOT + 1)
G = F // 256
R = 9
SLAB = 2048
LEVELS = 8


def trunk(nc, a, o):
    fp32 = mybir.dt.float32
    i32 = mybir.dt.int32
    u32 = mybir.dt.uint32
    ALU = mybir.AluOpType
    ACT = mybir.ActivationFunctionType
    AX = mybir.AxisListType

    ctx = ExitStack()
    with ctx:
        def sb(name, shape, dt=fp32):
            return ctx.enter_context(nc.sbuf_tensor(name, shape, dt))

        def sem(name):
            return ctx.enter_context(nc.semaphore(name))

        ring = sb("ring", [P, R, SLAB])
        xT = sb("xT", [P, KC, N])
        h_at = nc.sbuf_base
        hT = sb("hT", [P, KC, N])
        par = sb("par", [P, 5 * P])
        modT = sb("modT", [P, L, 6 * KC, COND])
        u_at = nc.sbuf_base
        uT = sb("uT", [P, U * N])
        mixed = nc.sbuf_base
        AT = sb("AT", [P, 2, H, P])
        ATx = sb("ATx", [P, H, P])
        vtok = sb("vtok", [P, 2, H, P])
        S = sb("S", [P, NS * H, P])
        oT = sb("oT", [P, H, N])
        bT = sb("bT", [P, H, T])
        yT = sb("yT", [P, KC, N])
        kept = nc.sbuf_base
        xaP = sb("xaP", [P, AC, CW - 1 + T])
        gw = sb("gw", [P, 2, AC, P])
        mixed_end = nc.sbuf_base
        short = nc.sbuf_base
        ar = sb("ar", [P, 7 * H * N])
        mask = sb("mask", [P, LEVELS, P], mybir.dt.uint8)
        ident = sb("ident", [P, P])
        ones = sb("ones", [P, P])
        mean = {w: sb(f"mean{w}", [P, P]) for w in (D, WA, P)}
        before = sb("before", [P, P])
        rtr = sb("rtr", [P, KC, NE])
        rs = sb("rs", [P, N])
        modA = sb("modA", [P, KC, COND])
        cond = sb("cond", [P, KC, COND])
        lb = sb("lb", [P, L, H])
        omlb = sb("omlb", [P, L, H])
        coef = sb("coef", [P, L, AC])
        sm = sb("sm", [P, 16, 16])
        iota = sb("iota", [P, P])
        outc = sb("outc", [P, 80])
        outr = [sb(f"outr{l}", [80, P]) for l in range(L)]
        eps = sb("eps", [P, 1])
        ridx = sb("ridx", [P, 3, NE], u32)
        gsl = sb("gsl", [P, 3, 2])
        wts = sb("wts", [P, 3, 2])
        tab = sb("tab", [P, 8], i32)
        f32r = mybir.dt.float32r

        def split_at(name, n, offset, words):
            return [[nc.alloc_sbuf_tensor_at(f"{name}_{part}{i}", [P, words], f32r,
                                             offset=offset + 4 * words * (2 * i + x))
                     for i in range(n)] for x, part in enumerate(("hi", "lo"))]

        assert 6 * 4 * SLAB <= mixed_end - mixed
        wH, wL = split_at("slab", 3, mixed, SLAB)
        (hH,), (hL,) = split_at("tokens", 1, short + 4 * 4608, 1024)
        aH, aL = split_at("act", 2, short, 256)
        assert 4 * (4 * SLAB + KC * N) <= kept - mixed
        fhH, fhL, faH, faL = (nc.alloc_sbuf_tensor_at(name, [P, n, N], f32r, offset=at_) for name, n, at_ in (
            ("h_hi", KC, mixed + 16 * SLAB), ("h_lo", KC, h_at), ("ffn_act_hi", FC, u_at),
            ("ffn_act_lo", FC, short)))
        ps = [ctx.enter_context(nc.psum_tensor(f"ps{i}", [P, 512], fp32)) for i in range(8)]

        u = uT[:, :].rearrange("p (c n) -> p c n", n=N)
        XA, GA, QB, FB, IB, GB = (u[:, 4 * i:4 * i + 4, :] for i in range(6))
        prow = uT[:, 0:5 * P].rearrange("p (t c) -> p t c", c=P)
        xrow = uT[:, 1024:1024 + 3 * D].rearrange("p (t c) -> p t c", c=D)
        modrow = hT[0:COND, :, :].rearrange("p c n -> p (c n)")[:, 0:512].rearrange("p (i n) -> p i n", i=2)
        yrow = xrow
        h2tok = uT[:, 0:3 * D].rearrange("p (t c) -> p t c", c=D)
        acc = uT[:, 3 * D:3 * D + KC * N].rearrange("p (c n) -> p c n", n=N)
        rt = uT[:, 5184:5184 + 24 * 3 * NE].rearrange("p (n t e) -> p n t e", t=3, e=NE)
        W4 = H * N

        def lot(i):
            return ar[:, i * W4:(i + 1) * W4].rearrange("p (h n) -> p h n", n=N)

        xc, rg, ig, ag, mu, gt, g2 = (lot(i) for i in range(7))
        LD = [ar[:, 1024 * i:1024 * (i + 1)] for i in range(2)]
        LW = [ar[:, 2048 + 1024 * i:3072 + 1024 * i] for i in range(2)]
        keT = ar[:, 4096:5120].rearrange("p (t h d) -> p t h d", t=2, h=H)
        ke = ar[:, 5120:6144].rearrange("p (h t) -> p h t", h=H)
        vbk = ar[:, 6144:6656].rearrange("p (g e) -> p g e", e=P)
        hgH, hgL = (x[:, :].rearrange("p (c j) -> p c j", j=LOT) for x in (hH, hL))
        ytok = ar[:, 1024:2048]
        sg = [ar[:, 2048 + 256 * i:2304 + 256 * i].rearrange("p (m j) -> p m j", m=2) for i in range(2)]
        ac = [ar[:, 2560 + 256 * i:2816 + 256 * i].rearrange("p (m j) -> p m j", m=2) for i in range(2)]
        sel = ar[:, 3072:3456].rearrange("p (t j) -> p t j", j=LOT)
        gat = ar[:, 3456:3840].rearrange("p (t j) -> p t j", j=LOT)
        gatT = ar[:, 3840:3840 + N]
        stmp = ar[:, 4224:4608].rearrange("p (t j) -> p t j", j=LOT)
        fsg, fac = ([ar[:, (FC + i + k) * N:(FC + i + k + 1) * N] for i in range(2)] for k in (0, 2))
        sfin = ar[:, 5120:5632]

        MODB, G1, G2 = 0, 96, 112
        CWW, CB, BA, BX, LAM, OG, LBL, HG, FG, CP = 128, 160, 168, 176, 184, 192, 200, 208, 216, 224
        CS, SH, SCV = 256, 320, 384

        class Stream:
            def __init__(self):
                self.pos = self.n = 0
                self.loads = [0] * R
                self.user = [None] * R

            def take(self):
                s = self.pos % R
                before_, self.user[s] = self.user[s], self.n
                self.pos += 1
                self.n += 1
                self.loads[s] += 1
                return s, self.loads[s], before_

            def align(self):
                self.pos += -self.pos % R

        IT = 4 * R
        LS = 3 * G

        def mod_rows(n):
            return ps[0 if n < MOD_DONE[0] and n % 2 else 7][0:COND, 0:256]

        def mod_columns(n, count=1):
            o_ = 2 * COND * (n - max(x for x in (0,) + MOD_DONE if x <= n))
            return ps[6][:, o_:o_ + 2 * COND * count].rearrange("p (c b) -> p c b", b=COND)

        full = [sem(f"slot_full{i}") for i in range(R)]
        used = sem("slab_used")
        s_row = sem("param_rows_loaded")
        s_xrow = sem("x_rows_loaded")
        s_gw = sem("gate_weights_loaded")
        s_gwz = sem("gate_weights_cleared")
        s_S = sem("sample_state_loaded")
        s_cst = sem("constants_ready")
        s_parT = sem("param_transposed")
        s_par = sem("param_ready")
        s_xTp = sem("x_transposed")
        s_xT = sem("x_ready")
        s_act0 = sem("setup_act")
        s_dve0 = sem("setup_dve")
        s_cond = sem("cond_ready")
        s_mev = sem("mod_rows")
        s_mtr = sem("mod_transposed")
        s_mod = sem("mod_ready")
        s_sq = sem("squares_ready")
        s_ms = sem("mean_square_ready")
        s_rs = sem("rsqrt_ready")
        s_h = sem("h_ready")
        s_up = sem("u_psum")
        s_u = sem("u_evacuated")
        s_fe = sem("f_exp")
        s_f = sem("f_ready")
        s_lnf = sem("ln_f")
        s_tq = sem("tanh_q")
        s_xc = sem("conv_ready")
        s_gp = sem("gate_psum")
        s_tg = sem("gate_tanh")
        s_rdy = sem("r_ready")
        s_a = sem("a_ready")
        s_m2 = sem("mult_squared")
        s_mu = sem("mult_ready")
        s_gi = sem("gelu_inner")
        s_tge = sem("gelu_tanh")
        s_tgb = sem("tanh_gb")
        s_z = sem("z_ready")
        s_zs = sem("z_squared")
        s_b = sem("b_ready")
        s_ld = sem("level_diff")
        s_le = sem("level_exp")
        s_lw = sem("level_operand")
        s_lp = sem("level_psum")
        s_lc = sem("level_copied")
        s_vp = sem("v_transposed")
        s_v = sem("vtok_ready")
        s_kx = sem("ke_exp")
        s_ke = sem("ke_ready")
        s_kp = sem("ke_transposed")
        s_keT = sem("keT_ready")
        s_sf = sem("final_state_psum")
        s_sfs = sem("final_state_ready")
        s_op = sem("o_psum")
        s_o = sem("o_evacuated")
        s_vb = sem("v_broadcast")
        s_vbd = sem("v_broadcast_used")
        s_S1 = sem("decayed_state")
        s_osp = sem("o_sample_psum")
        s_os = sem("o_squared")
        s_oms = sem("o_mean_square")
        s_ors = sem("o_rsqrt")
        s_y = sem("y_ready")
        s_wp = sem("w_out_psum")
        s_x1 = sem("residual_chunk")
        s_x = sem("x_updated")
        s_oc = sem("vector_outputs")
        s_ocp = sem("vector_outputs_transposed")
        s_or = sem("vector_output_rows")
        s_fhH = sem("h_hi")
        s_fhL = sem("h_lo")
        s_fwH = sem("ffn_slab_hi")
        s_fwL = sem("ffn_slab_lo")
        s_fs = sem("ffn_silu")
        s_fa = sem("ffn_act")
        s_faH = sem("ffn_act_hi")
        s_faL = sem("ffn_act_lo")
        s_fx = sem("ffn_down_used")
        s_lg = sem("logits_psum")
        s_lgc = sem("logits_used")
        s_htp = sem("h2_transposed")
        s_htk = sem("h2tok_ready")
        s_red = sem("router_exp_in")
        s_re = sem("router_exp")
        s_msk = sem("choice_mask")
        s_rk = sem("ranks_psum")
        s_tab = sem("lot_table")
        s_sel = sem("lot_choice")
        s_gth = sem("gather_psum")
        s_hgH = sem("gathered_hi")
        s_hgL = sem("gathered_lo")
        s_hi = sem("slab_hi")
        s_lo = sem("slab_lo")
        s_aT = sem("moe_act_transposed")
        s_aH = sem("moe_act_hi")
        s_aL = sem("moe_act_lo")
        s_gTp = sem("gate_transposed")
        s_gT = sem("gateT_ready")
        s_mus = sem("moe_silu")
        s_mua = sem("moe_act")
        s_yt = sem("moe_y_ready")
        s_sc = sem("scatter_psum")
        s_scd = sem("scatter_added")
        s_rtr = sem("router_loaded")
        s_moe = sem("moe_done")
        s_fin = sem("final_x")
        s_ft = sem("final_transposed")
        s_fr = sem("final_rows")
        s_out = sem("outputs_stored")
        s_st = sem("states_stored")
        c_dve = sem("dve_chain")
        c_lot = sem("choice_step")
        c_act = sem("act_chain")
        c_pool = sem("pool_chain")
        outs = [0]

        class Chain:
            def __init__(self, eng, s, base=0):
                self.eng, self.s, self.n, self.base = eng, s, 0, base

            def __call__(self, ins):
                self.n += 1
                ins.then_inc(self.s, 1)
                self.eng.wait_ge(self.s, self.base + self.n)

        def wide(x, n):
            return x.unsqueeze(len(x.shape)).broadcast_to(list(x.shape) + [n])

        def slots(eng, i):
            def at(t):
                s = t % R
                per = len(range(s, LS, R))
                eng.wait_ge(full[s], i * (16 * per) + 16 * (LOADS[s] + t // R + 1))
                return ring[:, s, :]
            return at

        block = ctx.enter_context(nc.Block())

        @block.sync
        def _(sp):
            st = Stream()

            def load(src, base_used=None):
                s, _, prev = st.take()
                if prev is not None:
                    sp.wait_ge(used, prev + 1)
                w = src.shape[1] * src.shape[2]
                dst = ring[:, s, 0:w].rearrange("p (k n) -> p k n", k=src.shape[1])
                sp.dma_start(dst, src).then_inc(full[s], 16)

            def projections(n0, n1):
                for n in range(n0, n1):
                    l, g = divmod(n, MG)
                    load(a["mod_w"][l].rearrange("(k p) n -> p k n", p=P)[:, :, g * 256:(g + 1) * 256])

            projections(0, MOD_DONE[0])
            for l in range(L):
                for g in ORDER_SLABS:
                    load(a["w_in"][l].rearrange("(k p) n -> p k n", p=P)[:, :, g * 256:(g + 1) * 256])
                projections(MOD_DONE[l], MOD_DONE[l + 1])
                for g in range(4):
                    load(a["w_out"][l].rearrange("(k p) n -> p k n", p=P)[:, :, g * 256:(g + 1) * 256])
                if l == 0:
                    for g in range(G):
                        for w in ("ffn_w1", "ffn_w3"):
                            load(a[w][0].rearrange("(k p) n -> p k n", p=P)[:, :, g * 256:(g + 1) * 256])
                    for q in range(4):
                        for k0, k1 in DOWN:
                            load(a["ffn_w2"][0].rearrange("(k p) n -> p k n", p=P)
                                 [:, k0:k1, q * 256:(q + 1) * 256])
            st.align()
            held = dict(enumerate(st.user))
            w1 = a["moe_w1"][0].rearrange("e (k p) n -> p e k n", p=P)
            w3 = a["moe_w3"][0].rearrange("e (k p) n -> p e k n", p=P)
            w2 = a["moe_w2"][0].rearrange("e (k p) n -> p e k n", p=P)

            def lot_slabs(e, i, first_lot):
                last = [None] * R
                for t in range(LS):
                    last[t % R] = t
                cur = list(last)
                new = [False] * R
                for t, (kind, g) in enumerate(LOT_ORDER):
                    s = t % R
                    if new[s]:
                        sp.wait_ge(s_lo, i * LS + cur[s] + 1)
                    elif first_lot:
                        sp.wait_ge(used, held[s] + 1)
                    else:
                        sp.wait_ge(s_lo, i * LS - LS + cur[s] + 1)
                    cur[s], new[s] = t, True
                    if kind == 2:
                        src = w2[:, bass.ds(e, 1), 2 * g:2 * g + 2, :].rearrange("p e k n -> p (e k) n")
                        dst = ring[:, s, :].rearrange("p (k n) -> p k n", k=2)
                    else:
                        src = (w1, w3)[kind][:, bass.ds(e, 1), :, g * 256:(g + 1) * 256]\
                            .rearrange("p e k n -> p (e k) n")
                        dst = ring[:, s, :].rearrange("p (k n) -> p k n", k=KC)
                    sp.dma_start(dst, src).then_inc(full[s], 16)

            lot_slabs(0, 0, True)
            with sp.Fori(1, NE) as i:
                lot_slabs(i, i, False)
            sp.wait_ge(s_tab, 1)
            lots = sp.value_load(tab[0:1, 0:1], min_val=NE, max_val=MAXLOTS)
            with sp.If(lots > NE):
                with sp.Fori(NE, lots) as i:
                    e = sp.value_load(tab[0:1, bass.ds(i - (NE - 1), 1)], min_val=0, max_val=NE - 1)
                    lot_slabs(e, i, False)

        @block.gpsimd
        def _(pool):
            ch = Chain(pool, c_pool)
            g = nc.gpsimd
            g.memset(gw[:], 0.0).then_inc(s_gwz, 1)
            ch(g.memset(ident[:], 0.0))
            ch(g.affine_select(out=ident[:], in_=ident[:], compare_op=ALU.not_equal, fill=1.0, base=0,
                               pattern=[[-1, P]], channel_multiplier=1))
            ch(g.memset(before[:], 1.0))
            ch(g.affine_select(out=before[:], in_=before[:], compare_op=ALU.is_gt, fill=0.0, base=0,
                               pattern=[[1, P]], channel_multiplier=-1))
            ch(g.memset(ones[:], 1.0))
            for w in (D, WA, P):
                ch(g.memset(mean[w][:], 1.0 / w))
            ch(g.memset(eps[:], EPS))
            ch(g.iota(iota[:], pattern=[[1, P]], base=0, channel_multiplier=0,
                      allow_small_or_imprecise_dtypes=True))
            ch(g.iota(ar[:, 0:P].bitcast(i32), pattern=[[1, P]], base=0, channel_multiplier=0))
            ch(g.iota(ar[:, P:2 * P].bitcast(i32), pattern=[[0, P]], base=0, channel_multiplier=1))
            g.memset(xaP[:, :, 0:CW - 1], 0.0).then_inc(s_cst, 1)

            for l in range(L):
                pool.wait_ge(s_S, 16 * (l + 1))
                pool.wait_ge(s_f, l + 1)
                fb = FB[:, :, T:N].rearrange("p h b -> p b h")
                for b in range(NS):
                    ins = g.tensor_tensor(out=S[:, b * H:(b + 1) * H, :], in0=S[:, b * H:(b + 1) * H, :],
                                          in1=wide(fb[:, b, :], P), op=ALU.mult)
                ins.then_inc(s_S1, 1)

        @block.tensor
        def _(pe):
            st = Stream()
            mm = nc.tensor.matmul

            def slab():
                s, n, _ = st.take()
                pe.wait_ge(full[s], 16 * n)
                return ring[:, s, :]

            pe.wait_ge(s_cst, 1)
            pe.wait_ge(s_row, 16 * PARAM_LOADS)
            for t, rows in enumerate((P, 104, P, 96, 96)):
                last = nc.tensor.transpose(ps[t // 4][:, t % 4 * P:t % 4 * P + rows], prow[0:rows, t, :],
                                           ident[0:rows, 0:rows])
            last.then_inc(s_parT, 1)
            pe.wait_ge(s_xrow, 16 * 2)
            for c in range(KC):
                b = ps[2 + c % 4]
                if c >= 4:
                    pe.wait_ge(s_xT, c - 3)
                for t in range(2):
                    nc.tensor.transpose(b[:, t * P:(t + 1) * P], xrow[:, t, c * P:(c + 1) * P], ident[:])
                nc.tensor.transpose(b[:, T:N], xrow[0:NS, 2, c * P:(c + 1) * P], ident[0:NS, 0:NS])\
                    .then_inc(s_xTp, 1)

            pe.wait_ge(s_cond, 1)
            mods = [0, 0]

            def turn_rows():
                n = mods[1]
                pe.wait_ge(s_mev, n + 1)
                if n in MOD_DONE:
                    pe.wait_ge(s_mod, MOD_DONE.index(n) + 1)
                for c in range(2):
                    last = nc.tensor.transpose(mod_columns(n)[:, c, :], modrow[:, n % 2, c * P:(c + 1) * P],
                                               ident[0:COND, 0:COND])
                last.then_inc(s_mtr, 1)
                mods[1] += 1

            def project(count):
                for _ in range(count):
                    n = mods[0]
                    w = slab()[:, 0:2048].rearrange("p (k n) -> p k n", k=KC)
                    ahead = 2 if n < MOD_DONE[0] else 1
                    if n >= ahead:
                        pe.wait_ge(s_mev, n + 1 - ahead)
                    for k in range(KC):
                        last = mm(mod_rows(n), cond[:, k, :], w[:, k, :], start=(k == 0), stop=(k == KC - 1))
                    last.then_inc(used, 1)
                    mods[0] += 1
                    if mods[1] < n:
                        turn_rows()

            project(MOD_DONE[0])
            turn_rows()

            def mean_square(n, l):
                pe.wait_ge(s_sq, n)
                for k in range(KC):
                    last = mm(ps[0][:, 0:N], mean[D][:], yT[:, k, :], start=(k == 0), stop=(k == KC - 1))
                last.then_inc(s_ms, 1)

            def layer(l):
                mean_square(2 * l + 1, l)
                pe.wait_ge(s_h, 2 * l + 1)
                j = 0
                for grp in ORDER:
                    for half in range(2):
                        w = slab()[:, 0:2048].rearrange("p (k n) -> p k n", k=KC)
                        for m in range(2):
                            if j >= 4:
                                pe.wait_ge(s_u, U * l + j - 3)
                            for k in range(KC):
                                last = mm(ps[j % 4][:, 0:N], w[:, k, m * P:(m + 1) * P], hT[:, k, :],
                                          start=(k == 0), stop=(k == KC - 1))
                            if m == 0:
                                last.then_inc(s_up, 1)
                            j += 1
                        last.then_inc(used, 1)
                    if grp == 4:
                        pe.wait_ge(s_u, U * l + j)
                        for t in range(2):
                            for h in range(H):
                                last = nc.tensor.transpose(ps[4 + t][:, h * P:(h + 1) * P],
                                                           IB[:, h, t * P:(t + 1) * P], ident[:])
                        last.then_inc(s_vp, 1)
                        pe.wait_ge(s_v, l + 1)
                        pe.wait_ge(s_xc, l + 1)
                        pe.wait_ge(s_gw, 64 * (l + 1))
                        for c in range(AC):
                            for w in range(2):
                                b = 4 + w
                                if c:
                                    pe.wait_ge(s_tg, 8 * l + 2 * c + w - 1)
                                mm(ps[b][:, 0:N], gw[:, w, c, :], xc[:, c, :], start=True, stop=True)\
                                    .then_inc(s_gp, 1)
                pe.wait_ge(s_u, U * (l + 1))
                project(FILL[l][0])
                pe.wait_ge(s_zs, l + 1)
                for c in range(AC):
                    last = mm(ps[4][:, 0:N], mean[WA][:], g2[:, c, :], start=(c == 0), stop=(c == AC - 1))
                last.then_inc(s_ms, 1)
                for v in range(LEVELS + 1):
                    pe.wait_ge(s_lw, (LEVELS + 1) * l + v + 1)
                    if v >= 2:
                        pe.wait_ge(s_lc, (LEVELS + 1) * l + v - 1)
                    lw = LW[v % 2].rearrange("p (h t) -> p h t", h=H)
                    if v == LEVELS:
                        for h in range(H):
                            last = mm(ps[2 * (v % 2)][:, h * P:(h + 1) * P], lw[:, h, 0:P], lw[:, h, P:T],
                                      start=True, stop=True)
                    else:
                        for t in range(2):
                            for h in range(H):
                                kk = lw[:, h, t * P:(t + 1) * P] if v else FB[:, h, t * P:(t + 1) * P]
                                qq = lw[:, h, t * P:(t + 1) * P] if v else QB[:, h, t * P:(t + 1) * P]
                                last = mm(ps[2 * (v % 2) + t][:, h * P:(h + 1) * P], kk, qq,
                                          start=True, stop=True)
                    last.then_inc(s_lp, 1)
                    project(FILL[l][1][v])
                pe.wait_ge(s_ke, l + 1)
                pe.wait_ge(s_rs, 3 * l + 2)
                for t in range(2):
                    for h in range(H):
                        last = nc.tensor.transpose(ps[4 + t][:, h * P:(h + 1) * P], ke[:, h, t * P:(t + 1) * P],
                                                   ident[:])
                last.then_inc(s_kp, 1)
                pe.wait_ge(s_lc, (LEVELS + 1) * (l + 1))
                for h in range(H):
                    b = ps[h // 2]
                    w = h % 2 * T
                    mm(b[:, w:w + P], vtok[:, 0, h, :], AT[:, 0, h, :], start=True, stop=True)
                    mm(b[:, w + P:w + T], vtok[:, 0, h, :], ATx[:, h, :], start=True, stop=False)
                    last = mm(b[:, w + P:w + T], vtok[:, 1, h, :], AT[:, 1, h, :], start=False, stop=True)
                last.then_inc(s_op, 1)
                pe.wait_ge(s_keT, l + 1)
                for h in range(H):
                    for t in range(2):
                        last = mm(ps[5][:, h * P:(h + 1) * P], keT[:, t, h, :], vtok[:, t, h, :],
                                  start=(t == 0), stop=(t == 1))
                last.then_inc(s_sf, 1)
                for b in range(NS):
                    if b >= 2:
                        pe.wait_ge(s_vbd, NS * l + b - 1)
                    for h in range(H):
                        last = mm(ps[2 + b % 2][:, h * P:(h + 1) * P],
                                  IB[:, h, T + b:T + b + 1].broadcast_to([P, P]), ident[:],
                                  start=True, stop=True)
                    last.then_inc(s_vb, 1)
                    project(FILL[l][2][b])
                pe.wait_ge(s_vbd, NS * (l + 1))
                pe.wait_ge(s_keT, l + 1)
                for b in range(NS):
                    for h in range(H):
                        c = h * NS + b
                        last = mm(ps[4][:, c:c + 1], S[:, b * H + h, :], QB[:, h, T + b:T + b + 1],
                                  start=True, stop=True)
                last.then_inc(s_osp, 1)
                project(FILL[l][3])
                pe.wait_ge(s_os, l + 1)
                for h in range(H):
                    last = mm(ps[h][:, 0:N], mean[P][:], yT[:, AC + h, :], start=True, stop=True)
                last.then_inc(s_oms, 1)
                project(FILL[l][4])
                turn_rows()
                assert mods[1] == MOD_DONE[l + 1]
                pe.wait_ge(s_y, l + 1)
                for g in range(4):
                    w = slab()[:, 0:2048].rearrange("p (k n) -> p k n", k=KC)
                    for m in range(2):
                        c = 2 * g + m
                        if c >= 4:
                            pe.wait_ge(s_x1, KC * l + c - 3)
                        for k in range(KC):
                            last = mm(ps[c % 4][:, 0:N], w[:, k, m * P:(m + 1) * P], yT[:, k, :],
                                      start=(k == 0), stop=(k == KC - 1))
                        if m == 0:
                            last.then_inc(s_wp, 1)
                    last.then_inc(used, 1)
                pe.wait_ge(s_oc, l + 1)
                nc.tensor.transpose(ps[4][0:80, 0:P], outc[:, :], ident[:]).then_inc(s_ocp, 1)
                mean_square(2 * l + 2, l)
                pe.wait_ge(s_h, 2 * l + 2)

            def products(out, x, xl, w, wl, start, stop):
                mm(out, x, w, start=start, stop=False)
                mm(out, x, wl, start=False, stop=False)
                return mm(out, xl, w, start=False, stop=stop)

            def dense():
                pe.wait_ge(s_fhL, 2)
                for d in range(FS):
                    slab()
                    pe.wait_ge(s_fwL, d + 1)
                    if d < 2 * G:
                        g, x = divmod(d, 2)
                        if x == 0 and g >= 2:
                            pe.wait_ge(s_fa, 2 * g - 2)
                        w, wl = (y[d % 2][:, :].rearrange("p (k n) -> p k n", k=KC) for y in (wH, wL))
                        for m in range(2):
                            ms = slice(m * P, (m + 1) * P)
                            for k in range(KC):
                                last = products(ps[g % 2 * 4 + x * 2 + m][:, 0:N], w[:, k, ms], wl[:, k, ms],
                                                fhH[:, k, :], fhL[:, k, :], k == 0, k == KC - 1)
                    else:
                        q, i = divmod(d - 2 * G, 3)
                        k0, k1 = DOWN[i]
                        if i == 0:
                            if q < 2:
                                pe.wait_ge(s_fa, FC - 2 + 2 * q)
                            else:
                                pe.wait_ge(s_fx, 2 * q - 2)
                        pe.wait_ge(s_faL, k1)
                        w, wl = (y[d % 2][:, 0:(k1 - k0) * 256].rearrange("p (k n) -> p k n", k=k1 - k0)
                                 for y in (wH, wL))
                        for m in range(2):
                            ms = slice(m * P, (m + 1) * P)
                            for k in range(k0, k1):
                                last = products(ps[(q + 1) % 2 * 4 + m][:, 0:N], w[:, k - k0, ms],
                                                wl[:, k - k0, ms], faH[:, k, :], faL[:, k, :],
                                                k == 0, k == FC - 1)
                    last.then_inc(used, 1)

            def route():
                rows = (P, P, NS)
                pe.wait_ge(s_rtr, 16)
                for t in range(3):
                    for k in range(KC):
                        last = mm(ps[1][0:rows[t], t * NE:(t + 1) * NE], hT[:, k, t * P:t * P + rows[t]],
                                  rtr[:, k, :], start=(k == 0), stop=(k == KC - 1))
                last.then_inc(s_lg, 1)
                for t in range(3):
                    for q in range(2):
                        n = 2 * t + q
                        if n >= 2:
                            pe.wait_ge(s_htk, n - 1)
                        for c in range(4):
                            last = nc.tensor.transpose(ps[2 + n % 2][0:rows[t], c * P:(c + 1) * P],
                                                       hT[:, 4 * q + c, t * P:t * P + rows[t]], ident[:])
                        last.then_inc(s_htp, 1)
                pe.wait_ge(s_msk, 1)
                m = rt[:, 2]
                for t in range(3):
                    o_ = ps[0][0:rows[t], t * NE:(t + 1) * NE]
                    for s in range(t):
                        mm(o_, ones[:, 0:rows[t]], m[:, s, :], start=(s == 0), stop=False)
                    mm(o_, before[0:rows[t], 0:rows[t]], m[0:rows[t], t, :], start=(t == 0), stop=True)
                for t in range(3):
                    last = mm(ps[0][:, 3 * NE:4 * NE], ones[0:rows[t], :], m[0:rows[t], t, :],
                              start=(t == 0), stop=(t == 2))
                last.then_inc(s_rk, 1)

            def gather(n, q):
                pe.wait_ge(s_sel, n + 1)
                for c in range(4 * q, 4 * q + 4):
                    for t in range(3):
                        last = mm(ps[7][:, c % 4 * P:c % 4 * P + P],
                                  h2tok[0:ROWS[t], t, c * P:(c + 1) * P], sel[0:ROWS[t], t, :],
                                  start=(t == 0), stop=(t == 2))
                last.then_inc(s_gth, 1)

            def turn_gates():
                for t in range(3):
                    last = nc.tensor.transpose(ps[7][:, t * P:t * P + ROWS[t]], gat[0:ROWS[t], t, :],
                                               ident[0:ROWS[t], 0:ROWS[t]])
                last.then_inc(s_gTp, 1)

            def moe():
                pe.wait_ge(s_tab, 1)
                lots = pe.value_load(tab[0:1, 0:1], min_val=NE, max_val=MAXLOTS)
                pe.wait_ge(s_htk, 6)
                gather(0, 0)
                pe.wait_ge(s_hgL, 1)
                gather(0, 1)
                with pe.Fori(0, lots) as i:
                    pe.wait_ge(s_hgL, i * 2 + 2)
                    for t, (kind, g) in enumerate(LOT_ORDER):
                        b = t % 3
                        pe.wait_ge(s_lo, i * LS + t + 1)
                        if kind < 2:
                            if g >= 2:
                                pe.wait_ge(s_mua, i * G + g - 1)
                            h_, l_ = (x[b][:, :].rearrange("p (k n) -> p k n", k=KC) for x in (wH, wL))
                            for k in range(KC):
                                last = products(ps[2 * kind + g % 2][:, 0:256], hgH[:, k, :], hgL[:, k, :],
                                                h_[:, k, :], l_[:, k, :], k == 0, k == KC - 1)
                        else:
                            if g == 0:
                                pe.wait_ge(s_yt, i * 2 + 2)
                            pe.wait_ge(s_aL, i * G + g + 1)
                            h_, l_ = (x[b][:, :].rearrange("p (k n) -> p k n", k=2) for x in (wH, wL))
                            for m in range(2):
                                js = slice(m * LOT, (m + 1) * LOT)
                                for n in range(2):
                                    cs = slice(n * 512, (n + 1) * 512)
                                    last = products(ps[4 + n][:, :], aH[g % 2][:, js], aL[g % 2][:, js],
                                                    h_[:, m, cs], l_[:, m, cs],
                                                    g == 0 and m == 0, g == G - 1 and m == 1)
                        last.then_inc(used, 1)
                        if t in TURN_AT:
                            g = TURN_AT[t]
                            pe.wait_ge(s_mua, i * G + g + 1)
                            for m in range(2):
                                last = nc.tensor.transpose(ps[6][:, m * P:(m + 1) * P], ac[g % 2][:, m, :],
                                                           ident[:])
                            last.then_inc(s_aT, 1)
                        if t in SCATTER_AT:
                            c = SCATTER_AT[t]
                            pe.wait_ge(s_gT, i + 1)
                            pe.wait_ge(s_scd, i * KC + c + 1)
                            mm(ps[7][:, 0:N], ytok[:, c * P:(c + 1) * P], gatT, start=True, stop=True)\
                                .then_inc(s_sc, 1)
                        if t == GATES_AT:
                            pe.wait_ge(s_scd, i * KC + KC + 1)
                            turn_gates()
                        if t == LS - 3:
                            pe.wait_ge(s_gT, i + 2)
                            gather(i + 1, 0)
                        if t == LS - 2:
                            pe.wait_ge(s_hgL, i * 2 + 3)
                            gather(i + 1, 1)
                pe.wait_ge(s_yt, lots * 2 + 2)
                pe.wait_ge(s_hgL, lots * 2 + 2)
                for c in range(KC):
                    if c >= 2:
                        pe.wait_ge(s_scd, lots * KC + c)
                    mm(ps[6 + c % 2][:, 0:N], ytok[:, c * P:(c + 1) * P], gatT, start=True, stop=True)\
                        .then_inc(s_sc, 1)

            layer(0)
            dense()
            layer(1)
            route()
            st.align()
            assert st.n == SLABS
            moe()
            pe.wait_ge(s_sq, 2 * L + 1)
            for k in range(KC):
                last = mm(ps[0][:, 0:N], mean[D][:], yT[:, k, :], start=(k == 0), stop=(k == KC - 1))
            last.then_inc(s_ms, 1)
            pe.wait_ge(s_fin, 1)
            rows = (P, P, NS)
            for t in range(3):
                for q in range(2):
                    n = 2 * t + q
                    if n >= 2:
                        pe.wait_ge(s_fr, n - 1)
                    for c in range(4):
                        last = nc.tensor.transpose(ps[2 + n % 2][0:rows[t], c * P:(c + 1) * P],
                                                   hT[:, 4 * q + c, t * P:t * P + rows[t]], ident[:])
                    last.then_inc(s_ft, 1)

        @block.scalar
        def _(act_):
            A = nc.scalar.activation
            ch = Chain(act_, c_act)

            def rows(name, tile, r0, src, n):
                act_.dma_start(prow[r0:r0 + n, tile, :], src).then_inc(s_row, 16)

            def flat(x, names):
                return x.rearrange(names, p=P)

            rows("mod_b", 0, 0, flat(a["mod_b"], "l (c p) -> (l c) p"), 96)
            rows("g1", 0, 96, flat(a["norm1_g"], "l (c p) -> (l c) p"), 16)
            rows("g2", 0, 112, flat(a["norm2_g"], "l (c p) -> (l c) p"), 16)
            rows("cw", 1, 0, flat(a["conv_w"], "l j (c p) -> (l j c) p"), 32)
            for n_, (name, r0) in enumerate((("conv_b", 32), ("rg_ba", 40), ("rg_bx", 48), ("rg_lambda", 56),
                                             ("rg_out_g", 64), ("hg_lb_logits", 72), ("hg_norm_g", 80))):
                rows(name, 1, r0, flat(a[name], "l (c p) -> (l c) p"), 8)
            rows("final_g", 1, 88, a["final_g"].rearrange("(c p) -> c p", p=P), 8)
            rows("c_prompt", 1, 96, flat(a["c_prompt"], "b (c p) -> (b c) p"), 8)
            rows("c_sample", 2, 0, flat(a["c_sample"], "b (c p) -> (b c) p"), 64)
            rows("state_h", 2, 64, flat(a["state_rglru_h"], "l b (c p) -> (l b c) p"), 64)
            for l in range(L):
                rows("conv", 3 + l, 0, flat(a["state_rglru_conv"][l], "b j (c p) -> (b j c) p"), 96)
            act_.dma_start(xrow[:, 0:2, :], a["x_prompt"][0].rearrange("(t p) c -> p t c", p=P))\
                .then_inc(s_xrow, 16)
            act_.dma_start(xrow[0:NS, 2, :], a["x_sample"].rearrange("b t c -> (b t) c")).then_inc(s_xrow, 16)
            act_.dma_start(S[:, :, :], a["state_hgrn"][0].rearrange("b h d e -> d (b h) e")).then_inc(s_S, 16)
            act_.dma_start(rtr[:, :, :], a["router_w"][0].rearrange("(k p) e -> p k e", p=P)).then_inc(s_rtr, 16)
            for l in range(L):
                act_.dma_start(o["new_conv_sample"][l, :, 0:2, :], a["state_rglru_conv"][l, :, 1:3, :])\
                    .then_inc(s_out, 16)
                outs[0] += 1
            act_.wait_ge(s_gwz, 1)

            def gate_weights(l):
                for x, name in enumerate(("rg_wa", "rg_wx")):
                    for half in range(2):
                        src = a[name][l].rearrange("(c two) i j -> two i c j", two=2)[half]
                        act_.dma_start(gw[64 * half:64 * half + 64, x, :, 64 * half:64 * half + 64], src)\
                            .then_inc(s_gw, 16)

            gate_weights(0)
            act_.wait_ge(s_parT, 1)
            ch(A(par[:, 0:232], ps[0][:, 0:232], ACT.Copy))
            ch(A(par[:, 256:480], ps[0][:, 256:480], ACT.Copy))
            A(par[:, 512:608], ps[1][:, 0:96], ACT.Copy).then_inc(s_par, 1)
            act_.wait_ge(s_par, 1)
            A(cond[:, :, 0], par[:, CP:CP + KC], ACT.Tanh, scale=0.5)
            A(cond[:, :, 1:COND], par[:, CS:CS + 64].rearrange("p (b c) -> p c b", c=KC), ACT.Tanh, scale=0.5)\
                .then_inc(s_act0, 1)
            for c in range(KC):
                act_.wait_ge(s_xTp, c + 1)
                A(xT[:, c, :], ps[2 + c % 4][:, 0:N], ACT.Copy).then_inc(s_xT, 1)
            act_.wait_ge(s_dve0, 1)
            A(sm[:, 1, 0:8], sm[:, 0, 0:8], ACT.Exp, scale=-1.0)
            A(sm[:, 3, 0:8], sm[:, 2, 0:8], ACT.Exp).then_inc(s_act0, 1)

            rowed = [0]

            def mod_row(count):
                for n in range(rowed[0], rowed[0] + count):
                    act_.wait_ge(used, MOD_SLAB[n] + 1)
                    A(modrow[:, n % 2, :], mod_rows(n), ACT.Copy).then_inc(s_mev, 1)
                rowed[0] += count

            mod_row(MOD_DONE[0])

            def rsqrt(out, in_):
                ch(A(out, in_, ACT.Ln, bias=eps[:, 0:1]))
                return A(out, out, ACT.Exp, scale=-0.5)

            def norm(n):
                if n == 0:
                    act_.wait_ge(s_xT, KC)
                else:
                    act_.wait_ge(s_x, n)
                A(yT[:, :, :], xT[:, :, :], ACT.Square).then_inc(s_sq, 1)

            def layer(l):
                if l:
                    norm(2 * l)
                else:
                    norm(0)
                act_.wait_ge(s_ms, 3 * l + 1)
                rsqrt(rs[:, :], ps[0][:, 0:N]).then_inc(s_rs, 1)
                j = 0
                for grp in ORDER:
                    for m in range(4):
                        if m % 2 == 0:
                            act_.wait_ge(s_up, (U // 2) * l + j // 2 + 1)
                        else:
                            act_.wait_ge(used, W_IN[l] + j // 2 + 1)
                        dst = xaP[:, m, CW - 1:] if grp == 0 else u[:, 4 * grp + m, :]
                        if grp == 0:
                            ch(A(u[:, m, T:N], ps[j % 4][:, T:N], ACT.Copy))
                            A(dst, ps[j % 4][:, 0:T], ACT.Copy).then_inc(s_u, 1)
                        else:
                            A(dst, ps[j % 4][:, 0:N], ACT.Copy).then_inc(s_u, 1)
                        j += 1
                    if grp == 3:
                        act_.wait_ge(s_u, U * l + j)
                        A(FB, FB, ACT.Exp, scale=-1.0).then_inc(s_fe, 1)
                    if grp == 2:
                        act_.wait_ge(s_f, l + 1)
                        A(oT[:, :, 0:T], oT[:, :, 0:T], ACT.Ln)
                        A(bT[:, :, :], bT[:, :, :], ACT.Ln, scale=2.0 ** 66).then_inc(s_lnf, 1)
                        act_.wait_ge(s_u, U * l + j)
                        A(g2, QB, ACT.Tanh, scale=0.5).then_inc(s_tq, 1)
                    if grp == 4:
                        act_.wait_ge(s_vp, l + 1)
                        ch(A(vtok[:, 0, :, :], ps[4][:, :].rearrange("p (h e) -> p h e", h=H), ACT.Copy))
                        A(vtok[:, 1, :, :], ps[5][:, :].rearrange("p (h e) -> p h e", h=H), ACT.Copy)\
                            .then_inc(s_v, 1)
                        for c in range(AC):
                            for w in range(2):
                                act_.wait_ge(s_gp, 8 * l + 2 * c + w + 1)
                                bias = sm[:, 4 + w, AC * l + c:AC * l + c + 1]
                                A((rg, ig)[w][:, c, :], ps[4 + w][:, 0:N], ACT.Tanh, bias=bias,
                                  scale=0.5).then_inc(s_tg, 1)
                        act_.wait_ge(s_rdy, l + 1)
                        for c in range(AC):
                            A(ag[:, c, :], rg[:, c, :], ACT.Exp, scale=coef[:, l, c:c + 1])
                        for c in range(AC):
                            ins = A(mu[:, c, :], rg[:, c, :], ACT.Tanh, scale=coef[:, l, c:c + 1])
                        ins.then_inc(s_a, 1)
                act_.wait_ge(s_gi, l + 1)
                A(gt, gt, ACT.Tanh, scale=0.7978845608028654).then_inc(s_tge, 1)
                act_.wait_ge(s_u, U * (l + 1))
                A(oT[:, :, :], GB, ACT.Tanh, scale=0.5).then_inc(s_tgb, 1)
                fill = FILL[l]
                mod_row(1)
                act_.wait_ge(s_m2, l + 1)
                A(mu, mu, ACT.Sqrt).then_inc(s_mu, 1)
                mod_row(fill[0] - 1)
                act_.wait_ge(s_ms, 3 * l + 2)
                rsqrt(rs[:, :], ps[4][:, 0:N]).then_inc(s_rs, 1)
                for v in range(1, LEVELS + 1):
                    act_.wait_ge(s_ld, LEVELS * l + v)
                    A(LD[v % 2], LD[v % 2], ACT.Exp).then_inc(s_le, 1)
                    if v >= 2:
                        mod_row(fill[1][v - 2])
                for h in range(H):
                    ins = A(ke[:, h, :], bT[:, h, :], ACT.Exp, scale=-1.0, bias=bT[:, h, T - 1:T])
                ins.then_inc(s_kx, 1)
                mod_row(sum(fill[1][LEVELS - 1:]))
                act_.wait_ge(s_kp, l + 1)
                ch(A(keT[:, 0], ps[4][:, :].rearrange("p (h e) -> p h e", h=H), ACT.Copy))
                A(keT[:, 1], ps[5][:, :].rearrange("p (h e) -> p h e", h=H), ACT.Copy).then_inc(s_keT, 1)
                act_.wait_ge(s_op, l + 1)
                ch(A(oT[:, 0:2, 0:T], ps[0][:, :].rearrange("p (h t) -> p h t", h=2), ACT.Copy))
                A(oT[:, 2:4, 0:T], ps[1][:, :].rearrange("p (h t) -> p h t", h=2), ACT.Copy)
                act_.wait_ge(s_sf, l + 1)
                act_.wait_ge(s_ke, l + 1)
                act_.wait_ge(s_kp, l + 1)
                A(sfin, ps[5][:, :], ACT.Copy).then_inc(s_sfs, 1)
                act_.wait_ge(s_sfs, l + 1)
                act_.dma_start(o["new_S_prompt"][l, 0].rearrange("h d e -> d h e"),
                               sfin.rearrange("p (h e) -> p h e", h=H)).then_inc(s_st, 16)
                mod_row(sum(fill[2]))
                act_.wait_ge(s_osp, l + 1)
                ch(A(oT[:, :, T:N], ps[4][:, 0:H * NS].rearrange("p (h b) -> p h b", h=H), ACT.Copy))
                A(yT[:, AC:, :], oT[:, :, :], ACT.Square).then_inc(s_os, 1)
                mod_row(fill[3])
                act_.wait_ge(s_vbd, NS * (l + 1))
                act_.dma_start(o["new_S_sample"][l].rearrange("b h d e -> d (b h) e"), S[:, :, :])\
                    .then_inc(s_st, 16)
                act_.wait_ge(s_oms, l + 1)
                for h in range(H):
                    ch(A(LN_OUT(h), ps[h][:, 0:N], ACT.Ln, bias=eps[:, 0:1]))
                A(ar[:, 0:W4], ar[:, 0:W4], ACT.Exp, scale=-0.5).then_inc(s_ors, 1)
                mod_row(fill[4])
                assert rowed[0] == MOD_DONE[l + 1]
                if l + 1 < L:
                    gate_weights(l + 1)
                act_.wait_ge(s_ocp, l + 1)
                A(outr[l][:, :], ps[4][0:80, 0:P], ACT.Copy).then_inc(s_or, 1)
                act_.wait_ge(s_or, l + 1)
                for dst, r0, n_ in (
                        (o["new_h_prompt"][l, 0].rearrange("(c p) -> c p", p=P), 0, 4),
                        (o["new_h_sample"][l].rearrange("b (c p) -> (b c) p", p=P), 4, 32),
                        (o["new_conv_prompt"][l, 0].rearrange("j (c p) -> (j c) p", p=P), 36, 12)):
                    act_.dma_start(dst, outr[l][r0:r0 + n_, :]).then_inc(s_out, 16)
                    outs[0] += 1
                for b in range(NS):
                    act_.dma_start(o["new_conv_sample"][l, b, CW - 2].rearrange("(c p) -> c p", p=P),
                                   outr[l][48 + 4 * b:52 + 4 * b, :]).then_inc(s_out, 16)
                    outs[0] += 1
                norm(2 * l + 1)
                if l == 0:
                    act_.wait_ge(s_st, 2 * 16)
                    for d in range(2):
                        ffn_slab(d)
                act_.wait_ge(s_ms, 3 * l + 3)
                rsqrt(rs[:, :], ps[0][:, 0:N]).then_inc(s_rs, 1)

            def LN_OUT(h):
                return ar[:, h * N:(h + 1) * N]

            def ffn_slab(d):
                s_, loads, width = FFN_SLOT[d]
                act_.wait_ge(full[s_], 16 * loads)
                if d >= 2:
                    act_.wait_ge(used, FFN + d - 1)
                A(wH[d % 2][:, 0:width], ring[:, s_, 0:width], ACT.Copy).then_inc(s_fwH, 1)

            layer(0)
            for half in range(2):
                act_.wait_ge(s_h, 2)
                c = slice(4 * half, 4 * half + 4)
                A(fhH[:, c, :], hT[:, c, :], ACT.Copy).then_inc(s_fhH, 1)
            for d in range(2, FS):
                ffn_slab(d)
                if d % 2 == 0 and d <= 2 * G:
                    g = d // 2 - 1
                    act_.wait_ge(s_fa, 2 * g) if g else None
                    for m in range(2):
                        A(fsg[m], ps[g % 2 * 4 + m][:, 0:N], ACT.Silu).then_inc(s_fs, 1)
                if d % 2 == 0 and 4 <= d <= 2 * G + 2:
                    g = d // 2 - 2
                    for m in range(2):
                        act_.wait_ge(s_fa, 2 * g + m + 1)
                        A(faH[:, 2 * g + m, :], fac[m], ACT.Copy).then_inc(s_faH, 1)
            act_.wait_ge(used, FFN + FS)
            act_.dma_start(S[:, :, :], a["state_hgrn"][1].rearrange("b h d e -> d (b h) e")).then_inc(s_S, 16)
            layer(1)
            rws = (P, P, NS)
            for n in range(6):
                act_.wait_ge(s_htp, n + 1)
                A(h2tok[0:rws[n // 2], n // 2, n % 2 * 512:n % 2 * 512 + 512], ps[2 + n % 2][0:rws[n // 2], :],
                  ACT.Copy).then_inc(s_htk, 1)
            act_.wait_ge(s_red, 1)
            A(rt[:, 20, :, 0], rt[:, 19, :, 0], ACT.Exp).then_inc(s_re, 1)
            act_.wait_ge(s_tab, 1)
            lots = act_.value_load(tab[0:1, 0:1], min_val=NE, max_val=MAXLOTS)

            cp = nc.scalar.copy

            def gathered(n, q):
                act_.wait_ge(s_gth, n * 2 + q + 1)
                cp(hgH[:, 4 * q:4 * q + 4, :], ps[7][:, :].rearrange("p (c j) -> p c j", c=4)).then_inc(s_hgH, 1)

            def outputs(n):
                act_.wait_ge(used, n * LS + SLABS)
                for m in range(2):
                    cp(ytok[:, m * 512:(m + 1) * 512], ps[4 + m][:, :]).then_inc(s_yt, 1)

            act_.wait_ge(s_st, 2 * 16 * L)
            gathered(0, 0)
            gathered(0, 1)
            with act_.Fori(0, lots) as i:
                slot = slots(act_, i)
                for t in range(LS):
                    w = slot(t)
                    act_.wait_ge(used, i * LS + SLABS + t - 2)
                    cp(wH[t % 3][:, :], w).then_inc(s_hi, 1)
                    if t == 2:
                        outputs(i)
                    if t in FORM_AT:
                        g = FORM_AT[t]
                        act_.wait_ge(used, i * LS + SLABS + LOT_ORDER.index((0, g)) + 1)
                        if g >= 2:
                            act_.wait_ge(s_mua, i * G + g - 1)
                        A(sg[g % 2], ps[g % 2][:, 0:256].rearrange("p (m j) -> p m j", m=2), ACT.Silu)\
                            .then_inc(s_mus, 1)
                    if t == LS - 1:
                        gathered(i + 1, 0)
                    if t in DOWN_AT:
                        g = DOWN_AT[t]
                        act_.wait_ge(s_aT, i * G + g + 1)
                        cp(aH[g % 2][:, :], ps[6][:, 0:256]).then_inc(s_aH, 1)
                gathered(i + 1, 1)
            outputs(lots)
            act_.wait_ge(s_x, 2 * L)
            A(yT[:, :, :], xT[:, :, :], ACT.Square).then_inc(s_sq, 1)
            act_.wait_ge(s_ms, 3 * L + 1)
            rsqrt(rs[:, :], ps[0][:, 0:N]).then_inc(s_rs, 1)
            for n in range(6):
                act_.wait_ge(s_ft, n + 1)
                A(yrow[0:rws[n // 2], n // 2, n % 2 * 512:n % 2 * 512 + 512], ps[2 + n % 2][0:rws[n // 2], :],
                  ACT.Copy).then_inc(s_fr, 1)
            act_.wait_ge(s_fr, 6)
            act_.dma_start(o["y_prompt"][0].rearrange("(t p) c -> p t c", p=P), yrow[:, 0:2, :])\
                .then_inc(s_out, 16)
            act_.dma_start(o["y_sample"].rearrange("b t c -> (b t) c"), yrow[0:NS, 2, :]).then_inc(s_out, 16)
            outs[0] += 2
            act_.wait_ge(s_out, 16 * outs[0])

        @block.vector
        def _(dve):
            V = nc.vector
            ch = Chain(dve, c_dve)
            tt, ts, stt = V.tensor_tensor, V.tensor_scalar, V.scalar_tensor_tensor

            dve.wait_ge(s_cst, 1)
            ti, si, xi = (ar[:, n * P:(n + 1) * P].bitcast(i32) for n in (0, 1, 2))
            ch(tt(xi, ti, si, ALU.bitwise_xor))
            ch(ts(mask[:, 0, :], xi, 0.0, None, ALU.is_equal))
            for v in range(1, LEVELS):
                sh = ar[:, 3 * P:4 * P].bitcast(i32)
                ch(ts(sh, xi, v - 1, None, ALU.logical_shift_right))
                ch(stt(mask[:, v, :], sh, 1.0, before[:], ALU.is_equal, ALU.mult))
            dve.wait_ge(s_par, 1)
            lam = par[:, LAM:LAM + 8]
            ch(stt(sm[:, 0, 0:8], lam, -1.0, lam, ALU.mult, ALU.max))
            l0, l1 = par[:, LBL:LBL + 4], par[:, LBL + 4:LBL + 8]
            ch(tt(sm[:, 6, 0:4], l0, l1, ALU.max))
            ch(tt(sm[:, 2, 0:4], l0, sm[:, 6, 0:4], ALU.subtract))
            tt(sm[:, 2, 4:8], l1, sm[:, 6, 0:4], ALU.subtract).then_inc(s_dve0, 1)
            ts(sm[:, 4, 0:8], par[:, BA:BA + 8], 0.5, None, ALU.mult)
            ch(ts(sm[:, 5, 0:8], par[:, BX:BX + 8], 0.5, None, ALU.mult))
            dve.wait_ge(s_act0, 1)
            ch(stt(cond[:, :, 0], cond[:, :, 0], 1.0, par[:, CP:CP + KC], ALU.add, ALU.mult))
            ch(stt(cond[:, :, 1:COND], cond[:, :, 1:COND], 1.0,
                   par[:, CS:CS + 64].rearrange("p (b c) -> p c b", c=KC), ALU.add, ALU.mult))
            ts(cond[:, :, :], cond[:, :, :], 0.5, None, ALU.mult).then_inc(s_cond, 1)
            dve.wait_ge(s_act0, 2)
            z, q, q2, pz = sm[:, 1, 0:8], sm[:, 7, 0:8], sm[:, 8, 0:8], sm[:, 9, 0:8]
            ch(ts(q, z, 2.0, None, ALU.add))
            ch(V.reciprocal(q, q))
            ch(tt(q, q, z, ALU.mult))
            ch(tt(q2, q, q, ALU.mult))
            ch(ts(pz, q2, 1.0 / 15, 1.0 / 13, ALU.mult, ALU.add))
            for d in (11, 9, 7, 5, 3, 1):
                ch(tt(pz, pz, q2, ALU.mult))
                ch(ts(pz, pz, 1.0 / d, None, ALU.add))
            ch(tt(pz, pz, q, ALU.mult))
            ch(ts(q, lam, -1.0, 0.0, ALU.mult, ALU.max))
            ch(stt(q, pz, 2.0, q, ALU.mult, ALU.add))
            ch(ts(coef[:].rearrange("p l c -> p (l c)"), q, -8.0, None, ALU.mult))
            e = sm[:, 3, 0:8]
            ch(tt(sm[:, 10, 0:4], e[:, 0:4], e[:, 4:8], ALU.add))
            ch(V.reciprocal(sm[:, 10, 0:4], sm[:, 10, 0:4]))
            ch(V.memset(lb[:, 0, :], 0.0))
            ch(tt(lb[:, 1, :], e[:, 4:8], sm[:, 10, 0:4], ALU.mult))
            ch(ts(omlb[:], lb[:], -1.0, 1.0, ALU.mult, ALU.add))

            def mod_batch(i):
                n0, n1 = ((0,) + MOD_DONE)[i:i + 2]
                dve.wait_ge(s_mtr, n1)
                tt(modT[:, :, :, :].rearrange("p l c b -> p (l c) b")[:, 2 * n0:2 * n1, :],
                   mod_columns(n0, n1 - n0), wide(par[:, MODB + 2 * n0:MODB + 2 * n1], COND), ALU.add)\
                    .then_inc(s_mod, 1)

            mod_batch(0)
            dve.wait_ge(s_mod, 1)

            def modulate(l, which, gcol):
                sc = modT[:, l, (3 * which + 1) * KC:(3 * which + 2) * KC, :]
                shf = modT[:, l, 3 * which * KC:(3 * which + 1) * KC, :]
                ch(stt(modA[:, :, :], sc, 1.0, wide(par[:, gcol + KC * l:gcol + KC * (l + 1)], COND),
                       ALU.add, ALU.mult))
                dve.wait_ge(s_rs, 3 * l + (1 if which == 0 else 3))
                ch(tt(hT[:, :, :], xT[:, :, :], rs[:, :].unsqueeze(1).broadcast_to([P, KC, N]), ALU.mult))
                for c in range(KC):
                    ts(hT[:, c, 0:T], hT[:, c, 0:T], modA[:, c, 0:1], shf[:, c, 0:1], ALU.mult, ALU.add)
                ch(tt(hT[:, :, T:N], hT[:, :, T:N], modA[:, :, 1:COND], ALU.mult))
                tt(hT[:, :, T:N], hT[:, :, T:N], shf[:, :, 1:COND], ALU.add).then_inc(s_h, 1)

            def residual(l, part, c, bank):
                gate = modT[:, l, (3 * part + 2) * KC + c, :]
                stt(xT[:, c, 0:T], bank[:, 0:T], gate[:, 0:1], xT[:, c, 0:T], ALU.mult, ALU.add)
                ch(tt(sm[:, 11, 0:NS], bank[:, T:N], gate[:, 1:COND], ALU.mult))
                return tt(xT[:, c, T:N], xT[:, c, T:N], sm[:, 11, 0:NS], ALU.add)

            def layer(l):
                modulate(l, 0, G1)
                ch(V.memset(AT[:, :, :, :], 0.0))
                dve.wait_ge(s_fe, l + 1)
                ch(ts(FB, FB, 1.0, None, ALU.add))
                ch(V.reciprocal(FB, FB))
                for h in range(H):
                    ins = ts(FB[:, h, :], FB[:, h, :], omlb[:, l, h:h + 1], lb[:, l, h:h + 1], ALU.mult, ALU.add)
                ch(ins)
                ch(ts(oT[:, :, 0:T], FB[:, :, 0:T], 2.0 ** -60, None, ALU.max))
                ts(bT[:, :, :], FB[:, :, 0:T], 2.0 ** -60, None, ALU.min).then_inc(s_f, 1)
                dve.wait_ge(s_tq, l + 1)
                ch(stt(QB, g2, 1.0, QB, ALU.add, ALU.mult))
                ch(ts(QB, QB, 0.5, None, ALU.mult))
                dve.wait_ge(s_lnf, l + 1)
                ch(stt(oT[:, :, 0:T], bT[:, :, :], LN64, oT[:, :, 0:T], ALU.subtract, ALU.add))
                dve.wait_ge(s_S1, l + 1)
                ch(ts(FB, FB, -1.0, 1.0, ALU.mult, ALU.add))
                for h in range(H):
                    ins = V.tensor_tensor_scan(bT[:, h, :], ones[:, 0:1].broadcast_to([P, T]), oT[:, h, 0:T],
                                               0.0, ALU.mult, ALU.add)
                ins.then_inc(s_b, 1)
                dve.wait_ge(s_u, U * l + 12)
                for c in range(AC):
                    for j in range(CW):
                        w = par[:, CWW + 16 * l + 4 * j + c:CWW + 16 * l + 4 * j + c + 1]
                        x = xaP[:, c, j:j + T]
                        if j == 0:
                            ch(ts(xc[:, c, 0:T], x, w, par[:, CB + 4 * l + c:CB + 4 * l + c + 1],
                                  ALU.mult, ALU.add))
                        else:
                            ch(stt(xc[:, c, 0:T], x, w, xc[:, c, 0:T], ALU.mult, ALU.add))
                cst = par[:, SCV + P * l:SCV + P * l + 96].rearrange("p (b j c) -> p j c b", j=CW - 1, c=AC)
                xs = xc[:, :, T:N]
                tmp = sm[:, 12:14, :].rearrange("p a b -> p (a b)").rearrange("p (c b) -> p c b", c=AC)
                for j in range(CW):
                    src = cst[:, j] if j < CW - 1 else XA[:, :, T:N]
                    w = wide(par[:, CWW + 16 * l + 4 * j:CWW + 16 * l + 4 * j + 4], NS)
                    ch(tt(tmp, src, w, ALU.mult))
                    other = wide(par[:, CB + 4 * l:CB + 4 * l + 4], NS) if j == 0 else xs
                    ins = tt(xs, tmp, other, ALU.add)
                    if j < CW - 1:
                        ch(ins)
                ins.then_inc(s_xc, 1)
                if l:
                    dve.wait_ge(s_or, l)
                oc = outc[:, :]
                V.tensor_copy(oc[:, 36:48].rearrange("p (j c) -> p c j", c=AC), xaP[:, :, T:T + 3])
                V.tensor_copy(oc[:, 48:80].rearrange("p (b c) -> p c b", c=AC), XA[:, :, T:N])
                dve.wait_ge(s_tg, 8 * (l + 1))
                ts(rg, rg, 0.5, 0.5, ALU.mult, ALU.add).then_inc(s_rdy, 1)
                ch(stt(ig, ig, 1.0, xc, ALU.add, ALU.mult))
                dve.wait_ge(s_u, U * l + 20)
                ch(tt(gt, GA, GA, ALU.mult))
                ch(ts(gt, gt, 0.044715, 1.0, ALU.mult, ALU.add))
                tt(gt, gt, GA, ALU.mult).then_inc(s_gi, 1)
                dve.wait_ge(s_a, l + 1)
                ch(ts(g2, mu, -1.0, 1.0, ALU.mult, ALU.add))
                ch(V.reciprocal(g2, g2))
                stt(mu, mu, -2.0, g2, ALU.mult, ALU.mult).then_inc(s_m2, 1)
                dve.wait_ge(s_mu, l + 1)
                ch(V.memset(ag[:, :, 0:1], 0.0))
                ch(V.memset(mu[:, :, 0:1], 1.0))
                ch(stt(ig, ig, 0.5, mu, ALU.mult, ALU.mult))
                for c in range(AC):
                    ins = V.tensor_tensor_scan(rg[:, c, 0:T], ag[:, c, 0:T], ig[:, c, 0:T], 0.0,
                                               ALU.mult, ALU.add)
                ch(ins)
                h0 = par[:, SH + 32 * l:SH + 32 * (l + 1)].rearrange("p (b c) -> p c b", c=AC)
                ch(tt(rg[:, :, T:N], ag[:, :, T:N], h0, ALU.mult))
                ch(tt(rg[:, :, T:N], rg[:, :, T:N], ig[:, :, T:N], ALU.add))
                V.tensor_copy(oc[:, 0:4], rg[:, :, T - 1])
                V.tensor_copy(oc[:, 4:36].rearrange("p (b c) -> p c b", c=AC), rg[:, :, T:N]).then_inc(s_oc, 1)
                dve.wait_ge(s_tge, l + 1)
                ch(stt(gt, gt, 1.0, GA, ALU.add, ALU.mult))
                ch(stt(gt, gt, 0.5, rg, ALU.mult, ALU.mult))
                tt(g2, gt, gt, ALU.mult).then_inc(s_zs, 1)
                dve.wait_ge(s_tgb, l + 1)
                ch(stt(GB, oT[:, :, :], 1.0, GB, ALU.add, ALU.mult))
                for h in range(H):
                    ts(GB[:, h, :], GB[:, h, :], 0.5, par[:, HG + 4 * l + h:HG + 4 * l + h + 1],
                       ALU.mult, ALU.mult)
                dve.wait_ge(s_rs, 3 * l + 2)
                for c in range(AC):
                    ins = stt(yT[:, c, :], gt[:, c, :],
                              par[:, OG + 4 * l + c:OG + 4 * l + c + 1], rs[:, :], ALU.mult, ALU.mult)
                ch(ins)

                def diff(v):
                    h2 = 1 << (v - 1)
                    b4 = bT[:, :, :].rearrange("p h (n two i) -> p (h n) two i", two=2, i=h2)
                    d4 = LD[v % 2].rearrange("p (n two i) -> p n two i", two=2, i=h2)
                    mid = b4[:, :, 0, h2 - 1:h2]
                    n = b4.shape[1]
                    midb = mid.broadcast_to([P, n, h2])
                    ch(tt(d4[:, :, 1, :], b4[:, :, 1, :], midb, ALU.subtract))
                    tt(d4[:, :, 0, :], midb, b4[:, :, 0, :], ALU.subtract).then_inc(s_ld, 1)

                def take(v):
                    dve.wait_ge(s_lp, (LEVELS + 1) * l + v + 1)
                    if l or v:
                        dve.wait_ge(s_lc, (LEVELS + 1) * l + v)
                    if v == LEVELS:
                        V.tensor_copy(ATx[:, :, :], ps[0][:, :].rearrange("p (h t) -> p h t", h=H))\
                            .then_inc(s_lc, 1)
                        return
                    for t in range(2):
                        ins = V.copy_predicated(AT[:, t], mask[:, v, :].unsqueeze(1).broadcast_to([P, H, P]),
                                                ps[2 * (v % 2) + t][:, :].rearrange("p (h t) -> p h t", h=H))
                    ins.then_inc(s_lc, 1)

                dve.sem_inc(s_lw, 1)
                diff(1)
                for v in range(1, LEVELS + 1):
                    if v < LEVELS:
                        dve.wait_ge(s_lw, (LEVELS + 1) * l + v)
                        diff(v + 1)
                    h2 = 1 << (v - 1)
                    dve.wait_ge(s_le, LEVELS * l + v)
                    d4, w4 = (x[v % 2].rearrange("p (h n two i) -> p h n two i", h=H, two=2, i=h2)
                              for x in (LD, LW))
                    for h in range(H):
                        qs = QB[:, h, 0:T].rearrange("p (n two i) -> p n two i", two=2, i=h2)
                        ks = FB[:, h, 0:T].rearrange("p (n two i) -> p n two i", two=2, i=h2)
                        tt(w4[:, h, :, 1, :], d4[:, h, :, 1, :], qs[:, :, 1, :], ALU.mult)
                        ins = tt(w4[:, h, :, 0, :], d4[:, h, :, 0, :], ks[:, :, 0, :], ALU.mult)
                    ins.then_inc(s_lw, 1)
                    take(v - 1)
                take(LEVELS)
                dve.wait_ge(s_kx, l + 1)
                tt(ke, ke, FB[:, :, 0:T], ALU.mult).then_inc(s_ke, 1)
                dve.wait_ge(s_S1, l + 1)
                for b in range(NS):
                    dve.wait_ge(s_vb, NS * l + b + 1)
                    if b:
                        dve.wait_ge(s_vbd, NS * l + b)
                    ch(tt(vbk, ps[2 + b % 2][:, :].rearrange("p (h e) -> p h e", h=H),
                          wide(FB[:, :, T + b], P), ALU.mult))
                    ins = tt(S[:, b * H:(b + 1) * H, :], S[:, b * H:(b + 1) * H, :], vbk, ALU.add)
                    ins.then_inc(s_vbd, 1)
                dve.wait_ge(s_ors, l + 1)
                ch(tt(yT[:, AC:, :], oT[:, :, :], ar[:, 0:W4].rearrange("p (h n) -> p h n", n=N), ALU.mult))
                tt(yT[:, AC:, :], yT[:, AC:, :], GB, ALU.mult).then_inc(s_y, 1)
                mod_batch(l + 1)
                dve.wait_ge(s_mod, l + 2)
                for c in range(KC):
                    if c % 2 == 0:
                        dve.wait_ge(s_wp, 4 * l + c // 2 + 1)
                    else:
                        dve.wait_ge(used, W_OUT[l] + c // 2 + 1)
                    if c:
                        dve.wait_ge(s_x1, KC * l + c)
                    ins = residual(l, 0, c, ps[c % 4])
                    ins.then_inc(s_x1, 1)
                dve.wait_ge(s_x1, KC * (l + 1))
                dve.sem_inc(s_x, 1)
                if l == 0:
                    for d in range(2):
                        ffn_slab(d)
                modulate(l, 1, G2)

            def ffn_slab(d):
                s_, _, width = FFN_SLOT[d]
                dve.wait_ge(s_fwH, d + 1)
                tt(wL[d % 2][:, 0:width], ring[:, s_, 0:width], wH[d % 2][:, 0:width].bitcast(fp32),
                   ALU.subtract).then_inc(s_fwL, 1)

            def ffn_residual(q):
                dve.wait_ge(used, FFN + 2 * G + 3 * q + 3)
                for c in (2 * q, 2 * q + 1):
                    if c:
                        dve.wait_ge(s_fx, c)
                    residual(0, 1, c, ps[(q + 1) % 2 * 4 + c % 2]).then_inc(s_fx, 1)

            layer(0)
            for half in range(2):
                dve.wait_ge(s_fhH, half + 1)
                c = slice(4 * half, 4 * half + 4)
                tt(fhL[:, c, :], hT[:, c, :], fhH[:, c, :].bitcast(fp32), ALU.subtract).then_inc(s_fhL, 1)
            for d in range(2, FS):
                ffn_slab(d)
                if d % 2 and d <= 2 * G + 1:
                    g = d // 2 - 1
                    dve.wait_ge(used, FFN + 2 * g + 2)
                    for m in range(2):
                        dve.wait_ge(s_fs, 2 * g + m + 1)
                        if g:
                            dve.wait_ge(s_faL, 2 * g - 1 + m)
                        tt(fac[m], fsg[m], ps[g % 2 * 4 + 2 + m][:, 0:N], ALU.mult).then_inc(s_fa, 1)
                if d % 2 == 0 and 4 <= d <= 2 * G + 2:
                    g = d // 2 - 2
                    for m in range(2):
                        dve.wait_ge(s_faH, 2 * g + m + 1)
                        tt(faL[:, 2 * g + m, :], fac[m], faH[:, 2 * g + m, :].bitcast(fp32), ALU.subtract)\
                            .then_inc(s_faL, 1)
                if d >= 2 * G + 4 and (d - 2 * G - 4) % 3 == 0:
                    ffn_residual((d - 2 * G - 4) // 3)
            ffn_residual(3)
            dve.wait_ge(s_fx, KC)
            dve.sem_inc(s_x, 1)
            layer(1)

            rws = (P, P, NS)
            LG, TOP, MSK, POS, OH0, OH1, BLK, EB, GS, T0, T1 = (rt[:, n] for n in (0, 1, 2, 3, 4, 5, 6, 7, 8, 9, 10))
            CNT, EXT, OFF, T2, FI = (rt[:, n, 0, :] for n in (11, 12, 13, 14, 15))
            dve.wait_ge(s_lg, 1)
            ch(V.memset(rt[:, :, :, :], 0.0))
            for t in range(3):
                ch(V.tensor_copy(LG[0:rws[t], t, :], ps[1][0:rws[t], t * NE:(t + 1) * NE]))
            for t in range(3):
                ch(V.max(TOP[:, t, :], LG[:, t, :]))
                ch(V.max_index(ridx[:, t, :], TOP[:, t, :], LG[:, t, :]))
            ch(V.tensor_copy(T0, ridx[:, :, :]))
            io8 = iota[:, 0:NE]
            for t in range(3):
                ch(ts(OH0[:, t, :], io8, T0[:, t, 0:1], None, ALU.is_equal))
                ch(ts(OH1[:, t, :], io8, T0[:, t, 1:2], None, ALU.is_equal))
            tt(MSK, OH0, OH1, ALU.add).then_inc(s_msk, 1)
            tt(rt[:, 19, :, 0], TOP[:, :, 1], TOP[:, :, 0], ALU.subtract).then_inc(s_red, 1)
            dve.wait_ge(s_re, 1)
            ch(ts(wts[:, :, 0], rt[:, 20, :, 0], 1.0, None, ALU.add))
            ch(V.reciprocal(wts[:, :, 0], wts[:, :, 0]))
            ch(tt(wts[:, :, 1], rt[:, 20, :, 0], wts[:, :, 0], ALU.mult))
            dve.wait_ge(s_rk, 1)
            for t in range(3):
                ch(V.tensor_copy(POS[0:rws[t], t, :], ps[0][0:rws[t], t * NE:(t + 1) * NE]))
            ch(V.tensor_copy(CNT, ps[0][:, 3 * NE:4 * NE]))
            ch(ts(T2, CNT, float(LOT), None, ALU.is_gt))
            ch(stt(EXT, CNT, float(2 * LOT), T2, ALU.is_gt, ALU.add))
            ch(V.tensor_tensor_scan(OFF, ones[:, 0:NE], EXT, 0.0, ALU.mult, ALU.add))
            ch(ts(tab[:, 0:1], OFF[:, NE - 1:NE], float(NE), None, ALU.add))
            ch(tt(OFF, OFF, EXT, ALU.subtract))
            ch(ts(OFF, OFF, float(NE), None, ALU.add))
            for i in range(MAXLOTS - NE):
                ch(tt(T2, OFF, EXT, ALU.add))
                ch(ts(T2, T2, float(NE + i), None, ALU.is_gt))
                ch(stt(FI, OFF, float(NE + i), T2, ALU.is_le, ALU.mult))
                ch(tt(FI, FI, io8, ALU.mult))
                ch(V.reduce_sum(sm[:, 15, i:i + 1], FI, AX.X))
            ch(V.tensor_copy(tab[:, 1:1 + MAXLOTS - NE], sm[:, 15, 0:MAXLOTS - NE]))
            ch(ts(BLK, POS, float(LOT), None, ALU.is_ge))
            ch(stt(T2, OFF, -1.0, io8, ALU.add, ALU.subtract))
            ch(tt(EB, BLK, T2.unsqueeze(1).broadcast_to([P, 3, NE]), ALU.mult))
            ch(tt(EB, EB, io8.unsqueeze(1).broadcast_to([P, 3, NE]), ALU.add))
            ch(stt(GS, EB, float(LOT), POS, ALU.mult, ALU.add))
            for n, oh in enumerate((OH0, OH1)):
                ch(tt(T1, GS, oh, ALU.mult))
                ch(V.reduce_sum(gsl[:, :, n], T1, AX.X))
            V.memset(acc[:, :, :], 0.0).then_inc(s_scd, 1)
            dve.wait_ge(s_scd, 1)
            V.memset(gatT, 0.0).then_inc(s_gT, 1)
            ch(V.memset(ps[4][:, :], 0.0))
            ch(V.memset(ps[5][:, :], 0.0))
            dve.sem_inc(s_tab, 1)
            dve.wait_ge(s_tab, 1)

            lots = dve.value_load(tab[0:1, 0:1], min_val=NE, max_val=MAXLOTS)

            def gathered(n, q):
                dve.wait_ge(s_hgH, n * 2 + q + 1)
                tt(hgL[:, 4 * q:4 * q + 4, :], ps[7][:, :].rearrange("p (c j) -> p c j", c=4),
                   hgH[:, 4 * q:4 * q + 4, :].bitcast(fp32), ALU.subtract).then_inc(s_hgL, 1)

            TILES = [(slice(0, ROWS[t]), t) for t in range(3)]

            def choice(step):
                for r, t in TILES:
                    S0, S1, W0 = sel[r, t, :], stmp[r, t, :], gat[r, t, :]
                    if step == 0:
                        ts(S0, iota[r, 0:LOT], gsl[r, t, 0:1], None, ALU.is_equal)
                        ins = ts(S1, iota[r, 0:LOT], gsl[r, t, 1:2], None, ALU.is_equal)
                    elif step == 1:
                        ins = ts(W0, S0, wts[r, t, 0:1], None, ALU.mult)
                    elif step == 2:
                        stt(W0, S1, wts[r, t, 1:2], W0, ALU.mult, ALU.add)
                        ins = tt(S0, S0, S1, ALU.add)
                if step == 2:
                    ins = ts(gsl[:, :, :], gsl[:, :, :], float(-LOT), None, ALU.add)
                return ins

            ch(choice(0))
            ch(choice(1))
            choice(2).then_inc(s_sel, 1)
            gathered(0, 0)
            gathered(0, 1)
            with dve.Fori(0, lots) as i:
                slot = slots(dve, i)
                for t in range(LS):
                    w = slot(t)
                    dve.wait_ge(s_hi, i * LS + t + 1)
                    tt(wL[t % 3][:, :], w, wH[t % 3][:, :].bitcast(fp32), ALU.subtract).then_inc(s_lo, 1)
                    if t in FORM_AT:
                        g = FORM_AT[t]
                        dve.wait_ge(s_mus, i * G + g + 1)
                        dve.wait_ge(used, i * LS + SLABS + LOT_ORDER.index((1, g)) + 1)
                        if g >= 2:
                            dve.wait_ge(s_aT, i * G + g - 1)
                        tt(ac[g % 2], sg[g % 2], ps[2 + g % 2][:, 0:256].rearrange("p (m j) -> p m j", m=2),
                           ALU.mult).then_inc(s_mua, 1)
                    if t == LS - 1:
                        gathered(i + 1, 0)
                    if t in DOWN_AT:
                        g = DOWN_AT[t]
                        dve.wait_ge(s_aH, i * G + g + 1)
                        tt(aL[g % 2][:, :], ps[6][:, 0:256], aH[g % 2][:, :].bitcast(fp32),
                           ALU.subtract).then_inc(s_aL, 1)
                    if t in ADD_AT:
                        c = ADD_AT[t]
                        dve.wait_ge(s_sc, i * KC + c + 1)
                        tt(acc[:, c, :], acc[:, c, :], ps[7][:, 0:N], ALU.add).then_inc(s_scd, 1)
                    if t == GATES_AT + 3:
                        dve.wait_ge(s_gTp, i + 1)
                        V.tensor_copy(gatT, ps[7][:, 0:N]).then_inc(s_gT, 1)
                    if t in CHOOSE_AT:
                        step = CHOOSE_AT[t]
                        dve.wait_ge(c_lot, i * 2 + step) if step else dve.wait_ge(s_sel, i + 1)
                        choice(step).then_inc(c_lot if step < 2 else s_sel, 1)
                gathered(i + 1, 1)
            for c in range(KC):
                dve.wait_ge(s_sc, lots * KC + c + 1)
                tt(acc[:, c, :], acc[:, c, :], ps[6 + c % 2][:, 0:N], ALU.add).then_inc(s_scd, 1)
            dve.wait_ge(s_scd, lots * KC + KC + 1)
            for c in range(KC):
                residual_ins = residual(1, 1, c, acc[:, c, :])
                ch(residual_ins)
            dve.sem_inc(s_x, 1)
            dve.wait_ge(s_rs, 3 * L + 1)
            for c in range(KC):
                ins = stt(hT[:, c, :], xT[:, c, :], par[:, FG + c:FG + c + 1], rs[:, :], ALU.mult, ALU.mult)
            ins.then_inc(s_fin, 1)


ORDER = (3, 2, 0, 4, 1, 5)
ORDER_SLABS = tuple(2 * g + h for g in ORDER for h in range(2))
DOWN = ((0, 8), (8, 16), (16, 22))
PARAM_LOADS = 4 + 7 + 4 + 2
LN64 = 6 * 0.6931471805599453
MG = 24
MOD_DONE = (8, 32, 48)
FILL = ((4, (1,) * 9, (1,) * 8, 2, 1), (4, (1,) * 9, (0, 0, 0, 0, 0, 0, 0, 1), 1, 1))
assert all(a + sum(b) + sum(c) + d + e == MOD_DONE[l + 1] - MOD_DONE[l]
           for l, (a, b, c, d, e) in enumerate(FILL))
W_IN = (MOD_DONE[0], MOD_DONE[1] + 16 + 34)
W_OUT = tuple(W_IN[l] + 12 + MOD_DONE[l + 1] - MOD_DONE[l] for l in range(2))
FFN = W_OUT[0] + 4
FS = 2 * G + 4 * len(DOWN)
assert FFN + FS == W_IN[1]
FFN_SLOT = [((FFN + d) % R, (FFN + d) // R + 1, SLAB if d < 2 * G else
             256 * (DOWN[(d - 2 * G) % 3][1] - DOWN[(d - 2 * G) % 3][0])) for d in range(FS)]
MOD_SLAB = tuple(range(8)) + tuple(W_IN[l] + 12 + i for l in range(2) for i in range(MOD_DONE[l + 1] - MOD_DONE[l]))
SLABS = W_OUT[1] + 4


def _loads():
    n = [0] * R
    for pos in range(SLABS):
        n[pos % R] += 1
    return n


LOADS = _loads()
ROWS = (P, P, NS)
LOT_ORDER = tuple(x for g in range(G) for x in ([(0, g), (1, g)] + ([(2, g - 1)] if g else []))) + ((2, G - 1),)

FORM_AT = {LOT_ORDER.index((0, g + 1)) if g < G - 1 else 3 * G - 1: g for g in range(G)}
TURN_AT = {LOT_ORDER.index((0, g + 1)) if g < G - 1 else 3 * G - 2: g for g in range(G)}
SCATTER_AT = {4 + 2 * c: c for c in range(KC)}
ADD_AT = {t + 3: c for t, c in SCATTER_AT.items()}
CHOOSE_AT = {25 + k: k for k in range(3)}
GATES_AT = 22
DOWN_AT = {LOT_ORDER.index((2, g)): g for g in range(G)}

_INS = ["x_prompt", "x_sample", "c_prompt", "c_sample", "state_rglru_h", "state_rglru_conv", "state_hgrn",
        "mod_w", "mod_b", "norm1_g", "norm2_g", "w_in", "conv_w", "conv_b", "rg_wa", "rg_ba", "rg_wx", "rg_bx",
        "rg_lambda", "rg_out_g", "hg_lb_logits", "hg_norm_g", "w_out", "ffn_w1", "ffn_w3", "ffn_w2",
        "router_w", "moe_w1", "moe_w3", "moe_w2", "final_g"]
_OUTS = [("y_prompt", (1, T, D)), ("y_sample", (NS, 1, D)), ("new_h_prompt", (L, 1, WA)),
         ("new_conv_prompt", (L, 1, CW - 1, WA)), ("new_S_prompt", (L, 1, H, P, P)),
         ("new_h_sample", (L, NS, WA)), ("new_conv_sample", (L, NS, CW - 1, WA)),
         ("new_S_sample", (L, NS, H, P, P))]


def kernel(**inputs):
    import numpy as np
    import concourse.bacc as bacc
    from concourse.bass_utils import run_bass_kernel_spmd as run

    nc = bacc.Bacc("TRN2", target_bir_lowering=False, num_devices=1)
    arrays, ins, outs = {}, {}, {}
    for name in _INS:
        x = np.ascontiguousarray(inputs[name])
        arrays[f"in_{name}"] = x
        ins[name] = nc.dram_tensor(f"in_{name}", x.shape, mybir.dt.from_np(x.dtype), kind="ExternalInput").ap()
    for name, shape in _OUTS:
        outs[name] = nc.dram_tensor(f"out_{name}", shape, mybir.dt.float32, kind="ExternalOutput").ap()
    trunk(nc, ins, outs)
    r = run(nc, [arrays], core_ids=[0])
    return tuple(r.results[0][f"out_{name}"] for name, _ in _OUTS)
```

```python
import concourse.bass as bass
from concourse import mybir
from contextlib import ExitStack

D = 1024
T = 256
NS = 8
N = T + NS
P = 128
KC = D // P
L = 2
WA = 512
AC = WA // P
H = 4
U = 3072 // P
F = 2816
FC = F // P
NE = 8
CW = 4
EPS = 1e-6
COND = 1 + NS
LOT = 128
MAXLOTS = NE + 2 * N // (LOT + 1)
G = F // 256
R = 9
SLAB = 2048
LEVELS = 8


def trunk(nc, a, o):
    fp32 = mybir.dt.float32
    i32 = mybir.dt.int32
    u32 = mybir.dt.uint32
    ALU = mybir.AluOpType
    ACT = mybir.ActivationFunctionType
    AX = mybir.AxisListType

    ctx = ExitStack()
    with ctx:
        def sb(name, shape, dt=fp32):
            return ctx.enter_context(nc.sbuf_tensor(name, shape, dt))

        def sem(name):
            return ctx.enter_context(nc.semaphore(name))

        ring = sb("ring", [P, R, SLAB])
        xT = sb("xT", [P, KC, N])
        h_at = nc.sbuf_base
        hT = sb("hT", [P, KC, N])
        par = sb("par", [P, 5 * P])
        modT = sb("modT", [P, L, 6 * KC, COND])
        u_at = nc.sbuf_base
        uT = sb("uT", [P, U * N])
        mixed = nc.sbuf_base
        AT = sb("AT", [P, 2, H, P])
        ATx = sb("ATx", [P, H, P])
        vtok = sb("vtok", [P, 2, H, P])
        S = sb("S", [P, NS * H, P])
        oT = sb("oT", [P, H, N])
        bT = sb("bT", [P, H, T])
        y_at = nc.sbuf_base
        assert 4 * 3 * SLAB <= y_at - mixed - 4 * H * (N + T)
        yT = sb("yT", [P, KC, N])
        kept = nc.sbuf_base
        xaP = sb("xaP", [P, AC, CW - 1 + T])
        gw = sb("gw", [P, 2, AC, P])
        mixed_end = nc.sbuf_base
        short = nc.sbuf_base
        ar = sb("ar", [P, 7 * H * N])
        mask = sb("mask", [P, LEVELS, P], mybir.dt.uint8)
        ident = sb("ident", [P, P])
        ones = sb("ones", [P, P])
        mean = {w: sb(f"mean{w}", [P, P]) for w in (D, WA, P)}
        before = sb("before", [P, P])
        rtr = sb("rtr", [P, KC, NE])
        rs = sb("rs", [P, N])
        modA = sb("modA", [P, KC, COND])
        cond = sb("cond", [P, KC, COND])
        lb = sb("lb", [P, L, H])
        omlb = sb("omlb", [P, L, H])
        coef = sb("coef", [P, L, AC])
        sm = sb("sm", [P, 16, 16])
        iota = sb("iota", [P, P])
        outc = sb("outc", [P, 80])
        outr = [sb(f"outr{l}", [80, P]) for l in range(L)]
        eps = sb("eps", [P, 1])
        ridx = sb("ridx", [P, 3, NE], u32)
        gsl = sb("gsl", [P, 3, 2])
        wts = sb("wts", [P, 3, 2])
        tab = sb("tab", [P, 8], i32)
        f32r = mybir.dt.float32r

        def split_at(name, n, offset, words):
            return [[nc.alloc_sbuf_tensor_at(f"{name}_{part}{i}", [P, words], f32r,
                                             offset=offset + 4 * words * (2 * i + x))
                     for i in range(n)] for x, part in enumerate(("hi", "lo"))]

        assert 6 * 4 * SLAB <= mixed_end - mixed
        wH, wL = split_at("slab", 3, mixed, SLAB)
        (hH,), (hL,) = split_at("tokens", 1, short + 4 * 4608, 1024)
        aH, aL = split_at("act", 2, short, 256)
        yhH = nc.alloc_sbuf_tensor_at("h1_hi", [P, KC, N], f32r, offset=y_at)
        assert 4 * (4 * SLAB + KC * N) <= kept - mixed
        fhH, fhL, faH, faL = (nc.alloc_sbuf_tensor_at(name, [P, n, N], f32r, offset=at_) for name, n, at_ in (
            ("h_hi", KC, mixed + 16 * SLAB), ("h_lo", KC, h_at), ("ffn_act_hi", FC, u_at),
            ("ffn_act_lo", FC, short)))
        ps = [ctx.enter_context(nc.psum_tensor(f"ps{i}", [P, 512], fp32)) for i in range(8)]

        u = uT[:, :].rearrange("p (c n) -> p c n", n=N)
        XA, GA, QB, FB, IB, GB = (u[:, 4 * i:4 * i + 4, :] for i in range(6))
        prow = uT[:, 0:5 * P].rearrange("p (t c) -> p t c", c=P)
        xrow = uT[:, 1024:1024 + 3 * D].rearrange("p (t c) -> p t c", c=D)
        modrow = hT[0:COND, :, :].rearrange("p c n -> p (c n)")[:, 0:512].rearrange("p (i n) -> p i n", i=2)
        yrow = xrow
        h2tok = uT[:, 0:3 * D].rearrange("p (t c) -> p t c", c=D)
        acc = uT[:, 3 * D:3 * D + KC * N].rearrange("p (c n) -> p c n", n=N)
        rt = uT[:, 5184:5184 + 24 * 3 * NE].rearrange("p (n t e) -> p n t e", t=3, e=NE)
        W4 = H * N
        sqa = ar[:, 0:KC * N].rearrange("p (c n) -> p c n", n=N)
        squares = [yT, sqa, yT, sqa, yT]

        def lot(i):
            return ar[:, i * W4:(i + 1) * W4].rearrange("p (h n) -> p h n", n=N)

        xc, rg, ig, ag, mu, gt, g2 = (lot(i) for i in range(7))
        LD = [ar[:, 1024 * i:1024 * (i + 1)] for i in range(2)]
        LW = [ar[:, 2048 + 1024 * i:3072 + 1024 * i] for i in range(2)]
        keT = ar[:, 4096:5120].rearrange("p (t h d) -> p t h d", t=2, h=H)
        ke = ar[:, 5120:6144].rearrange("p (h t) -> p h t", h=H)
        vbk = ar[:, 6144:6656].rearrange("p (g e) -> p g e", e=P)
        hgH, hgL = (x[:, :].rearrange("p (c j) -> p c j", j=LOT) for x in (hH, hL))
        ytok = ar[:, 1024:2048]
        sg = [ar[:, 2048 + 256 * i:2304 + 256 * i].rearrange("p (m j) -> p m j", m=2) for i in range(2)]
        ac = [ar[:, 2560 + 256 * i:2816 + 256 * i].rearrange("p (m j) -> p m j", m=2) for i in range(2)]
        sel = ar[:, 3072:3456].rearrange("p (t j) -> p t j", j=LOT)
        gat = ar[:, 3456:3840].rearrange("p (t j) -> p t j", j=LOT)
        fs = modA[:, :, :].rearrange("p c b -> p (c b)")[:, 0:H * NS].rearrange("p (h b) -> p h b", h=H)
        gatT = ar[:, 3840:3840 + N]
        stmp = ar[:, 4224:4608].rearrange("p (t j) -> p t j", j=LOT)
        fsg, fac = ([ar[:, (FC + i + k) * N:(FC + i + k + 1) * N] for i in range(2)] for k in (0, 2))
        sfin = ar[:, 5120:5632]

        MODB, G1, G2 = 0, 96, 112
        CWW, CB, BA, BX, LAM, OG, LBL, HG, FG = 128, 160, 168, 176, 184, 192, 200, 208, 216
        CS, CP, SCV, SH = 256, 320, 384, 480

        class Stream:
            def __init__(self):
                self.pos = self.n = 0
                self.loads = [0] * R
                self.user = [None] * R

            def take(self):
                s = self.pos % R
                before_, self.user[s] = self.user[s], self.n
                self.pos += 1
                self.n += 1
                self.loads[s] += 1
                return s, self.loads[s], before_

            def align(self):
                self.pos += -self.pos % R

        IT = 4 * R
        LS = 3 * G

        def mod_rows(n):
            return ps[0 if n < MOD_DONE[0] and n % 2 else 7][0:COND, 0:256]

        def mod_columns(n, count=1):
            o_ = 2 * COND * (n - max(x for x in (0,) + MOD_DONE if x <= n))
            return ps[6][:, o_:o_ + 2 * COND * count].rearrange("p (c b) -> p c b", b=COND)

        full = [sem(f"slot_full{i}") for i in range(R)]
        used = sem("slab_used")
        s_row = sem("param_rows_loaded")
        s_crow = sem("condition_rows_loaded")
        s_cT = sem("condition_transposed")
        s_craw = sem("condition_columns")
        s_xrow = sem("x_rows_loaded")
        s_gw = sem("gate_weights_loaded")
        s_gwz = sem("gate_weights_cleared")
        s_S = sem("sample_state_loaded")
        s_cst = sem("constants_ready")
        s_parT = sem("param_transposed")
        s_par = sem("param_ready")
        s_xTp = sem("x_transposed")
        s_xT = sem("x_ready")
        s_act0 = sem("setup_act")
        s_dve0 = sem("setup_dve")
        s_cond = sem("cond_ready")
        s_mev = sem("mod_rows")
        s_mtr = sem("mod_transposed")
        s_mod = sem("mod_ready")
        s_sq = sem("squares_ready")
        s_ms = sem("mean_square_ready")
        s_rs = sem("rsqrt_ready")
        s_h = sem("h_ready")
        s_up = sem("u_psum")
        s_u = sem("u_evacuated")
        s_fe = sem("f_exp")
        s_f = sem("f_ready")
        s_lnf = sem("ln_f")
        s_tq = sem("tanh_q")
        s_xc = sem("conv_ready")
        s_gp = sem("gate_psum")
        s_tg = sem("gate_tanh")
        s_rdy = sem("r_ready")
        s_a = sem("a_ready")
        s_m2 = sem("mult_squared")
        s_mu = sem("mult_ready")
        s_gi = sem("gelu_inner")
        s_tge = sem("gelu_tanh")
        s_tgb = sem("tanh_gb")
        s_zs = sem("z_squared")
        s_b = sem("b_ready")
        s_ld = sem("level_diff")
        s_le = sem("level_exp")
        s_lw = sem("level_operand")
        s_lp = sem("level_psum")
        s_lc = sem("level_copied")
        s_vp = sem("v_transposed")
        s_v = sem("vtok_ready")
        s_kx = sem("ke_exp")
        s_ke = sem("ke_ready")
        s_kp = sem("ke_transposed")
        s_keT = sem("keT_ready")
        s_sf = sem("final_state_psum")
        s_sfs = sem("final_state_ready")
        s_op = sem("o_psum")
        s_vb = sem("v_broadcast")
        s_vbd = sem("v_broadcast_used")
        s_S1 = sem("decayed_state")
        s_osp = sem("o_sample_psum")
        s_os = sem("o_squared")
        s_oms = sem("o_mean_square")
        s_ors = sem("o_rsqrt")
        s_y = sem("y_ready")
        s_wp = sem("w_out_psum")
        s_x1 = sem("residual_chunk")
        s_x = sem("x_updated")
        s_oc = sem("vector_outputs")
        s_ocp = sem("vector_outputs_transposed")
        s_or = sem("vector_output_rows")
        s_whH = sem("h1_hi")
        s_whL = sem("h1_lo")
        s_wiH = sem("w_in_slab_hi")
        s_wiL = sem("w_in_half_lo")
        s_wiu = sem("w_in_half_lo_used")
        s_fhH = sem("h_hi")
        s_fhL = sem("h_lo")
        s_fwH = sem("ffn_slab_hi")
        s_fwL = sem("ffn_slab_lo")
        s_fs = sem("ffn_silu")
        s_fa = sem("ffn_act")
        s_faH = sem("ffn_act_hi")
        s_faL = sem("ffn_act_lo")
        s_fx = sem("ffn_down_used")
        s_lg = sem("logits_psum")
        s_htp = sem("h2_transposed")
        s_htk = sem("h2tok_ready")
        s_red = sem("router_exp_in")
        s_re = sem("router_exp")
        s_msk = sem("choice_mask")
        s_rk = sem("ranks_psum")
        s_tab = sem("lot_table")
        s_sel = sem("lot_choice")
        s_gth = sem("gather_psum")
        s_hgH = sem("gathered_hi")
        s_hgL = sem("gathered_lo")
        s_hi = sem("slab_hi")
        s_lo = sem("slab_lo")
        s_aT = sem("moe_act_transposed")
        s_aH = sem("moe_act_hi")
        s_aL = sem("moe_act_lo")
        s_gTp = sem("gate_transposed")
        s_gT = sem("gateT_ready")
        s_mus = sem("moe_silu")
        s_mua = sem("moe_act")
        s_yt = sem("moe_y_ready")
        s_sc = sem("scatter_psum")
        s_scd = sem("scatter_added")
        s_rtr = sem("router_loaded")
        s_fin = sem("final_x")
        s_ft = sem("final_transposed")
        s_fr = sem("final_rows")
        s_out = sem("outputs_stored")
        s_st = sem("states_stored")
        c_dve = sem("dve_chain")
        c_lot = sem("choice_step")
        c_act = sem("act_chain")
        c_pool = sem("pool_chain")
        outs = [0]

        class Chain:
            def __init__(self, eng, s, base=0):
                self.eng, self.s, self.n, self.base = eng, s, 0, base

            def __call__(self, ins):
                self.n += 1
                ins.then_inc(self.s, 1)
                self.eng.wait_ge(self.s, self.base + self.n)

        def wide(x, n):
            return x.unsqueeze(len(x.shape)).broadcast_to(list(x.shape) + [n])

        def slots(eng, i):
            def at(t):
                s = t % R
                per = len(range(s, LS, R))
                eng.wait_ge(full[s], i * (16 * per) + 16 * (LOADS[s] + t // R + 1))
                return ring[:, s, :]
            return at

        block = ctx.enter_context(nc.Block())

        @block.sync
        def _(sp):
            st = Stream()

            def load(src, base_used=None):
                s, n, prev = st.take()
                if prev is not None:
                    sp.wait_ge(used, prev + 1)
                w = src.shape[1] * src.shape[2]
                dst = ring[:, s, 0:w].rearrange("p (k n) -> p k n", k=src.shape[1])
                sp.dma_start(dst, src).then_inc(full[s], 16)

            def projections(n0, n1):
                for n in range(n0, n1):
                    l, g = divmod(n, MG)
                    load(a["mod_w"][l].rearrange("(k p) n -> p k n", p=P)[:, :, g * 256:(g + 1) * 256])

            projections(0, 2)
            for tile, r0, src, n in (
                    (0, 0, a["mod_b"], 96), (0, 96, a["norm1_g"], 16), (0, 112, a["norm2_g"], 16),
                    (1, 0, a["conv_w"].rearrange("l j n -> (l j) n"), 32), (1, 32, a["conv_b"], 8),
                    (1, 40, a["rg_ba"], 8), (1, 48, a["rg_bx"], 8), (1, 56, a["rg_lambda"], 8),
                    (1, 64, a["rg_out_g"], 8), (1, 72, a["hg_lb_logits"], 8), (1, 80, a["hg_norm_g"], 8)):
                sp.dma_start(prow[r0:r0 + n, tile, :], src.rearrange("l (c p) -> (l c) p", p=P)).then_inc(s_row, 16)
            sp.dma_start(prow[88:96, 1, :], a["final_g"].rearrange("(c p) -> c p", p=P)).then_inc(s_row, 16)
            for l in range(L):
                sp.dma_start(prow[0:96, 3 + l, :], a["state_rglru_conv"][l].rearrange("b j (c p) -> (b j c) p", p=P))\
                    .then_inc(s_row, 16)
                sp.dma_start(prow[96:P, 3 + l, :], a["state_rglru_h"][l].rearrange("b (c p) -> (b c) p", p=P))\
                    .then_inc(s_row, 16)
            sp.dma_start(xrow[:, 0:2, :], a["x_prompt"][0].rearrange("(t p) c -> p t c", p=P)).then_inc(s_xrow, 16)
            sp.dma_start(xrow[0:NS, 2, :], a["x_sample"].rearrange("b t c -> (b t) c")).then_inc(s_xrow, 16)
            projections(2, MOD_DONE[0])
            for l in range(L):
                for g in ORDER_SLABS:
                    load(a["w_in"][l].rearrange("(k p) n -> p k n", p=P)[:, :, g * 256:(g + 1) * 256])
                projections(MOD_DONE[l], MOD_DONE[l + 1])
                for g in range(4):
                    load(a["w_out"][l].rearrange("(k p) n -> p k n", p=P)[:, :, g * 256:(g + 1) * 256])
                if l == 0:
                    for g in range(G):
                        for w in ("ffn_w1", "ffn_w3"):
                            load(a[w][0].rearrange("(k p) n -> p k n", p=P)[:, :, g * 256:(g + 1) * 256])
                    for q in range(4):
                        for k0, k1 in DOWN:
                            load(a["ffn_w2"][0].rearrange("(k p) n -> p k n", p=P)
                                 [:, k0:k1, q * 256:(q + 1) * 256])
            projections(MOD_DONE[2], MOD_DONE[3])
            st.align()
            held = dict(enumerate(st.user))
            w1 = a["moe_w1"][0].rearrange("e (k p) n -> p e k n", p=P)
            w3 = a["moe_w3"][0].rearrange("e (k p) n -> p e k n", p=P)
            w2 = a["moe_w2"][0].rearrange("e (k p) n -> p e k n", p=P)

            def lot_slabs(e, i, first_lot):
                last = [None] * R
                for t in range(LS):
                    last[t % R] = t
                cur = list(last)
                new = [False] * R
                for t, (kind, g) in enumerate(LOT_ORDER):
                    s = t % R
                    if new[s]:
                        sp.wait_ge(s_lo, i * LS + cur[s] + 1)
                    elif first_lot:
                        sp.wait_ge(used, held[s] + 1)
                    else:
                        sp.wait_ge(s_lo, i * LS - LS + cur[s] + 1)
                    cur[s], new[s] = t, True
                    if kind == 2:
                        src = w2[:, bass.ds(e, 1), 2 * g:2 * g + 2, :].rearrange("p e k n -> p (e k) n")
                        dst = ring[:, s, :].rearrange("p (k n) -> p k n", k=2)
                    else:
                        src = (w1, w3)[kind][:, bass.ds(e, 1), :, g * 256:(g + 1) * 256]\
                            .rearrange("p e k n -> p (e k) n")
                        dst = ring[:, s, :].rearrange("p (k n) -> p k n", k=KC)
                    sp.dma_start(dst, src).then_inc(full[s], 16)

            lot_slabs(0, 0, True)
            with sp.Fori(1, NE) as i:
                lot_slabs(i, i, False)
            sp.wait_ge(s_tab, 1)
            lots = sp.value_load(tab[0:1, 0:1], min_val=NE, max_val=MAXLOTS)
            with sp.If(lots > NE):
                with sp.Fori(NE, lots) as i:
                    e = sp.value_load(tab[0:1, bass.ds(i - (NE - 1), 1)], min_val=0, max_val=NE - 1)
                    lot_slabs(e, i, False)

        @block.gpsimd
        def _(pool):
            ch = Chain(pool, c_pool)
            g = nc.gpsimd
            g.memset(gw[:], 0.0).then_inc(s_gwz, 1)
            ch(g.memset(ident[:], 0.0))
            ch(g.affine_select(out=ident[:], in_=ident[:], compare_op=ALU.not_equal, fill=1.0, base=0,
                               pattern=[[-1, P]], channel_multiplier=1))
            ch(g.memset(before[:], 1.0))
            ch(g.affine_select(out=before[:], in_=before[:], compare_op=ALU.is_gt, fill=0.0, base=0,
                               pattern=[[1, P]], channel_multiplier=-1))
            ch(g.memset(ones[:], 1.0))
            for w in (D, WA, P):
                ch(g.memset(mean[w][:], 1.0 / w))
            ch(g.memset(eps[:], EPS))
            ch(g.iota(iota[:], pattern=[[1, P]], base=0, channel_multiplier=0,
                      allow_small_or_imprecise_dtypes=True))
            ch(g.iota(ar[:, 0:P].bitcast(i32), pattern=[[1, P]], base=0, channel_multiplier=0))
            ch(g.iota(ar[:, P:2 * P].bitcast(i32), pattern=[[0, P]], base=0, channel_multiplier=1))
            g.memset(xaP[:, :, 0:CW - 1], 0.0).then_inc(s_cst, 1)

            for l in range(L):
                if l:
                    pool.wait_ge(used, FFN + FS)
                for t in range(12):
                    s_ = (W_IN[l] + t) % R
                    pool.wait_ge(s_wiH, 12 * l + t + 1)
                    for m in range(2):
                        if t:
                            pool.wait_ge(s_wiu, 24 * l + 2 * t + m - 1)
                        lo, x, hi = (y.rearrange("p (k n) -> p k n", k=KC)[:, :, m * P:(m + 1) * P]
                                     for y in (wL[0][:, :], ring[:, s_, :], wH[t % 2][:, :].bitcast(fp32)))
                        g.tensor_tensor(out=lo, in0=x, in1=hi, op=ALU.subtract).then_inc(s_wiL, 1)
                pool.wait_ge(s_S, 16 * (l + 1))
                pool.wait_ge(s_f, l + 1)
                fb = fs.rearrange("p h b -> p b h")
                for b in range(NS):
                    ins = g.tensor_tensor(out=S[:, b * H:(b + 1) * H, :], in0=S[:, b * H:(b + 1) * H, :],
                                          in1=wide(fb[:, b, :], P), op=ALU.mult)
                ins.then_inc(s_S1, 1)

        @block.tensor
        def _(pe):
            st = Stream()
            mm = nc.tensor.matmul

            def slab():
                s, n, _ = st.take()
                pe.wait_ge(full[s], 16 * n)
                return ring[:, s, :]

            pe.wait_ge(s_cst, 1)
            pe.wait_ge(s_crow, 16 * 2)
            nc.tensor.transpose(ps[0][:, 0:64 + KC], prow[0:64 + KC, 2, :], ident[0:64 + KC, 0:64 + KC])\
                .then_inc(s_cT, 1)
            pe.wait_ge(s_cond, 1)
            mods = [0, 0]

            def turn_rows():
                n = mods[1]
                pe.wait_ge(s_mev, n + 1)
                if n in MOD_DONE:
                    pe.wait_ge(s_mod, MOD_DONE.index(n) + 1)
                for c in range(2):
                    last = nc.tensor.transpose(mod_columns(n)[:, c, :], modrow[:, n % 2, c * P:(c + 1) * P],
                                               ident[0:COND, 0:COND])
                last.then_inc(s_mtr, 1)
                mods[1] += 1

            def project(count):
                for _ in range(count):
                    n = mods[0]
                    w = slab()[:, 0:2048].rearrange("p (k n) -> p k n", k=KC)
                    ahead = 2 if n < MOD_DONE[0] else 1
                    if n >= ahead:
                        pe.wait_ge(s_mev, n + 1 - ahead)
                    for k in range(KC):
                        last = mm(mod_rows(n), cond[:, k, :], w[:, k, :], start=(k == 0), stop=(k == KC - 1))
                    last.then_inc(used, 1)
                    mods[0] += 1
                    if mods[1] < n:
                        turn_rows()

            project(2)
            pe.wait_ge(s_row, 16 * PARAM_LOADS)
            for t, (tile, rows) in enumerate(((0, P), (1, 96), (3, P), (4, P))):
                last = nc.tensor.transpose(ps[1][:, t * P:t * P + rows], prow[0:rows, tile, :],
                                           ident[0:rows, 0:rows])
            last.then_inc(s_parT, 1)
            pe.wait_ge(s_xrow, 16 * 2)
            for c in range(KC):
                b = ps[2 + c % 4]
                if c >= 4:
                    pe.wait_ge(s_xT, c - 3)
                for t in range(2):
                    nc.tensor.transpose(b[:, t * P:(t + 1) * P], xrow[:, t, c * P:(c + 1) * P], ident[:])
                nc.tensor.transpose(b[:, T:N], xrow[0:NS, 2, c * P:(c + 1) * P], ident[0:NS, 0:NS])\
                    .then_inc(s_xTp, 1)
            project(2)

            def mean_square(n, chunks):
                for c in chunks:
                    pe.wait_ge(s_sq, KC * n + c + 1)
                    last = mm(ps[NORM_BANK[n]][:, 0:N], mean[D][:], squares[n][:, c, :],
                              start=(c == 0), stop=(c == KC - 1))
                if c == KC - 1:
                    last.then_inc(s_ms, 1)

            mean_square(0, range(KC))
            project(MOD_DONE[0] - 4)
            turn_rows()

            def layer(l):
                j = 0
                for grp in ORDER:
                    for half in range(2):
                        slab()
                        w, wl = (x[:, :].rearrange("p (k n) -> p k n", k=KC) for x in (wH[j // 2 % 2], wL[0]))
                        for m in range(2):
                            if j >= 4:
                                pe.wait_ge(s_u, U * l + j - 3)
                            pe.wait_ge(s_wiL, U * l + j + 1)
                            ms = slice(m * P, (m + 1) * P)
                            bank = ps[j % 4][:, 0:N]
                            for k in range(KC):
                                if j == 0 and k % 2 == 0:
                                    pe.wait_ge(s_whL, 4 * l + k // 2 + 1)
                                last = mm(bank, wl[:, k, ms], yhH[:, k, :], start=(k == 0), stop=False)
                            last.then_inc(s_wiu, 1)
                            for k in range(KC):
                                mm(bank, w[:, k, ms], fhL[:, k, :], start=False, stop=False)
                                last = mm(bank, w[:, k, ms], yhH[:, k, :], start=False, stop=(k == KC - 1))
                            if m == 0:
                                last.then_inc(s_up, 1)
                            j += 1
                        last.then_inc(used, 1)
                    if grp == 4:
                        pe.wait_ge(s_xc, l + 1)
                        pe.wait_ge(s_gw, 64 * (l + 1))
                        for c in range(AC):
                            for w in range(2):
                                b = 4 + w
                                if c:
                                    pe.wait_ge(s_tg, 8 * l + 2 * c + w - 1)
                                mm(ps[b][:, 0:N], gw[:, w, c, :], xc[:, c, :], start=True, stop=True)\
                                    .then_inc(s_gp, 1)
                pe.wait_ge(s_u, U * (l + 1))
                for t in range(2):
                    for h in range(H):
                        last = nc.tensor.transpose(ps[t][:, h * P:(h + 1) * P],
                                                   IB[:, h, t * P:(t + 1) * P], ident[:])
                last.then_inc(s_vp, 1)
                project(FILL[l][0])
                pe.wait_ge(s_zs, l + 1)
                for c in range(AC):
                    last = mm(ps[4][:, 0:N], mean[WA][:], g2[:, c, :], start=(c == 0), stop=(c == AC - 1))
                last.then_inc(s_ms, 1)
                pe.wait_ge(s_v, l + 1)
                for v in range(LEVELS + 1):
                    pe.wait_ge(s_lw, (LEVELS + 1) * l + v + 1)
                    if v >= 2:
                        pe.wait_ge(s_lc, (LEVELS + 1) * l + v - 1)
                    lw = LW[v % 2].rearrange("p (h t) -> p h t", h=H)
                    if v == LEVELS:
                        for h in range(H):
                            last = mm(ps[2 * (v % 2)][:, h * P:(h + 1) * P], lw[:, h, 0:P], lw[:, h, P:T],
                                      start=True, stop=True)
                    else:
                        for t in range(2):
                            for h in range(H):
                                kk = lw[:, h, t * P:(t + 1) * P] if v else FB[:, h, t * P:(t + 1) * P]
                                qq = lw[:, h, t * P:(t + 1) * P] if v else QB[:, h, t * P:(t + 1) * P]
                                last = mm(ps[2 * (v % 2) + t][:, h * P:(h + 1) * P], kk, qq,
                                          start=True, stop=True)
                    last.then_inc(s_lp, 1)
                    project(FILL[l][1][v])
                pe.wait_ge(s_ke, l + 1)
                pe.wait_ge(s_rs, 3 * l + 2)
                for t in range(2):
                    for h in range(H):
                        last = nc.tensor.transpose(ps[4 + t][:, h * P:(h + 1) * P], ke[:, h, t * P:(t + 1) * P],
                                                   ident[:])
                last.then_inc(s_kp, 1)
                pe.wait_ge(s_lc, (LEVELS + 1) * (l + 1))
                for h in range(H):
                    b = ps[h // 2]
                    w = h % 2 * T
                    mm(b[:, w:w + P], vtok[:, 0, h, :], AT[:, 0, h, :], start=True, stop=True)
                    mm(b[:, w + P:w + T], vtok[:, 0, h, :], ATx[:, h, :], start=True, stop=False)
                    last = mm(b[:, w + P:w + T], vtok[:, 1, h, :], AT[:, 1, h, :], start=False, stop=True)
                last.then_inc(s_op, 1)
                pe.wait_ge(s_keT, l + 1)
                for h in range(H):
                    for t in range(2):
                        last = mm(ps[5][:, h * P:(h + 1) * P], keT[:, t, h, :], vtok[:, t, h, :],
                                  start=(t == 0), stop=(t == 1))
                last.then_inc(s_sf, 1)
                pe.wait_ge(s_keT, l + 1)
                for b in range(NS + 2):
                    if b >= 2:
                        pe.wait_ge(s_vbd, NS * l + b - 1)
                    if b < NS:
                        for h in range(H):
                            last = mm(ps[2 + b % 2][:, h * P:(h + 1) * P],
                                      IB[:, h, T + b:T + b + 1].broadcast_to([P, P]), ident[:],
                                      start=True, stop=True)
                        last.then_inc(s_vb, 1)
                        project(FILL[l][2][b])
                    if b >= 2:
                        for h in range(H):
                            c = h * NS + b - 2
                            last = mm(ps[4][:, c:c + 1], S[:, (b - 2) * H + h, :],
                                      QB[:, h, T + b - 2:T + b - 1], start=True, stop=True)
                last.then_inc(s_osp, 1)
                project(FILL[l][3])
                pe.wait_ge(s_os, l + 1)
                for h in range(H):
                    last = mm(ps[h][:, 0:N], mean[P][:], yT[:, AC + h, :], start=True, stop=True)
                last.then_inc(s_oms, 1)
                project(FILL[l][4])
                turn_rows()
                assert mods[1] == MOD_DONE[l + 1]
                pe.wait_ge(s_oc, l + 1)
                nc.tensor.transpose(ps[4][0:80, 0:P], outc[:, :], ident[:]).then_inc(s_ocp, 1)
                pe.wait_ge(s_y, l + 1)
                for g in range(4):
                    w = slab()[:, 0:2048].rearrange("p (k n) -> p k n", k=KC)
                    for m in range(2):
                        c = 2 * g + m
                        if c >= 4:
                            pe.wait_ge(s_x1, KC * l + c - 3)
                        for k in range(KC):
                            last = mm(ps[c % 4][:, 0:N], w[:, k, m * P:(m + 1) * P], yT[:, k, :],
                                      start=(k == 0), stop=(k == KC - 1))
                        if m == 0:
                            last.then_inc(s_wp, 1)
                    last.then_inc(used, 1)
                    if g:
                        mean_square(2 * l + 1, (2 * g - 2, 2 * g - 1))
                mean_square(2 * l + 1, range(6, KC))
                if l:
                    pe.wait_ge(s_h, 2 * KC * (l + 1))

            def products(out, x, xl, w, wl, start, stop):
                mm(out, x, w, start=start, stop=False)
                mm(out, x, wl, start=False, stop=False)
                return mm(out, xl, w, start=False, stop=stop)

            def dense():
                for d in range(FS):
                    slab()
                    pe.wait_ge(s_fwL, d + 1)
                    if d < 2 * G:
                        g, x = divmod(d, 2)
                        if x == 0 and g >= 2:
                            pe.wait_ge(s_fa, 2 * g - 2)
                        w, wl = (y[d % 2][:, :].rearrange("p (k n) -> p k n", k=KC) for y in (wH, wL))
                        for m in range(2):
                            ms = slice(m * P, (m + 1) * P)
                            for k in range(KC):
                                if d == 0 and m == 0 and k % 2 == 0:
                                    pe.wait_ge(s_fhL, k // 2 + 1)
                                last = products(ps[g % 2 * 4 + x * 2 + m][:, 0:N], w[:, k, ms], wl[:, k, ms],
                                                fhH[:, k, :], fhL[:, k, :], k == 0, k == KC - 1)
                    else:
                        q, i = divmod(d - 2 * G, 3)
                        k0, k1 = DOWN[i]
                        if i == 0:
                            if q < 2:
                                pe.wait_ge(s_fa, FC - 2 + 2 * q)
                            else:
                                pe.wait_ge(s_fx, 2 * q - 2)
                        pe.wait_ge(s_faL, k1)
                        w, wl = (y[d % 2][:, 0:(k1 - k0) * 256].rearrange("p (k n) -> p k n", k=k1 - k0)
                                 for y in (wH, wL))
                        for m in range(2):
                            ms = slice(m * P, (m + 1) * P)
                            for k in range(k0, k1):
                                last = products(ps[(q + 1) % 2 * 4 + m][:, 0:N], w[:, k - k0, ms],
                                                wl[:, k - k0, ms], faH[:, k, :], faL[:, k, :],
                                                k == 0, k == FC - 1)
                    last.then_inc(used, 1)
                    if d > 2 * G + 2 and (d - 2 * G) % 3 == 2:
                        mean_square(2, (2 * q - 2, 2 * q - 1))
                mean_square(2, range(6, KC))

            def route():
                rows = (P, P, NS)
                pe.wait_ge(s_rtr, 16)
                for t in range(3):
                    for k in range(KC):
                        last = mm(ps[1][0:rows[t], t * NE:(t + 1) * NE], hT[:, k, t * P:t * P + rows[t]],
                                  rtr[:, k, :], start=(k == 0), stop=(k == KC - 1))
                last.then_inc(s_lg, 1)
                for t in range(3):
                    for q in range(2):
                        n = 2 * t + q
                        if n >= 2:
                            pe.wait_ge(s_htk, n - 1)
                        for c in range(4):
                            last = nc.tensor.transpose(ps[2 + n % 2][0:rows[t], c * P:(c + 1) * P],
                                                       hT[:, 4 * q + c, t * P:t * P + rows[t]], ident[:])
                        last.then_inc(s_htp, 1)
                pe.wait_ge(s_msk, 1)
                m = rt[:, 2]
                for t in range(3):
                    o_ = ps[0][0:rows[t], t * NE:(t + 1) * NE]
                    for s in range(t):
                        mm(o_, ones[:, 0:rows[t]], m[:, s, :], start=(s == 0), stop=False)
                    mm(o_, before[0:rows[t], 0:rows[t]], m[0:rows[t], t, :], start=(t == 0), stop=True)
                for t in range(3):
                    last = mm(ps[0][:, 3 * NE:4 * NE], ones[0:rows[t], :], m[0:rows[t], t, :],
                              start=(t == 0), stop=(t == 2))
                last.then_inc(s_rk, 1)
                project(MOD_LAST)
                turn_rows()

            def gather(n, q):
                pe.wait_ge(s_sel, n + 1)
                for c in range(4 * q, 4 * q + 4):
                    for t in range(3):
                        last = mm(ps[7][:, c % 4 * P:c % 4 * P + P],
                                  h2tok[0:ROWS[t], t, c * P:(c + 1) * P], sel[0:ROWS[t], t, :],
                                  start=(t == 0), stop=(t == 2))
                last.then_inc(s_gth, 1)

            def turn_gates():
                for t in range(3):
                    last = nc.tensor.transpose(ps[7][:, t * P:t * P + ROWS[t]], gat[0:ROWS[t], t, :],
                                               ident[0:ROWS[t], 0:ROWS[t]])
                last.then_inc(s_gTp, 1)

            def moe():
                pe.wait_ge(s_htk, 6)
                gather(0, 0)
                pe.wait_ge(s_hgL, 1)
                gather(0, 1)
                pe.wait_ge(s_tab, 1)
                lots = pe.value_load(tab[0:1, 0:1], min_val=NE, max_val=MAXLOTS)
                with pe.Fori(0, lots) as i:
                    pe.wait_ge(s_hgL, i * 2 + 2)
                    for t, (kind, g) in enumerate(LOT_ORDER):
                        b = t % 3
                        pe.wait_ge(s_lo, i * LS + t + 1)
                        if kind < 2:
                            if g >= 2:
                                pe.wait_ge(s_mua, i * G + g - 1)
                            h_, l_ = (x[b][:, :].rearrange("p (k n) -> p k n", k=KC) for x in (wH, wL))
                            for k in range(KC):
                                last = products(ps[2 * kind + g % 2][:, 0:256], hgH[:, k, :], hgL[:, k, :],
                                                h_[:, k, :], l_[:, k, :], k == 0, k == KC - 1)
                        else:
                            if g == 0:
                                pe.wait_ge(s_yt, i * 2 + 2)
                            pe.wait_ge(s_aL, i * G + g + 1)
                            h_, l_ = (x[b][:, :].rearrange("p (k n) -> p k n", k=2) for x in (wH, wL))
                            for m in range(2):
                                js = slice(m * LOT, (m + 1) * LOT)
                                for n in range(2):
                                    cs = slice(n * 512, (n + 1) * 512)
                                    last = products(ps[4 + n][:, :], aH[g % 2][:, js], aL[g % 2][:, js],
                                                    h_[:, m, cs], l_[:, m, cs],
                                                    g == 0 and m == 0, g == G - 1 and m == 1)
                        last.then_inc(used, 1)
                        if t in TURN_AT:
                            g = TURN_AT[t]
                            pe.wait_ge(s_mua, i * G + g + 1)
                            for m in range(2):
                                last = nc.tensor.transpose(ps[6][:, m * P:(m + 1) * P], ac[g % 2][:, m, :],
                                                           ident[:])
                            last.then_inc(s_aT, 1)
                        if t in SCATTER_AT:
                            c = SCATTER_AT[t]
                            pe.wait_ge(s_gT, i + 1)
                            pe.wait_ge(s_scd, i * KC + c + 1)
                            mm(ps[7][:, 0:N], ytok[:, c * P:(c + 1) * P], gatT, start=True, stop=True)\
                                .then_inc(s_sc, 1)
                        if t == GATES_AT:
                            pe.wait_ge(s_scd, i * KC + KC + 1)
                            turn_gates()
                        if t == LS - 3:
                            pe.wait_ge(s_gT, i + 2)
                            gather(i + 1, 0)
                        if t == LS - 2:
                            pe.wait_ge(s_hgL, i * 2 + 3)
                            gather(i + 1, 1)
                pe.wait_ge(s_yt, lots * 2 + 2)
                pe.wait_ge(s_hgL, lots * 2 + 2)
                for c in range(KC):
                    if c >= 2:
                        pe.wait_ge(s_scd, lots * KC + c)
                    mm(ps[6 + c % 2][:, 0:N], ytok[:, c * P:(c + 1) * P], gatT, start=True, stop=True)\
                        .then_inc(s_sc, 1)
                    if c >= 3:
                        mean_square(2 * L, (c - 3,))
                mean_square(2 * L, range(KC - 3, KC))

            layer(0)
            dense()
            layer(1)
            route()
            st.align()
            assert st.n == SLABS
            moe()
            for n in range(6):
                q, t = divmod(n, 3)
                if n >= 2:
                    pe.wait_ge(s_fr, n - 1)
                for c in range(4 * q, 4 * q + 4):
                    if t == 0:
                        pe.wait_ge(s_fin, c + 1)
                    last = nc.tensor.transpose(ps[2 + n % 2][0:ROWS[t], c % 4 * P:(c % 4 + 1) * P],
                                               hT[:, c, t * P:t * P + ROWS[t]], ident[:])
                last.then_inc(s_ft, 1)

        @block.scalar
        def _(act_):
            A = nc.scalar.activation
            ch = Chain(act_, c_act)

            for r0, src, n in ((0, a["c_sample"], 64), (64, a["c_prompt"], KC)):
                act_.dma_start(prow[r0:r0 + n, 2, :], src.rearrange("b (c p) -> (b c) p", p=P)).then_inc(s_crow, 16)
            act_.wait_ge(s_cT, 1)
            A(par[:, CS:CS + 64 + KC], ps[0][:, 0:64 + KC], ACT.Copy).then_inc(s_craw, 1)
            act_.wait_ge(s_craw, 1)
            A(cond[:, :, 0], par[:, CP:CP + KC], ACT.Tanh, scale=0.5)
            A(cond[:, :, 1:COND], par[:, CS:CS + 64].rearrange("p (b c) -> p c b", c=KC), ACT.Tanh, scale=0.5)\
                .then_inc(s_act0, 1)
            act_.dma_start(rtr[:, :, :], a["router_w"][0].rearrange("(k p) e -> p k e", p=P)).then_inc(s_rtr, 16)
            for l in range(L):
                act_.dma_start(o["new_conv_sample"][l, :, 0:2, :], a["state_rglru_conv"][l, :, 1:3, :])\
                    .then_inc(s_out, 16)
                outs[0] += 1
            act_.wait_ge(s_gwz, 1)

            def gate_weights(l):
                for x, name in enumerate(("rg_wa", "rg_wx")):
                    for half in range(2):
                        src = a[name][l].rearrange("(c two) i j -> two i c j", two=2)[half]
                        act_.dma_start(gw[64 * half:64 * half + 64, x, :, 64 * half:64 * half + 64], src)\
                            .then_inc(s_gw, 16)

            gate_weights(0)
            def rsqrt(out, in_):
                ch(A(out, in_, ACT.Ln, bias=eps[:, 0:1]))
                return A(out, out, ACT.Exp, scale=-0.5)

            rowed = [0]

            def mod_row(count):
                for n in range(rowed[0], rowed[0] + count):
                    act_.wait_ge(used, MOD_SLAB[n] + 1)
                    A(modrow[:, n % 2, :], mod_rows(n), ACT.Copy).then_inc(s_mev, 1)
                rowed[0] += count

            mod_row(2)
            act_.wait_ge(s_parT, 1)
            ch(A(par[:, 0:224], ps[1][:, 0:224], ACT.Copy))
            A(par[:, 384:640], ps[1][:, 256:512], ACT.Copy).then_inc(s_par, 1)
            for c in range(KC):
                act_.wait_ge(s_xTp, c + 1)
                A(xT[:, c, :], ps[2 + c % 4][:, 0:N], ACT.Copy).then_inc(s_xT, 1)
            act_.wait_ge(s_dve0, 1)
            A(sm[:, 1, 0:8], sm[:, 0, 0:8], ACT.Exp, scale=-1.0)
            A(sm[:, 3, 0:8], sm[:, 2, 0:8], ACT.Exp).then_inc(s_act0, 1)

            act_.wait_ge(s_xT, KC)
            for c in range(KC):
                A(squares[0][:, c, :], xT[:, c, :], ACT.Square).then_inc(s_sq, 1)
            mod_row(2)
            act_.wait_ge(s_ms, 1)
            rsqrt(rs[:, :], ps[NORM_BANK[0]][:, 0:N]).then_inc(s_rs, 1)
            mod_row(MOD_DONE[0] - 4)

            def square(n, c):
                A(squares[n][:, c, :], xT[:, c, :], ACT.Square).then_inc(s_sq, 1)

            def layer(l):
                if l:
                    act_.wait_ge(s_ms, 3 * l + 1)
                    rsqrt(rs[:, :], ps[NORM_BANK[2 * l]][:, 0:N]).then_inc(s_rs, 1)

                def in_slab(t):
                    n = W_IN[l] + t
                    act_.wait_ge(full[n % R], 16 * (n // R + 1))
                    if t >= 2:
                        act_.wait_ge(used, n - 1)
                    A(wH[t % 2][:, :], ring[:, n % R, :], ACT.Copy).then_inc(s_wiH, 1)

                if l:
                    act_.wait_ge(used, FFN + FS)
                in_slab(0)
                for i in range(4):
                    act_.wait_ge(s_h, 2 * KC * l + 2 * i + 2)
                    c = slice(2 * i, 2 * i + 2)
                    A(yhH[:, c, :], hT[:, c, :], ACT.Copy).then_inc(s_whH, 1)
                in_slab(1)
                j = 0
                for grp in ORDER:
                    for m in range(4):
                        if m % 2 == 0:
                            act_.wait_ge(s_up, (U // 2) * l + j // 2 + 1)
                        else:
                            act_.wait_ge(used, W_IN[l] + j // 2 + 1)
                        dst = xaP[:, m, CW - 1:] if grp == 0 else u[:, 4 * grp + m, :]
                        if grp == 0:
                            ch(A(u[:, m, T:N], ps[j % 4][:, T:N], ACT.Copy))
                            A(dst, ps[j % 4][:, 0:T], ACT.Copy).then_inc(s_u, 1)
                        else:
                            A(dst, ps[j % 4][:, 0:N], ACT.Copy).then_inc(s_u, 1)
                        j += 1
                        if j % 2 == 0 and j // 2 + 1 < 12:
                            in_slab(j // 2 + 1)
                    if grp == 3:
                        act_.wait_ge(s_u, U * l + j)
                        A(FB, FB, ACT.Exp, scale=-1.0).then_inc(s_fe, 1)
                    if grp == 2:
                        act_.wait_ge(s_f, l + 1)
                        A(oT[:, :, 0:T], oT[:, :, 0:T], ACT.Ln)
                        A(bT[:, :, :], bT[:, :, :], ACT.Ln, scale=2.0 ** 66).then_inc(s_lnf, 1)
                        act_.wait_ge(s_u, U * l + j)
                        A(g2, QB, ACT.Tanh, scale=0.5).then_inc(s_tq, 1)
                    if grp == 4:
                        for c in range(AC):
                            for w in range(2):
                                act_.wait_ge(s_gp, 8 * l + 2 * c + w + 1)
                                bias = sm[:, 4 + w, AC * l + c:AC * l + c + 1]
                                A((rg, ig)[w][:, c, :], ps[4 + w][:, 0:N], ACT.Tanh, bias=bias,
                                  scale=0.5).then_inc(s_tg, 1)
                        act_.wait_ge(s_rdy, l + 1)
                        for c in range(AC):
                            A(ag[:, c, :], rg[:, c, :], ACT.Exp, scale=coef[:, l, c:c + 1])
                        for c in range(AC):
                            ins = A(mu[:, c, :], rg[:, c, :], ACT.Tanh, scale=coef[:, l, c:c + 1])
                        ins.then_inc(s_a, 1)
                act_.wait_ge(s_gi, l + 1)
                A(gt, gt, ACT.Tanh, scale=0.7978845608028654).then_inc(s_tge, 1)
                act_.wait_ge(s_u, U * (l + 1))
                A(oT[:, :, :], GB, ACT.Tanh, scale=0.5).then_inc(s_tgb, 1)
                act_.dma_start(S[:, :, :], a["state_hgrn"][l].rearrange("b h d e -> d (b h) e")).then_inc(s_S, 16)
                act_.wait_ge(s_vp, l + 1)
                ch(A(vtok[:, 0, :, :], ps[0][:, :].rearrange("p (h e) -> p h e", h=H), ACT.Copy))
                A(vtok[:, 1, :, :], ps[1][:, :].rearrange("p (h e) -> p h e", h=H), ACT.Copy).then_inc(s_v, 1)
                fill = FILL[l]
                mod_row(1)
                act_.wait_ge(s_m2, l + 1)
                A(mu, mu, ACT.Sqrt).then_inc(s_mu, 1)
                mod_row(fill[0] - 1)
                act_.wait_ge(s_ms, 3 * l + 2)
                rsqrt(rs[:, :], ps[4][:, 0:N]).then_inc(s_rs, 1)
                for v in range(1, LEVELS + 1):
                    act_.wait_ge(s_ld, LEVELS * l + v)
                    A(LD[v % 2], LD[v % 2], ACT.Exp).then_inc(s_le, 1)
                    if v >= 2:
                        mod_row(fill[1][v - 2])
                for h in range(H):
                    ins = A(ke[:, h, :], bT[:, h, :], ACT.Exp, scale=-1.0, bias=bT[:, h, T - 1:T])
                ins.then_inc(s_kx, 1)
                mod_row(sum(fill[1][LEVELS - 1:]))
                act_.wait_ge(s_kp, l + 1)
                ch(A(keT[:, 0], ps[4][:, :].rearrange("p (h e) -> p h e", h=H), ACT.Copy))
                A(keT[:, 1], ps[5][:, :].rearrange("p (h e) -> p h e", h=H), ACT.Copy).then_inc(s_keT, 1)
                act_.wait_ge(s_op, l + 1)
                ch(A(oT[:, 0:2, 0:T], ps[0][:, :].rearrange("p (h t) -> p h t", h=2), ACT.Copy))
                A(oT[:, 2:4, 0:T], ps[1][:, :].rearrange("p (h t) -> p h t", h=2), ACT.Copy)
                act_.wait_ge(s_sf, l + 1)
                act_.wait_ge(s_ke, l + 1)
                act_.wait_ge(s_kp, l + 1)
                A(sfin, ps[5][:, :], ACT.Copy).then_inc(s_sfs, 1)
                act_.wait_ge(s_sfs, l + 1)
                act_.dma_start(o["new_S_prompt"][l, 0].rearrange("h d e -> d h e"),
                               sfin.rearrange("p (h e) -> p h e", h=H)).then_inc(s_st, 16)
                mod_row(sum(fill[2]))
                act_.wait_ge(s_osp, l + 1)
                ch(A(oT[:, :, T:N], ps[4][:, 0:H * NS].rearrange("p (h b) -> p h b", h=H), ACT.Copy))
                A(yT[:, AC:, :], oT[:, :, :], ACT.Square).then_inc(s_os, 1)
                mod_row(fill[3])
                act_.wait_ge(s_vbd, NS * (l + 1))
                act_.dma_start(o["new_S_sample"][l].rearrange("b h d e -> d (b h) e"), S[:, :, :])\
                    .then_inc(s_st, 16)
                act_.wait_ge(s_oms, l + 1)
                for h in range(H):
                    ch(A(LN_OUT(h), ps[h][:, 0:N], ACT.Ln, bias=eps[:, 0:1]))
                A(ar[:, 0:W4], ar[:, 0:W4], ACT.Exp, scale=-0.5).then_inc(s_ors, 1)
                mod_row(fill[4])
                assert rowed[0] == MOD_DONE[l + 1]
                act_.wait_ge(s_ocp, l + 1)
                A(outr[l][:, :], ps[4][0:80, 0:P], ACT.Copy).then_inc(s_or, 1)
                if l == 0:
                    act_.wait_ge(s_st, 2 * 16)
                    for d in range(2):
                        ffn_slab(d)
                for c in range(KC):
                    act_.wait_ge(s_x1, KC * l + c + 1)
                    square(2 * l + 1, c)
                act_.wait_ge(s_ms, 3 * l + 3)
                rsqrt(rs[:, :], ps[NORM_BANK[2 * l + 1]][:, 0:N]).then_inc(s_rs, 1)

            def vector_stores(l):
                act_.wait_ge(s_or, l + 1)
                for dst, r0, n_ in (
                        (o["new_h_prompt"][l, 0].rearrange("(c p) -> c p", p=P), 0, 4),
                        (o["new_h_sample"][l].rearrange("b (c p) -> (b c) p", p=P), 4, 32),
                        (o["new_conv_prompt"][l, 0].rearrange("j (c p) -> (j c) p", p=P), 36, 12)):
                    act_.dma_start(dst, outr[l][r0:r0 + n_, :]).then_inc(s_out, 16)
                    outs[0] += 1
                for b in range(NS):
                    act_.dma_start(o["new_conv_sample"][l, b, CW - 2].rearrange("(c p) -> c p", p=P),
                                   outr[l][48 + 4 * b:52 + 4 * b, :]).then_inc(s_out, 16)
                    outs[0] += 1

            def LN_OUT(h):
                return ar[:, h * N:(h + 1) * N]

            def ffn_slab(d):
                s_, loads, width = FFN_SLOT[d]
                act_.wait_ge(full[s_], 16 * loads)
                if d >= 2:
                    act_.wait_ge(used, FFN + d - 1)
                A(wH[d % 2][:, 0:width], ring[:, s_, 0:width], ACT.Copy).then_inc(s_fwH, 1)

            layer(0)
            for i in range(4):
                act_.wait_ge(s_h, KC + 2 * i + 2)
                c = slice(2 * i, 2 * i + 2)
                A(fhH[:, c, :], hT[:, c, :], ACT.Copy).then_inc(s_fhH, 1)
            for d in range(2, FS):
                ffn_slab(d)
                if d == 9:
                    gate_weights(1)
                if d == 13:
                    vector_stores(0)
                if d % 2 == 0 and d <= 2 * G:
                    g = d // 2 - 1
                    act_.wait_ge(s_fa, 2 * g) if g else None
                    for m in range(2):
                        A(fsg[m], ps[g % 2 * 4 + m][:, 0:N], ACT.Silu).then_inc(s_fs, 1)
                if d % 2 == 0 and 4 <= d <= 2 * G + 2:
                    g = d // 2 - 2
                    for m in range(2):
                        act_.wait_ge(s_fa, 2 * g + m + 1)
                        A(faH[:, 2 * g + m, :], fac[m], ACT.Copy).then_inc(s_faH, 1)
                if d >= 2 * G + 5 and (d - 2 * G - 5) % 3 == 0:
                    q = (d - 2 * G - 5) // 3
                    for c in (2 * q, 2 * q + 1):
                        act_.wait_ge(s_fx, c + 1)
                        square(2, c)
            for c in range(6, KC):
                act_.wait_ge(s_fx, c + 1)
                square(2, c)
            layer(1)
            rws = (P, P, NS)
            for n in range(6):
                act_.wait_ge(s_htp, n + 1)
                A(h2tok[0:rws[n // 2], n // 2, n % 2 * 512:n % 2 * 512 + 512], ps[2 + n % 2][0:rws[n // 2], :],
                  ACT.Copy).then_inc(s_htk, 1)
            act_.wait_ge(s_red, 1)
            A(rt[:, 20, :, 0], rt[:, 19, :, 0], ACT.Exp).then_inc(s_re, 1)
            vector_stores(1)
            mod_row(MOD_LAST)

            cp = nc.scalar.copy

            def gathered(n, q):
                act_.wait_ge(s_gth, n * 2 + q + 1)
                cp(hgH[:, 4 * q:4 * q + 4, :], ps[7][:, :].rearrange("p (c j) -> p c j", c=4)).then_inc(s_hgH, 1)

            def outputs(n):
                act_.wait_ge(used, n * LS + SLABS)
                for m in range(2):
                    cp(ytok[:, m * 512:(m + 1) * 512], ps[4 + m][:, :]).then_inc(s_yt, 1)

            act_.wait_ge(s_st, 2 * 16 * L)
            gathered(0, 0)
            gathered(0, 1)
            act_.wait_ge(s_tab, 1)
            lots = act_.value_load(tab[0:1, 0:1], min_val=NE, max_val=MAXLOTS)
            with act_.Fori(0, lots) as i:
                slot = slots(act_, i)
                for t in range(LS):
                    w = slot(t)
                    act_.wait_ge(used, i * LS + SLABS + t - 2)
                    cp(wH[t % 3][:, :], w).then_inc(s_hi, 1)
                    if t == 2:
                        outputs(i)
                    if t in FORM_AT:
                        g = FORM_AT[t]
                        act_.wait_ge(used, i * LS + SLABS + LOT_ORDER.index((0, g)) + 1)
                        if g >= 2:
                            act_.wait_ge(s_mua, i * G + g - 1)
                        A(sg[g % 2], ps[g % 2][:, 0:256].rearrange("p (m j) -> p m j", m=2), ACT.Silu)\
                            .then_inc(s_mus, 1)
                    if t == LS - 1:
                        gathered(i + 1, 0)
                    if t in DOWN_AT:
                        g = DOWN_AT[t]
                        act_.wait_ge(s_aT, i * G + g + 1)
                        cp(aH[g % 2][:, :], ps[6][:, 0:256]).then_inc(s_aH, 1)
                gathered(i + 1, 1)
            outputs(lots)
            for c in range(KC):
                act_.wait_ge(s_x, c + 1)
                square(2 * L, c)
            act_.wait_ge(s_ms, 3 * L + 1)
            rsqrt(rs[:, :], ps[NORM_BANK[2 * L]][:, 0:N]).then_inc(s_rs, 1)
            for n in range(6):
                q, t = divmod(n, 3)
                qs = slice(q * 512, (q + 1) * 512)
                act_.wait_ge(s_ft, n + 1)
                A(yrow[0:ROWS[t], t, qs], ps[2 + n % 2][0:ROWS[t], :], ACT.Copy).then_inc(s_fr, 1)
                if t == 1:
                    act_.wait_ge(s_fr, n + 1)
                    act_.dma_start(o["y_prompt"][0].rearrange("(t p) c -> p t c", p=P)[:, :, qs],
                                   yrow[:, 0:2, qs]).then_inc(s_out, 16)
                    outs[0] += 1
            act_.wait_ge(s_fr, 6)
            act_.dma_start(o["y_sample"].rearrange("b t c -> (b t) c"), yrow[0:NS, 2, :]).then_inc(s_out, 16)
            outs[0] += 1
            act_.wait_ge(s_out, 16 * outs[0])
            act_.wait_ge(s_st, 2 * 16 * L)

        @block.vector
        def _(dve):
            V = nc.vector
            ch = Chain(dve, c_dve)
            tt, ts, stt = V.tensor_tensor, V.tensor_scalar, V.scalar_tensor_tensor

            dve.wait_ge(s_act0, 1)
            ch(stt(cond[:, :, 0], cond[:, :, 0], 1.0, par[:, CP:CP + KC], ALU.add, ALU.mult))
            ch(stt(cond[:, :, 1:COND], cond[:, :, 1:COND], 1.0,
                   par[:, CS:CS + 64].rearrange("p (b c) -> p c b", c=KC), ALU.add, ALU.mult))
            ts(cond[:, :, :], cond[:, :, :], 0.5, None, ALU.mult).then_inc(s_cond, 1)
            dve.wait_ge(s_cst, 1)
            ti, si, xi = (ar[:, n * P:(n + 1) * P].bitcast(i32) for n in (0, 1, 2))
            ch(tt(xi, ti, si, ALU.bitwise_xor))
            ch(ts(mask[:, 0, :], xi, 0.0, None, ALU.is_equal))
            for v in range(1, LEVELS):
                sh = ar[:, 3 * P:4 * P].bitcast(i32)
                ch(ts(sh, xi, v - 1, None, ALU.logical_shift_right))
                ch(stt(mask[:, v, :], sh, 1.0, before[:], ALU.is_equal, ALU.mult))
            dve.wait_ge(s_par, 1)
            lam = par[:, LAM:LAM + 8]
            ch(stt(sm[:, 0, 0:8], lam, -1.0, lam, ALU.mult, ALU.max))
            l0, l1 = par[:, LBL:LBL + 4], par[:, LBL + 4:LBL + 8]
            ch(tt(sm[:, 6, 0:4], l0, l1, ALU.max))
            ch(tt(sm[:, 2, 0:4], l0, sm[:, 6, 0:4], ALU.subtract))
            tt(sm[:, 2, 4:8], l1, sm[:, 6, 0:4], ALU.subtract).then_inc(s_dve0, 1)
            ts(sm[:, 4, 0:8], par[:, BA:BA + 8], 0.5, None, ALU.mult)
            ch(ts(sm[:, 5, 0:8], par[:, BX:BX + 8], 0.5, None, ALU.mult))
            dve.wait_ge(s_act0, 2)
            z, q, q2, pz = sm[:, 1, 0:8], sm[:, 7, 0:8], sm[:, 8, 0:8], sm[:, 9, 0:8]
            ch(ts(q, z, 2.0, None, ALU.add))
            ch(V.reciprocal(q, q))
            ch(tt(q, q, z, ALU.mult))
            ch(tt(q2, q, q, ALU.mult))
            ch(ts(pz, q2, 1.0 / 15, 1.0 / 13, ALU.mult, ALU.add))
            for d in (11, 9, 7, 5, 3, 1):
                ch(tt(pz, pz, q2, ALU.mult))
                ch(ts(pz, pz, 1.0 / d, None, ALU.add))
            ch(tt(pz, pz, q, ALU.mult))
            ch(ts(q, lam, -1.0, 0.0, ALU.mult, ALU.max))
            ch(stt(q, pz, 2.0, q, ALU.mult, ALU.add))
            ch(ts(coef[:].rearrange("p l c -> p (l c)"), q, -8.0, None, ALU.mult))
            e = sm[:, 3, 0:8]
            ch(tt(sm[:, 10, 0:4], e[:, 0:4], e[:, 4:8], ALU.add))
            ch(V.reciprocal(sm[:, 10, 0:4], sm[:, 10, 0:4]))
            ch(V.memset(lb[:, 0, :], 0.0))
            ch(tt(lb[:, 1, :], e[:, 4:8], sm[:, 10, 0:4], ALU.mult))
            ch(ts(omlb[:], lb[:], -1.0, 1.0, ALU.mult, ALU.add))

            def mod_batch(i):
                n0, n1 = ((0,) + MOD_DONE)[i:i + 2]
                dve.wait_ge(s_mtr, n1)
                tt(modT[:, :, :, :].rearrange("p l c b -> p (l c) b")[:, 2 * n0:2 * n1, :],
                   mod_columns(n0, n1 - n0), wide(par[:, MODB + 2 * n0:MODB + 2 * n1], COND), ALU.add)\
                    .then_inc(s_mod, 1)

            mod_batch(0)
            dve.wait_ge(s_mod, 1)

            def modulate(l, which, gcol):
                sc = modT[:, l, (3 * which + 1) * KC:(3 * which + 2) * KC, :]
                shf = modT[:, l, 3 * which * KC:(3 * which + 1) * KC, :]
                ch(stt(modA[:, :, :], sc, 1.0, wide(par[:, gcol + KC * l:gcol + KC * (l + 1)], COND),
                       ALU.add, ALU.mult))
                dve.wait_ge(s_rs, 3 * l + (1 if which == 0 else 3))
                hs = hT[:, :, T:N]
                ch(tt(hs, xT[:, :, T:N], rs[:, T:N].unsqueeze(1).broadcast_to([P, KC, NS]), ALU.mult))
                ch(tt(hs, hs, modA[:, :, 1:COND], ALU.mult))
                ch(tt(hs, hs, shf[:, :, 1:COND], ALU.add))
                for c in range(KC + 1):
                    if c < KC:
                        stt(hT[:, c, 0:T], xT[:, c, 0:T], modA[:, c, 0:1], rs[:, 0:T], ALU.mult, ALU.mult)\
                            .then_inc(c_dve, 1)
                        ch.n += 1
                    if c:
                        dve.wait_ge(c_dve, ch.n - (c < KC))
                        ts(hT[:, c - 1, 0:T], hT[:, c - 1, 0:T], shf[:, c - 1, 0:1], None, ALU.add)\
                            .then_inc(s_h, 1)

            def residual(l, part, c, bank):
                gate = modT[:, l, (3 * part + 2) * KC + c, :]
                tmp = sm[:, 11, c % 2 * NS:(c % 2 + 1) * NS]
                tt(tmp, bank[:, T:N], gate[:, 1:COND], ALU.mult).then_inc(c_dve, 1)
                ch.n += 1
                stt(xT[:, c, 0:T], bank[:, 0:T], gate[:, 0:1], xT[:, c, 0:T], ALU.mult, ALU.add)
                dve.wait_ge(c_dve, ch.n)
                return tt(xT[:, c, T:N], xT[:, c, T:N], tmp, ALU.add)

            def layer(l):
                modulate(l, 0, G1)
                for i in range(4):
                    dve.wait_ge(s_whH, 4 * l + i + 1)
                    c = slice(2 * i, 2 * i + 2)
                    tt(fhL[:, c, :], hT[:, c, :], yhH[:, c, :].bitcast(fp32), ALU.subtract).then_inc(s_whL, 1)
                dve.wait_ge(s_fe, l + 1)
                ch(ts(FB, FB, 1.0, None, ALU.add))
                ch(V.reciprocal(FB, FB))
                for h in range(H):
                    ins = ts(FB[:, h, :], FB[:, h, :], omlb[:, l, h:h + 1], lb[:, l, h:h + 1], ALU.mult, ALU.add)
                ch(ins)
                V.tensor_copy(fs, FB[:, :, T:N])
                ch(ts(oT[:, :, 0:T], FB[:, :, 0:T], 2.0 ** -60, None, ALU.max))
                ts(bT[:, :, :], FB[:, :, 0:T], 2.0 ** -60, None, ALU.min).then_inc(s_f, 1)
                dve.wait_ge(s_tq, l + 1)
                ch(stt(QB, g2, 1.0, QB, ALU.add, ALU.mult))
                ch(ts(QB, QB, 0.5, None, ALU.mult))
                dve.wait_ge(s_lnf, l + 1)
                ch(stt(oT[:, :, 0:T], bT[:, :, :], LN64, oT[:, :, 0:T], ALU.subtract, ALU.add))
                ch(ts(FB, FB, -1.0, 1.0, ALU.mult, ALU.add))
                for h in range(H):
                    ins = V.tensor_tensor_scan(bT[:, h, :], ones[:, 0:1].broadcast_to([P, T]), oT[:, h, 0:T],
                                               0.0, ALU.mult, ALU.add)
                ins.then_inc(s_b, 1)
                dve.wait_ge(s_u, U * l + 12)
                for c in range(AC):
                    for j in range(CW):
                        w = par[:, CWW + 16 * l + 4 * j + c:CWW + 16 * l + 4 * j + c + 1]
                        x = xaP[:, c, j:j + T]
                        if j == 0:
                            ch(ts(xc[:, c, 0:T], x, w, par[:, CB + 4 * l + c:CB + 4 * l + c + 1],
                                  ALU.mult, ALU.add))
                        else:
                            ch(stt(xc[:, c, 0:T], x, w, xc[:, c, 0:T], ALU.mult, ALU.add))
                cst = par[:, SCV + P * l:SCV + P * l + 96].rearrange("p (b j c) -> p j c b", j=CW - 1, c=AC)
                xs = xc[:, :, T:N]
                tmp = sm[:, 12:14, :].rearrange("p a b -> p (a b)").rearrange("p (c b) -> p c b", c=AC)
                for j in range(CW):
                    src = cst[:, j] if j < CW - 1 else XA[:, :, T:N]
                    w = wide(par[:, CWW + 16 * l + 4 * j:CWW + 16 * l + 4 * j + 4], NS)
                    ch(tt(tmp, src, w, ALU.mult))
                    other = wide(par[:, CB + 4 * l:CB + 4 * l + 4], NS) if j == 0 else xs
                    ins = tt(xs, tmp, other, ALU.add)
                    if j < CW - 1:
                        ch(ins)
                ins.then_inc(s_xc, 1)
                if l:
                    dve.wait_ge(s_or, l)
                oc = outc[:, :]
                V.tensor_copy(oc[:, 36:48].rearrange("p (j c) -> p c j", c=AC), xaP[:, :, T:T + 3])
                V.tensor_copy(oc[:, 48:80].rearrange("p (b c) -> p c b", c=AC), XA[:, :, T:N])
                dve.wait_ge(s_tg, 8 * (l + 1))
                ts(rg, rg, 0.5, 0.5, ALU.mult, ALU.add).then_inc(s_rdy, 1)
                ch(stt(ig, ig, 1.0, xc, ALU.add, ALU.mult))
                dve.wait_ge(s_u, U * l + 20)
                ch(tt(gt, GA, GA, ALU.mult))
                ch(ts(gt, gt, 0.044715, 1.0, ALU.mult, ALU.add))
                tt(gt, gt, GA, ALU.mult).then_inc(s_gi, 1)
                dve.wait_ge(s_a, l + 1)
                ch(ts(g2, mu, -1.0, 1.0, ALU.mult, ALU.add))
                ch(V.reciprocal(g2, g2))
                stt(mu, mu, -2.0, g2, ALU.mult, ALU.mult).then_inc(s_m2, 1)
                dve.wait_ge(s_mu, l + 1)
                ch(V.memset(ag[:, :, 0:1], 0.0))
                ch(V.memset(mu[:, :, 0:1], 1.0))
                ch(stt(ig, ig, 0.5, mu, ALU.mult, ALU.mult))
                for c in range(AC):
                    ins = V.tensor_tensor_scan(rg[:, c, 0:T], ag[:, c, 0:T], ig[:, c, 0:T], 0.0,
                                               ALU.mult, ALU.add)
                ch(ins)
                h0 = par[:, SH + P * l:SH + P * l + 32].rearrange("p (b c) -> p c b", c=AC)
                ch(tt(rg[:, :, T:N], ag[:, :, T:N], h0, ALU.mult))
                ch(tt(rg[:, :, T:N], rg[:, :, T:N], ig[:, :, T:N], ALU.add))
                V.tensor_copy(oc[:, 0:4], rg[:, :, T - 1])
                V.tensor_copy(oc[:, 4:36].rearrange("p (b c) -> p c b", c=AC), rg[:, :, T:N]).then_inc(s_oc, 1)
                dve.wait_ge(s_tge, l + 1)
                ch(stt(gt, gt, 1.0, GA, ALU.add, ALU.mult))
                ch(stt(gt, gt, 0.5, rg, ALU.mult, ALU.mult))
                tt(g2, gt, gt, ALU.mult).then_inc(s_zs, 1)
                dve.wait_ge(s_tgb, l + 1)
                ch(stt(GB, oT[:, :, :], 1.0, GB, ALU.add, ALU.mult))
                for h in range(H):
                    ts(GB[:, h, :], GB[:, h, :], 0.5, par[:, HG + 4 * l + h:HG + 4 * l + h + 1],
                       ALU.mult, ALU.mult)
                dve.wait_ge(s_rs, 3 * l + 2)
                for c in range(AC):
                    ins = stt(yT[:, c, :], gt[:, c, :],
                              par[:, OG + 4 * l + c:OG + 4 * l + c + 1], rs[:, :], ALU.mult, ALU.mult)
                ch(ins)

                def diff(v):
                    h2 = 1 << (v - 1)
                    b4 = bT[:, :, :].rearrange("p h (n two i) -> p (h n) two i", two=2, i=h2)
                    d4 = LD[v % 2].rearrange("p (n two i) -> p n two i", two=2, i=h2)
                    mid = b4[:, :, 0, h2 - 1:h2]
                    n = b4.shape[1]
                    midb = mid.broadcast_to([P, n, h2])
                    ch(tt(d4[:, :, 1, :], b4[:, :, 1, :], midb, ALU.subtract))
                    tt(d4[:, :, 0, :], midb, b4[:, :, 0, :], ALU.subtract).then_inc(s_ld, 1)

                def take(v):
                    dve.wait_ge(s_lp, (LEVELS + 1) * l + v + 1)
                    if l or v:
                        dve.wait_ge(s_lc, (LEVELS + 1) * l + v)
                    if v == LEVELS:
                        V.tensor_copy(ATx[:, :, :], ps[0][:, :].rearrange("p (h t) -> p h t", h=H))\
                            .then_inc(s_lc, 1)
                        return
                    for t in range(2):
                        ins = V.copy_predicated(AT[:, t], mask[:, v, :].unsqueeze(1).broadcast_to([P, H, P]),
                                                ps[2 * (v % 2) + t][:, :].rearrange("p (h t) -> p h t", h=H))
                    ins.then_inc(s_lc, 1)

                dve.wait_ge(s_u, U * (l + 1))
                ch(V.memset(AT[:, :, :, :], 0.0))
                dve.sem_inc(s_lw, 1)
                diff(1)
                for v in range(1, LEVELS + 1):
                    if v < LEVELS:
                        dve.wait_ge(s_lw, (LEVELS + 1) * l + v)
                        diff(v + 1)
                    h2 = 1 << (v - 1)
                    dve.wait_ge(s_le, LEVELS * l + v)
                    d4, w4 = (x[v % 2].rearrange("p (h n two i) -> p h n two i", h=H, two=2, i=h2)
                              for x in (LD, LW))
                    for h in range(H):
                        qs = QB[:, h, 0:T].rearrange("p (n two i) -> p n two i", two=2, i=h2)
                        ks = FB[:, h, 0:T].rearrange("p (n two i) -> p n two i", two=2, i=h2)
                        tt(w4[:, h, :, 1, :], d4[:, h, :, 1, :], qs[:, :, 1, :], ALU.mult)
                        ins = tt(w4[:, h, :, 0, :], d4[:, h, :, 0, :], ks[:, :, 0, :], ALU.mult)
                    ins.then_inc(s_lw, 1)
                    take(v - 1)
                take(LEVELS)
                dve.wait_ge(s_kx, l + 1)
                tt(ke, ke, FB[:, :, 0:T], ALU.mult).then_inc(s_ke, 1)
                dve.wait_ge(s_S1, l + 1)
                for b in range(NS):
                    dve.wait_ge(s_vb, NS * l + b + 1)
                    if b:
                        dve.wait_ge(s_vbd, NS * l + b)
                    ch(tt(vbk, ps[2 + b % 2][:, :].rearrange("p (h e) -> p h e", h=H),
                          wide(FB[:, :, T + b], P), ALU.mult))
                    ins = tt(S[:, b * H:(b + 1) * H, :], S[:, b * H:(b + 1) * H, :], vbk, ALU.add)
                    ins.then_inc(s_vbd, 1)
                dve.wait_ge(s_ors, l + 1)
                ch(tt(yT[:, AC:, :], oT[:, :, :], ar[:, 0:W4].rearrange("p (h n) -> p h n", n=N), ALU.mult))
                tt(yT[:, AC:, :], yT[:, AC:, :], GB, ALU.mult).then_inc(s_y, 1)
                mod_batch(l + 1)
                dve.wait_ge(s_mod, l + 2)
                if l == 0:
                    dve.wait_ge(s_y, 1)
                    for d in range(2):
                        ffn_slab(d)
                for c in range(KC):
                    if c % 2 == 0:
                        dve.wait_ge(s_wp, 4 * l + c // 2 + 1)
                    else:
                        dve.wait_ge(used, W_OUT[l] + c // 2 + 1)
                    if c >= 2:
                        dve.wait_ge(s_x1, KC * l + c - 1)
                    ins = residual(l, 0, c, ps[c % 4])
                    ins.then_inc(s_x1, 1)
                dve.wait_ge(s_x1, KC * (l + 1))
                modulate(l, 1, G2)

            def ffn_slab(d):
                s_, _, width = FFN_SLOT[d]
                dve.wait_ge(s_fwH, d + 1)
                tt(wL[d % 2][:, 0:width], ring[:, s_, 0:width], wH[d % 2][:, 0:width].bitcast(fp32),
                   ALU.subtract).then_inc(s_fwL, 1)

            def ffn_residual(q):
                dve.wait_ge(used, FFN + 2 * G + 3 * q + 3)
                for c in (2 * q, 2 * q + 1):
                    if c >= 2:
                        dve.wait_ge(s_fx, c - 1)
                    residual(0, 1, c, ps[(q + 1) % 2 * 4 + c % 2]).then_inc(s_fx, 1)

            layer(0)
            for i in range(4):
                dve.wait_ge(s_fhH, i + 1)
                c = slice(2 * i, 2 * i + 2)
                tt(fhL[:, c, :], hT[:, c, :], fhH[:, c, :].bitcast(fp32), ALU.subtract).then_inc(s_fhL, 1)
            for d in range(2, FS):
                ffn_slab(d)
                if d % 2 and d <= 2 * G + 1:
                    g = d // 2 - 1
                    dve.wait_ge(used, FFN + 2 * g + 2)
                    for m in range(2):
                        dve.wait_ge(s_fs, 2 * g + m + 1)
                        if g:
                            dve.wait_ge(s_faL, 2 * g - 1 + m)
                        tt(fac[m], fsg[m], ps[g % 2 * 4 + 2 + m][:, 0:N], ALU.mult).then_inc(s_fa, 1)
                if d % 2 == 0 and 4 <= d <= 2 * G + 2:
                    g = d // 2 - 2
                    for m in range(2):
                        dve.wait_ge(s_faH, 2 * g + m + 1)
                        tt(faL[:, 2 * g + m, :], fac[m], faH[:, 2 * g + m, :].bitcast(fp32), ALU.subtract)\
                            .then_inc(s_faL, 1)
                if d >= 2 * G + 4 and (d - 2 * G - 4) % 3 == 0:
                    ffn_residual((d - 2 * G - 4) // 3)
            ffn_residual(3)
            dve.wait_ge(s_fx, KC)
            layer(1)

            rws = (P, P, NS)
            LG, TOP, MSK, POS, OH0, OH1, BLK, EB, GS, T0, T1 = (rt[:, n] for n in (0, 1, 2, 3, 4, 5, 6, 7, 8, 9, 10))
            CNT, EXT, OFF, T2, FI = (rt[:, n, 0, :] for n in (11, 12, 13, 14, 15))
            V.memset(acc[:, :, :], 0.0).then_inc(s_scd, 1)
            dve.wait_ge(s_scd, 1)
            V.memset(gatT, 0.0).then_inc(s_gT, 1)
            V.memset(ps[4][:, :], 0.0)
            V.memset(ps[5][:, :], 0.0)
            ch(V.memset(rt[:, :, :, :], 0.0))
            dve.wait_ge(s_lg, 1)
            for t in range(3):
                ch(V.tensor_copy(LG[0:rws[t], t, :], ps[1][0:rws[t], t * NE:(t + 1) * NE]))
            for t in range(3):
                ch(V.max(TOP[:, t, :], LG[:, t, :]))
                ch(V.max_index(ridx[:, t, :], TOP[:, t, :], LG[:, t, :]))
            ch(V.tensor_copy(T0, ridx[:, :, :]))
            io8 = iota[:, 0:NE]
            for t in range(3):
                ch(ts(OH0[:, t, :], io8, T0[:, t, 0:1], None, ALU.is_equal))
                ch(ts(OH1[:, t, :], io8, T0[:, t, 1:2], None, ALU.is_equal))
            tt(MSK, OH0, OH1, ALU.add).then_inc(s_msk, 1)
            tt(rt[:, 19, :, 0], TOP[:, :, 1], TOP[:, :, 0], ALU.subtract).then_inc(s_red, 1)
            dve.wait_ge(s_re, 1)
            ch(ts(wts[:, :, 0], rt[:, 20, :, 0], 1.0, None, ALU.add))
            ch(V.reciprocal(wts[:, :, 0], wts[:, :, 0]))
            ch(tt(wts[:, :, 1], rt[:, 20, :, 0], wts[:, :, 0], ALU.mult))
            dve.wait_ge(s_rk, 1)
            for t in range(3):
                ch(V.tensor_copy(POS[0:rws[t], t, :], ps[0][0:rws[t], t * NE:(t + 1) * NE]))
            ch(V.tensor_copy(CNT, ps[0][:, 3 * NE:4 * NE]))
            ch(ts(T2, CNT, float(LOT), None, ALU.is_gt))
            ch(stt(EXT, CNT, float(2 * LOT), T2, ALU.is_gt, ALU.add))
            ch(V.tensor_tensor_scan(OFF, ones[:, 0:NE], EXT, 0.0, ALU.mult, ALU.add))
            ch(ts(tab[:, 0:1], OFF[:, NE - 1:NE], float(NE), None, ALU.add))
            ch(tt(OFF, OFF, EXT, ALU.subtract))
            ch(ts(OFF, OFF, float(NE), None, ALU.add))
            ch(ts(BLK, POS, float(LOT), None, ALU.is_ge))
            ch(stt(T2, OFF, -1.0, io8, ALU.add, ALU.subtract))
            ch(tt(EB, BLK, T2.unsqueeze(1).broadcast_to([P, 3, NE]), ALU.mult))
            ch(tt(EB, EB, io8.unsqueeze(1).broadcast_to([P, 3, NE]), ALU.add))
            ch(stt(GS, EB, float(LOT), POS, ALU.mult, ALU.add))
            for n, oh in enumerate((OH0, OH1)):
                ch(tt(T1, GS, oh, ALU.mult))
                ch(V.reduce_sum(gsl[:, :, n], T1, AX.X))

            def gathered(n, q):
                dve.wait_ge(s_hgH, n * 2 + q + 1)
                tt(hgL[:, 4 * q:4 * q + 4, :], ps[7][:, :].rearrange("p (c j) -> p c j", c=4),
                   hgH[:, 4 * q:4 * q + 4, :].bitcast(fp32), ALU.subtract).then_inc(s_hgL, 1)

            TILES = [(slice(0, ROWS[t]), t) for t in range(3)]

            def choice(step):
                for r, t in TILES:
                    S0, S1, W0 = sel[r, t, :], stmp[r, t, :], gat[r, t, :]
                    if step == 0:
                        ts(S0, iota[r, 0:LOT], gsl[r, t, 0:1], None, ALU.is_equal)
                        ins = ts(S1, iota[r, 0:LOT], gsl[r, t, 1:2], None, ALU.is_equal)
                    elif step == 1:
                        ins = ts(W0, S0, wts[r, t, 0:1], None, ALU.mult)
                    elif step == 2:
                        stt(W0, S1, wts[r, t, 1:2], W0, ALU.mult, ALU.add)
                        ins = tt(S0, S0, S1, ALU.add)
                if step == 2:
                    ins = ts(gsl[:, :, :], gsl[:, :, :], float(-LOT), None, ALU.add)
                return ins

            ch(choice(0))
            ch(choice(1))
            choice(2).then_inc(s_sel, 1)
            mod_batch(3)
            gathered(0, 0)
            for i in range(MAXLOTS - NE):
                ch(tt(T2, OFF, EXT, ALU.add))
                ch(ts(T2, T2, float(NE + i), None, ALU.is_gt))
                ch(stt(FI, OFF, float(NE + i), T2, ALU.is_le, ALU.mult))
                ch(tt(FI, FI, io8, ALU.mult))
                ch(V.reduce_sum(sm[:, 15, i:i + 1], FI, AX.X))
            ch(V.tensor_copy(tab[:, 1:1 + MAXLOTS - NE], sm[:, 15, 0:MAXLOTS - NE]))
            dve.sem_inc(s_tab, 1)
            gathered(0, 1)
            dve.wait_ge(s_tab, 1)
            lots = dve.value_load(tab[0:1, 0:1], min_val=NE, max_val=MAXLOTS)
            with dve.Fori(0, lots) as i:
                slot = slots(dve, i)
                for t in range(LS):
                    w = slot(t)
                    dve.wait_ge(s_hi, i * LS + t + 1)
                    tt(wL[t % 3][:, :], w, wH[t % 3][:, :].bitcast(fp32), ALU.subtract).then_inc(s_lo, 1)
                    if t in FORM_AT:
                        g = FORM_AT[t]
                        dve.wait_ge(s_mus, i * G + g + 1)
                        dve.wait_ge(used, i * LS + SLABS + LOT_ORDER.index((1, g)) + 1)
                        if g >= 2:
                            dve.wait_ge(s_aT, i * G + g - 1)
                        tt(ac[g % 2], sg[g % 2], ps[2 + g % 2][:, 0:256].rearrange("p (m j) -> p m j", m=2),
                           ALU.mult).then_inc(s_mua, 1)
                    if t == LS - 1:
                        gathered(i + 1, 0)
                    if t in DOWN_AT:
                        g = DOWN_AT[t]
                        dve.wait_ge(s_aH, i * G + g + 1)
                        tt(aL[g % 2][:, :], ps[6][:, 0:256], aH[g % 2][:, :].bitcast(fp32),
                           ALU.subtract).then_inc(s_aL, 1)
                    if t in ADD_AT:
                        c = ADD_AT[t]
                        dve.wait_ge(s_sc, i * KC + c + 1)
                        tt(acc[:, c, :], acc[:, c, :], ps[7][:, 0:N], ALU.add).then_inc(s_scd, 1)
                    if t == GATES_AT + 3:
                        dve.wait_ge(s_gTp, i + 1)
                        V.tensor_copy(gatT, ps[7][:, 0:N]).then_inc(s_gT, 1)
                    if t in CHOOSE_AT:
                        step = CHOOSE_AT[t]
                        dve.wait_ge(c_lot, i * 2 + step) if step else dve.wait_ge(s_sel, i + 1)
                        choice(step).then_inc(c_lot if step < 2 else s_sel, 1)
                gathered(i + 1, 1)
            for c in range(KC):
                dve.wait_ge(s_sc, lots * KC + c + 1)
                tt(acc[:, c, :], acc[:, c, :], ps[6 + c % 2][:, 0:N], ALU.add).then_inc(s_scd, 1)
                if c >= 2:
                    dve.wait_ge(s_x, c - 1)
                dve.wait_ge(s_scd, lots * KC + c + 2)
                residual(1, 1, c, acc[:, c, :]).then_inc(s_x, 1)
            dve.wait_ge(s_x, KC)
            dve.wait_ge(s_rs, 3 * L + 1)
            for c in range(KC):
                stt(hT[:, c, :], xT[:, c, :], par[:, FG + c:FG + c + 1], rs[:, :], ALU.mult, ALU.mult)\
                    .then_inc(s_fin, 1)


ORDER = (3, 2, 0, 4, 1, 5)
ORDER_SLABS = tuple(2 * g + h for g in ORDER for h in range(2))
DOWN = ((0, 8), (8, 16), (16, 22))
NORM_BANK = (5, 5, 3, 5, 0)
PARAM_LOADS = 11 + 1 + 4
LN64 = 6 * 0.6931471805599453
MG = 24
MOD_DONE = (8, 32, 44, 48)
FILL = ((4, (1,) * 9, (1,) * 8, 2, 1), (3, (1, 0, 1, 0, 1, 0, 1, 0, 0), (0, 0, 1, 0, 0, 1, 0, 0), 2, 1))
assert all(a + sum(b) + sum(c) + d + e == MOD_DONE[l + 1] - MOD_DONE[l]
           for l, (a, b, c, d, e) in enumerate(FILL))
W_IN = (MOD_DONE[0], MOD_DONE[1] + 16 + 34)
W_OUT = tuple(W_IN[l] + 12 + MOD_DONE[l + 1] - MOD_DONE[l] for l in range(2))
FFN = W_OUT[0] + 4
FS = 2 * G + 4 * len(DOWN)
assert FFN + FS == W_IN[1]
FFN_SLOT = [((FFN + d) % R, (FFN + d) // R + 1, SLAB if d < 2 * G else
             256 * (DOWN[(d - 2 * G) % 3][1] - DOWN[(d - 2 * G) % 3][0])) for d in range(FS)]
MOD_LAST = MOD_DONE[3] - MOD_DONE[2]
MOD_SLAB = tuple(range(8)) + tuple(W_IN[l] + 12 + i for l in range(2)
                                   for i in range(MOD_DONE[l + 1] - MOD_DONE[l]))\
    + tuple(W_OUT[1] + 4 + i for i in range(MOD_LAST))
SLABS = W_OUT[1] + 4 + MOD_LAST


def _loads():
    n = [0] * R
    for pos in range(SLABS):
        n[pos % R] += 1
    return n


LOADS = _loads()
ROWS = (P, P, NS)
LOT_ORDER = tuple(x for g in range(G) for x in ([(0, g), (1, g)] + ([(2, g - 1)] if g else []))) + ((2, G - 1),)

FORM_AT = {LOT_ORDER.index((0, g + 1)) if g < G - 1 else 3 * G - 1: g for g in range(G)}
TURN_AT = {LOT_ORDER.index((0, g + 1)) if g < G - 1 else 3 * G - 2: g for g in range(G)}
SCATTER_AT = {4 + 2 * c: c for c in range(KC)}
ADD_AT = {t + 3: c for t, c in SCATTER_AT.items()}
CHOOSE_AT = {25 + k: k for k in range(3)}
GATES_AT = 22
DOWN_AT = {LOT_ORDER.index((2, g)): g for g in range(G)}

_INS = ["x_prompt", "x_sample", "c_prompt", "c_sample", "state_rglru_h", "state_rglru_conv", "state_hgrn",
        "mod_w", "mod_b", "norm1_g", "norm2_g", "w_in", "conv_w", "conv_b", "rg_wa", "rg_ba", "rg_wx", "rg_bx",
        "rg_lambda", "rg_out_g", "hg_lb_logits", "hg_norm_g", "w_out", "ffn_w1", "ffn_w3", "ffn_w2",
        "router_w", "moe_w1", "moe_w3", "moe_w2", "final_g"]
_OUTS = [("y_prompt", (1, T, D)), ("y_sample", (NS, 1, D)), ("new_h_prompt", (L, 1, WA)),
         ("new_conv_prompt", (L, 1, CW - 1, WA)), ("new_S_prompt", (L, 1, H, P, P)),
         ("new_h_sample", (L, NS, WA)), ("new_conv_sample", (L, NS, CW - 1, WA)),
         ("new_S_sample", (L, NS, H, P, P))]


def kernel(**inputs):
    import numpy as np
    import concourse.bacc as bacc
    from concourse.bass_utils import run_bass_kernel_spmd as run

    nc = bacc.Bacc("TRN2", target_bir_lowering=False, num_devices=1)
    arrays, ins, outs = {}, {}, {}
    for name in _INS:
        x = np.ascontiguousarray(inputs[name])
        arrays[f"in_{name}"] = x
        ins[name] = nc.dram_tensor(f"in_{name}", x.shape, mybir.dt.from_np(x.dtype), kind="ExternalInput").ap()
    for name, shape in _OUTS:
        outs[name] = nc.dram_tensor(f"out_{name}", shape, mybir.dt.float32, kind="ExternalOutput").ap()
    trunk(nc, ins, outs)
    r = run(nc, [arrays], core_ids=[0])
    return tuple(r.results[0][f"out_{name}"] for name, _ in _OUTS)
```
